# Optimizing a Trainium2 kernel written in Bass

```python
import math
import jax, jax.numpy as jnp
from jax import lax
import numpy as np

D_MODEL = 1024
BATCH = 1
SEQ = 256
DEPTH = 1

EPS = 1e-6
CONV_WIDTH = 4
N_BRANCHES = 3
GMLP_WIDTH = D_MODEL
GMLP_GROUPS = 8
GMLP_GROUP_DIM = GMLP_WIDTH // GMLP_GROUPS
GMLP_CHUNK = 128
LRU_WIDTH = D_MODEL
LRU_HEADS = 8
LRU_HEAD_DIM = LRU_WIDTH // LRU_HEADS
LRU_C = 8.0
SSD_WIDTH = D_MODEL
SSD_HEAD_DIM = 64
SSD_HEADS = SSD_WIDTH // SSD_HEAD_DIM
SSD_GROUPS = 4
SSD_HEADS_PER_GROUP = SSD_HEADS // SSD_GROUPS
SSD_STATE = 128
SSD_CHUNK = 128
SSD_CONV_DIM = SSD_WIDTH + 2 * SSD_GROUPS * SSD_STATE
MLP_HIDDEN = 4 * D_MODEL
GMLP_IN = 2 * GMLP_WIDTH
LRU_IN = 2 * LRU_WIDTH
SSD_IN = SSD_WIDTH + SSD_CONV_DIM + SSD_HEADS
GATE_IN = N_BRANCHES * D_MODEL
D_IN = GMLP_IN + LRU_IN + SSD_IN + GATE_IN
SPLIT_POINTS = (GMLP_IN,
                GMLP_IN + LRU_IN,
                GMLP_IN + LRU_IN + SSD_WIDTH,
                GMLP_IN + LRU_IN + SSD_WIDTH + SSD_CONV_DIM,
                GMLP_IN + LRU_IN + SSD_IN)


def rms_norm(x, g):
    x32 = x.astype(jnp.float32)
    y = x32 * lax.rsqrt(jnp.mean(x32 * x32, axis=-1, keepdims=True) + EPS)
    return (y * g.astype(jnp.float32)).astype(x.dtype)

def layer_norm(x, g, b):
    x32 = x.astype(jnp.float32)
    mu = jnp.mean(x32, axis=-1, keepdims=True)
    xc = x32 - mu
    y = xc * lax.rsqrt(jnp.mean(xc * xc, axis=-1, keepdims=True) + EPS)
    return (y * g.astype(jnp.float32) + b.astype(jnp.float32)).astype(x.dtype)

def causal_dwconv(x, w, b):
    k, c = w.shape
    y = lax.conv_general_dilated(x, w[:, None, :], window_strides=(1,), padding=[(k - 1, 0)],
                                 dimension_numbers=('NWC', 'WIO', 'NWC'), feature_group_count=c)
    return y + b

def gmlp_mixer(za, ln_g, ln_b, w_s, b_s):
    bsz, seq, _ = za.shape
    u, v = jnp.split(jax.nn.gelu(za), 2, axis=-1)
    v = layer_norm(v, ln_g, ln_b)
    nc = seq // GMLP_CHUNK
    vc = v.reshape(bsz, nc, GMLP_CHUNK, GMLP_GROUPS, GMLP_GROUP_DIM)
    causal = jnp.tril(jnp.ones((GMLP_CHUNK, GMLP_CHUNK), dtype=bool))
    w = jnp.where(causal, w_s, 0)
    mixed = jnp.einsum('gts,bcsgd->bctgd', w, vc) + b_s.T[:, :, None]
    return u * mixed.reshape(bsz, seq, GMLP_WIDTH)

def rg_lru_mixer(zb, conv_w, conv_b, w_r, b_r, w_i, b_i, lam):
    bsz, seq, _ = zb.shape
    xb, gate = jnp.split(zb, 2, axis=-1)
    xb = causal_dwconv(xb, conv_w, conv_b)
    xh = xb.reshape(bsz, seq, LRU_HEADS, LRU_HEAD_DIM)
    r = jax.nn.sigmoid(jnp.einsum('bshi,hij->bshj', xh, w_r).reshape(bsz, seq, LRU_WIDTH) + b_r)
    i = jax.nn.sigmoid(jnp.einsum('bshi,hij->bshj', xh, w_i).reshape(bsz, seq, LRU_WIDTH) + b_i)
    log_a = -LRU_C * r.astype(jnp.float32) * jax.nn.softplus(-lam.astype(jnp.float32))
    a = jnp.exp(log_a)
    inp = jnp.sqrt(-jnp.expm1(2.0 * log_a)) * (i * xb).astype(jnp.float32)

    def combine(c1, c2):
        a1, b1 = c1
        a2, b2 = c2
        return a1 * a2, a2 * b1 + b2

    _, h = lax.associative_scan(combine, (a, inp), axis=1)
    return jax.nn.gelu(gate) * h.astype(gate.dtype)

def segsum(x):
    t = x.shape[-1]
    cs = jnp.cumsum(x, axis=-1)
    seg = cs[..., :, None] - cs[..., None, :]
    return jnp.where(jnp.tril(jnp.ones((t, t), dtype=bool)), seg, -jnp.inf)

def ssd_mixer(z, xbc, dt_raw, conv_w, conv_b, dt_bias, a_log, d_skip, norm_g):
    bsz, seq, _ = z.shape
    nc = seq // SSD_CHUNK
    g, r, q = SSD_GROUPS, SSD_HEADS_PER_GROUP, SSD_CHUNK
    xbc = jax.nn.silu(causal_dwconv(xbc, conv_w, conv_b))
    xs, bm, cm = jnp.split(xbc, [SSD_WIDTH, SSD_WIDTH + g * SSD_STATE], axis=-1)
    dt = jax.nn.softplus((dt_raw + dt_bias).astype(jnp.float32))
    a = -jnp.exp(a_log.astype(jnp.float32))
    x32 = xs.astype(jnp.float32).reshape(bsz, nc, q, g, r, SSD_HEAD_DIM)
    xdt = x32 * dt.reshape(bsz, nc, q, g, r)[..., None]
    bc = bm.astype(jnp.float32).reshape(bsz, nc, q, g, SSD_STATE)
    cc = cm.astype(jnp.float32).reshape(bsz, nc, q, g, SSD_STATE)
    adt = (dt * a).reshape(bsz, nc, q, g, r).transpose(0, 3, 4, 1, 2)
    a_cs = jnp.cumsum(adt, axis=-1)
    decay = jnp.exp(segsum(adt))
    cb = jnp.einsum('bclgn,bcsgn->bgcls', cc, bc)
    y_diag = jnp.einsum('bgcls,bgrcls,bcsgrp->bclgrp', cb, decay, xdt)
    decay_states = jnp.exp(a_cs[..., -1:] - a_cs)
    states = jnp.einsum('bcsgn,bgrcs,bcsgrp->cbgrpn', bc, decay_states, xdt)
    chunk_decay = jnp.exp(a_cs[..., -1]).transpose(3, 0, 1, 2)

    def step(h, inp):
        dec, st = inp
        return h * dec[..., None, None] + st, h

    _, prev = lax.scan(step, jnp.zeros_like(states[0]), (chunk_decay, states))
    y_off = jnp.einsum('bclgn,cbgrpn,bgrcl->bclgrp', cc, prev, jnp.exp(a_cs))
    y = y_diag + y_off + x32 * d_skip.astype(jnp.float32).reshape(g, r)[:, :, None]
    y = y.reshape(bsz, seq, SSD_WIDTH) * jax.nn.silu(z.astype(jnp.float32))
    yg = y.reshape(bsz, seq, g, SSD_WIDTH // g)
    yg = yg * lax.rsqrt(jnp.mean(yg * yg, axis=-1, keepdims=True) + EPS)
    y = yg.reshape(bsz, seq, SSD_WIDTH) * norm_g.astype(jnp.float32)
    return y.astype(z.dtype)

def _normal(k, shape, scale):
    return scale * jax.random.normal(k, shape, jnp.float32)

def first_inputs(seed: int = 0) -> dict:
    key = jax.random.key(seed)
    ks = jax.random.split(key, 32)
    L = DEPTH
    a0 = jax.random.uniform(ks[15], (L, LRU_WIDTH), jnp.float32, minval=0.9, maxval=0.999)
    dt0 = jnp.exp(jax.random.uniform(ks[18], (L, SSD_HEADS), jnp.float32,
                                     minval=math.log(1e-3), maxval=math.log(1e-1)))
    return {
        'x': _normal(ks[0], (BATCH, SEQ, D_MODEL), 1.0),
        'norm_mix_g': 1.0 + _normal(ks[1], (L, D_MODEL), 0.1),
        'w_in': _normal(ks[2], (L, D_MODEL, D_IN), D_MODEL ** -0.5),
        'b_gate': _normal(ks[3], (L, N_BRANCHES, D_MODEL), 0.1),
        'gmlp_ln_g': 1.0 + _normal(ks[4], (L, GMLP_WIDTH), 0.1),
        'gmlp_ln_b': _normal(ks[5], (L, GMLP_WIDTH), 0.1),
        'gmlp_w_s': _normal(ks[6], (L, GMLP_GROUPS, GMLP_CHUNK, GMLP_CHUNK), GMLP_CHUNK ** -0.5),
        'gmlp_b_s': 1.0 + _normal(ks[7], (L, GMLP_GROUPS, GMLP_CHUNK), 0.1),
        'lru_conv_w': _normal(ks[8], (L, CONV_WIDTH, LRU_WIDTH), CONV_WIDTH ** -0.5),
        'lru_conv_b': _normal(ks[9], (L, LRU_WIDTH), 0.1),
        'lru_w_r': _normal(ks[10], (L, LRU_HEADS, LRU_HEAD_DIM, LRU_HEAD_DIM), LRU_HEAD_DIM ** -0.5),
        'lru_b_r': _normal(ks[11], (L, LRU_WIDTH), 0.1),
        'lru_w_i': _normal(ks[12], (L, LRU_HEADS, LRU_HEAD_DIM, LRU_HEAD_DIM), LRU_HEAD_DIM ** -0.5),
        'lru_b_i': _normal(ks[13], (L, LRU_WIDTH), 0.1),
        'lru_lambda': jnp.log(a0) - jnp.log1p(-a0),
        'ssd_conv_w': _normal(ks[16], (L, CONV_WIDTH, SSD_CONV_DIM), CONV_WIDTH ** -0.5),
        'ssd_conv_b': _normal(ks[17], (L, SSD_CONV_DIM), 0.1),
        'ssd_dt_bias': dt0 + jnp.log(-jnp.expm1(-dt0)),
        'ssd_a_log': jnp.log(jax.random.uniform(ks[19], (L, SSD_HEADS), jnp.float32, minval=1.0, maxval=16.0)),
        'ssd_d': 1.0 + _normal(ks[20], (L, SSD_HEADS), 0.1),
        'ssd_norm_g': 1.0 + _normal(ks[21], (L, SSD_WIDTH), 0.1),
        'w_branch_a': _normal(ks[22], (L, GMLP_WIDTH, D_MODEL), GMLP_WIDTH ** -0.5),
        'w_branch_b': _normal(ks[23], (L, LRU_WIDTH, D_MODEL), LRU_WIDTH ** -0.5),
        'w_branch_c': _normal(ks[24], (L, SSD_WIDTH, D_MODEL), SSD_WIDTH ** -0.5),
        'w_out': _normal(ks[25], (L, D_MODEL, D_MODEL), D_MODEL ** -0.5),
        'norm_mlp_g': 1.0 + _normal(ks[26], (L, D_MODEL), 0.1),
        'w_mlp_up': _normal(ks[27], (L, D_MODEL, MLP_HIDDEN), D_MODEL ** -0.5),
        'w_mlp_down': _normal(ks[28], (L, MLP_HIDDEN, D_MODEL), MLP_HIDDEN ** -0.5),
        'final_norm_g': 1.0 + _normal(ks[29], (D_MODEL,), 0.1),
    }

def first_block(x, norm_mix_g, w_in, b_gate, gmlp_ln_g, gmlp_ln_b, gmlp_w_s, gmlp_b_s,
              lru_conv_w, lru_conv_b, lru_w_r, lru_b_r, lru_w_i, lru_b_i, lru_lambda,
              ssd_conv_w, ssd_conv_b, ssd_dt_bias, ssd_a_log, ssd_d, ssd_norm_g,
              w_branch_a, w_branch_b, w_branch_c, w_out, norm_mlp_g, w_mlp_up, w_mlp_down,
              final_norm_g):
    bsz, seq, _ = x.shape
    h = x
    for l in range(DEPTH):
        hn = rms_norm(h, norm_mix_g[l])
        proj = jnp.einsum('bsd,de->bse', hn, w_in[l])
        za, zb, zc, xbc, dt_raw, g_raw = jnp.split(proj, SPLIT_POINTS, axis=-1)
        ya = gmlp_mixer(za, gmlp_ln_g[l], gmlp_ln_b[l], gmlp_w_s[l], gmlp_b_s[l])
        yb = rg_lru_mixer(zb, lru_conv_w[l], lru_conv_b[l], lru_w_r[l], lru_b_r[l],
                          lru_w_i[l], lru_b_i[l], lru_lambda[l])
        yc = ssd_mixer(zc, xbc, dt_raw, ssd_conv_w[l], ssd_conv_b[l], ssd_dt_bias[l],
                       ssd_a_log[l], ssd_d[l], ssd_norm_g[l])
        gates = jax.nn.sigmoid(g_raw.reshape(bsz, seq, N_BRANCHES, D_MODEL) + b_gate[l])
        merged = (gates[:, :, 0] * jnp.einsum('bse,ed->bsd', ya, w_branch_a[l])
                  + gates[:, :, 1] * jnp.einsum('bse,ed->bsd', yb, w_branch_b[l])
                  + gates[:, :, 2] * jnp.einsum('bse,ed->bsd', yc, w_branch_c[l]))
        h = h + jnp.einsum('bsd,de->bse', merged, w_out[l])
        hn = rms_norm(h, norm_mlp_g[l])
        up = jax.nn.relu(jnp.einsum('bsd,df->bsf', hn, w_mlp_up[l]))
        h = h + jnp.einsum('bsf,fd->bsd', up * up, w_mlp_down[l])
    return rms_norm(h, final_norm_g)


HEAD_DIM = 64
ATT_HEADS = 8
ATT_WIDTH = ATT_HEADS * HEAD_DIM
RWKV_HEADS = 8
RWKV_WIDTH = RWKV_HEADS * HEAD_DIM
MIX_WIDTH = ATT_WIDTH + RWKV_WIDTH
D_FF = 2816
N_DIRS = 2
DECAY_LORA = 64
ICLR_LORA = 64
GATE_LORA = 128
DILATED_PATTERNS = ((128, 1), (512, 4), (2048, 16))
ROPE_THETA = 10000.0
NORM_EPS = 1e-6
GN_EPS = 64e-5
ATT_IN = 3 * ATT_WIDTH
RWKV_IN = 3 * RWKV_WIDTH + N_DIRS * DECAY_LORA + N_DIRS * ICLR_LORA + GATE_LORA
IN_WIDTH = ATT_IN + RWKV_IN


def _rmsnorm(x, g):
    xf = x.astype(jnp.float32)
    return xf * lax.rsqrt(jnp.mean(xf * xf, axis=-1, keepdims=True) + NORM_EPS) * g.astype(jnp.float32)

def _swiglu(h, w_gate, w_up, w_down):
    return (jax.nn.silu(h @ w_gate) * (h @ w_up)) @ w_down

def _rope(t, cos, sin):
    half = t.shape[-1] // 2
    t1, t2 = t[..., :half], t[..., half:]
    c, s = cos[None, :, None, :], sin[None, :, None, :]
    return jnp.concatenate([t1 * c - t2 * s, t2 * c + t1 * s], axis=-1)

def _dilated_attention(q, k, v, window, dilation):
    B, S, H, Dh = q.shape
    L = S // dilation
    W = window // (2 * dilation)
    nb = -(-L // W)
    Lp = nb * W
    pad = Lp - L

    def to_sub(t):
        return t.reshape(B, L, dilation, H, Dh).transpose(0, 3, 2, 1, 4)

    qb = jnp.pad(to_sub(q), ((0, 0), (0, 0), (0, 0), (0, pad), (0, 0))).reshape(B, H, dilation, nb, W, Dh)

    def band(t):
        tp = jnp.pad(to_sub(t), ((0, 0), (0, 0), (0, 0), (W, W + pad), (0, 0))).reshape(B, H, dilation, nb + 2, W, Dh)
        return jnp.concatenate([tp[:, :, :, :-2], tp[:, :, :, 1:-1], tp[:, :, :, 2:]], axis=4)

    kb, vb = band(k), band(v)
    blk = jnp.arange(nb)[:, None, None] * W
    qi = blk + jnp.arange(W)[None, :, None]
    ki = blk - W + jnp.arange(3 * W)[None, None, :]
    valid = (jnp.abs(ki - qi) <= W) & (ki >= 0) & (ki < L)

    s = jnp.einsum('bhrnqd,bhrnkd->bhrnqk', qb, kb).astype(jnp.float32)
    s = jnp.where(valid, s, -jnp.inf)
    m = jnp.max(s, axis=-1, keepdims=True)
    p = jnp.exp(s - m)
    den = jnp.sum(p, axis=-1, keepdims=True)
    o = jnp.einsum('bhrnqk,bhrnkd->bhrnqd', p, vb.astype(jnp.float32)) / den
    lse = (m + jnp.log(den))[..., 0]
    o = o.reshape(B, H, dilation, Lp, Dh)[:, :, :, :L].transpose(0, 3, 2, 1, 4).reshape(B, S, H, Dh)
    lse = lse.reshape(B, H, dilation, Lp)[:, :, :, :L].transpose(0, 3, 2, 1).reshape(B, S, H)
    return o, lse

def _attention_group(za, cos, sin, out_g):
    B, S, _ = za.shape
    q, k, v = jnp.split(za, 3, axis=-1)
    q = _rope(q.reshape(B, S, ATT_HEADS, HEAD_DIM), cos, sin) * (HEAD_DIM ** -0.5)
    k = _rope(k.reshape(B, S, ATT_HEADS, HEAD_DIM), cos, sin)
    v = v.reshape(B, S, ATT_HEADS, HEAD_DIM)
    outs, lses = [], []
    for window, dilation in DILATED_PATTERNS:
        o, l = _dilated_attention(q, k, v, window, dilation)
        outs.append(o)
        lses.append(l)
    wts = jax.nn.softmax(jnp.stack(lses, axis=0), axis=0)
    o = jnp.sum(wts[..., None] * jnp.stack(outs, axis=0), axis=0)
    o = o * lax.rsqrt(jnp.mean(o * o, axis=-1, keepdims=True) + NORM_EPS)
    return o.reshape(B, S, ATT_WIDTH) * out_g

def _rwkv7_step(state, inp):
    r, w, k, v, kk, kka = inp
    sa = jnp.einsum('dbhvk,dbhk->dbhv', state, kk)
    state = state * w[..., None, :] - sa[..., :, None] * kka[..., None, :] + v[..., :, None] * k[..., None, :]
    y = jnp.einsum('dbhvk,dbhk->dbhv', state, r)
    return state, y

def _rwkv7_group(u, mu_prev, mu_next, w0, w2, a0, a2, g2, k_k, k_a, r_k, lnx_w, lnx_b):
    B, S, _ = u.shape
    H, N, C = RWKV_HEADS, HEAD_DIM, RWKV_WIDTH
    u = u.astype(jnp.float32)
    prev = jnp.pad(u, ((0, 0), (1, 0), (0, 0)))[:, :-1]
    nxt = jnp.pad(u, ((0, 0), (0, 1), (0, 0)))[:, 1:]
    u = u + mu_prev * (prev - u) + mu_next * (nxt - u)
    cuts = np.cumsum([C, C, C, N_DIRS * DECAY_LORA, N_DIRS * ICLR_LORA]).tolist()
    r, k, v, wd, ad, gd = jnp.split(u, cuts, axis=-1)
    wd = wd.reshape(B, S, N_DIRS, DECAY_LORA)
    ad = ad.reshape(B, S, N_DIRS, ICLR_LORA)
    w_logit = w0 + jnp.einsum('bsdr,drc->bsdc', jnp.tanh(wd), w2)
    decay = jnp.exp(-jnp.exp(-jax.nn.softplus(-w_logit) - 0.5))
    a = jax.nn.sigmoid(a0 + jnp.einsum('bsdr,drc->bsdc', ad, a2))
    g = jax.nn.sigmoid(gd) @ g2
    kk = (k * k_k).reshape(B, S, H, N)
    kk = kk / jnp.maximum(jnp.sqrt(jnp.sum(kk * kk, axis=-1, keepdims=True)), 1e-12)
    kk = kk.reshape(B, S, C)
    k_dir = k[:, :, None, :] * (1.0 + (a - 1.0) * k_a)

    def both(t):
        return jnp.broadcast_to(t[:, :, None, :], (B, S, N_DIRS, C))

    def orient(t):
        t = jnp.concatenate([t[:, :, :1], jnp.flip(t[:, :, 1:], axis=1)], axis=2)
        return t.reshape(B, S, N_DIRS, H, N).transpose(1, 2, 0, 3, 4)

    xs = (orient(both(r)), orient(decay), orient(k_dir), orient(both(v)),
          orient(both(kk)), orient(kk[:, :, None, :] * a))
    state0 = jnp.zeros((N_DIRS, B, H, N, N), jnp.float32)
    _, ys = lax.scan(_rwkv7_step, state0, xs)
    ys = ys.transpose(2, 0, 1, 3, 4)
    y = ys[:, :, 0] + jnp.flip(ys[:, :, 1], axis=1)
    mu = jnp.mean(y, axis=-1, keepdims=True)
    var = jnp.mean(jnp.square(y - mu), axis=-1, keepdims=True)
    y = ((y - mu) * lax.rsqrt(var + GN_EPS)).reshape(B, S, C) * lnx_w + lnx_b
    bonus = jnp.einsum('bshn,bsdhn,hn->bsh', r.reshape(B, S, H, N),
                       k_dir.reshape(B, S, N_DIRS, H, N), r_k) / N_DIRS
    y = y + (bonus[..., None] * v.reshape(B, S, H, N)).reshape(B, S, C)
    return y * g

def second_inputs(seed: int = 0) -> dict:
    key = jax.random.key(seed)
    keys = iter(jax.random.split(key, 40))

    def rnd(shape, scale):
        return scale * jax.random.normal(next(keys), (DEPTH,) + shape, jnp.float32)

    def gain(shape):
        return 1.0 + rnd(shape, 0.05)

    def unif(shape, lo, hi):
        return jax.random.uniform(next(keys), (DEPTH,) + shape, jnp.float32, lo, hi)

    x = jax.random.normal(next(keys), (BATCH, SEQ, D_MODEL), jnp.float32)
    return {
        "x": x,
        "ffn1_pre_g": gain((D_MODEL,)),
        "ffn1_w_gate": rnd((D_MODEL, D_FF), D_MODEL ** -0.5),
        "ffn1_w_up": rnd((D_MODEL, D_FF), D_MODEL ** -0.5),
        "ffn1_w_down": rnd((D_FF, D_MODEL), D_FF ** -0.5),
        "ffn1_post_g": gain((D_MODEL,)),
        "mix_pre_g": gain((D_MODEL,)),
        "w_in": rnd((D_MODEL, IN_WIDTH), D_MODEL ** -0.5),
        "rwkv_mu_prev": unif((RWKV_IN,), 0.0, 0.5),
        "rwkv_mu_next": unif((RWKV_IN,), 0.0, 0.5),
        "rwkv_w0": unif((N_DIRS, RWKV_WIDTH), -4.0, 1.0),
        "rwkv_w2": rnd((N_DIRS, DECAY_LORA, RWKV_WIDTH), 0.5 * DECAY_LORA ** -0.5),
        "rwkv_a0": rnd((N_DIRS, RWKV_WIDTH), 0.3),
        "rwkv_a2": rnd((N_DIRS, ICLR_LORA, RWKV_WIDTH), 0.5 * ICLR_LORA ** -0.5),
        "rwkv_g2": rnd((GATE_LORA, RWKV_WIDTH), GATE_LORA ** -0.5),
        "rwkv_k_k": 0.85 + rnd((RWKV_WIDTH,), 0.05),
        "rwkv_k_a": gain((RWKV_WIDTH,)),
        "rwkv_r_k": rnd((RWKV_HEADS, HEAD_DIM), 0.1),
        "rwkv_lnx_w": gain((RWKV_WIDTH,)),
        "rwkv_lnx_b": rnd((RWKV_WIDTH,), 0.02),
        "attn_out_g": gain((ATT_WIDTH,)),
        "w_out": rnd((MIX_WIDTH, D_MODEL), MIX_WIDTH ** -0.5),
        "mix_post_g": gain((D_MODEL,)),
        "ffn2_pre_g": gain((D_MODEL,)),
        "ffn2_w_gate": rnd((D_MODEL, D_FF), D_MODEL ** -0.5),
        "ffn2_w_up": rnd((D_MODEL, D_FF), D_MODEL ** -0.5),
        "ffn2_w_down": rnd((D_FF, D_MODEL), D_FF ** -0.5),
        "ffn2_post_g": gain((D_MODEL,)),
    }

def second_block(x, ffn1_pre_g, ffn1_w_gate, ffn1_w_up, ffn1_w_down, ffn1_post_g,
              mix_pre_g, w_in,
              rwkv_mu_prev, rwkv_mu_next, rwkv_w0, rwkv_w2, rwkv_a0, rwkv_a2, rwkv_g2,
              rwkv_k_k, rwkv_k_a, rwkv_r_k, rwkv_lnx_w, rwkv_lnx_b,
              attn_out_g, w_out, mix_post_g,
              ffn2_pre_g, ffn2_w_gate, ffn2_w_up, ffn2_w_down, ffn2_post_g):
    S = x.shape[1]
    pos = jnp.arange(S, dtype=jnp.float32)
    inv_freq = ROPE_THETA ** (-jnp.arange(0, HEAD_DIM, 2, dtype=jnp.float32) / HEAD_DIM)
    ang = pos[:, None] * inv_freq[None, :]
    cos, sin = jnp.cos(ang), jnp.sin(ang)

    h = x.astype(jnp.float32)
    for l in range(DEPTH):
        f = _swiglu(_rmsnorm(h, ffn1_pre_g[l]), ffn1_w_gate[l], ffn1_w_up[l], ffn1_w_down[l])
        h = h + 0.5 * _rmsnorm(f, ffn1_post_g[l])
        z = _rmsnorm(h, mix_pre_g[l]) @ w_in[l]
        y_att = _attention_group(z[..., :ATT_IN], cos, sin, attn_out_g[l])
        y_rwkv = _rwkv7_group(z[..., ATT_IN:], rwkv_mu_prev[l], rwkv_mu_next[l], rwkv_w0[l], rwkv_w2[l],
                              rwkv_a0[l], rwkv_a2[l], rwkv_g2[l], rwkv_k_k[l], rwkv_k_a[l], rwkv_r_k[l],
                              rwkv_lnx_w[l], rwkv_lnx_b[l])
        mix = jnp.concatenate([y_att, y_rwkv], axis=-1) @ w_out[l]
        h = h + _rmsnorm(mix, mix_post_g[l])
        f = _swiglu(_rmsnorm(h, ffn2_pre_g[l]), ffn2_w_gate[l], ffn2_w_up[l], ffn2_w_down[l])
        h = h + 0.5 * _rmsnorm(f, ffn2_post_g[l])
    return h.astype(x.dtype)


def setup_inputs(seed=0):
    out = dict(first_inputs(seed))
    for name, value in second_inputs(seed + 1).items():
        if name != "x":
            out[name + "_2"] = value
    return out


def reference(
    x, norm_mix_g, w_in, b_gate, gmlp_ln_g, gmlp_ln_b, gmlp_w_s, gmlp_b_s, lru_conv_w,
    lru_conv_b, lru_w_r, lru_b_r, lru_w_i, lru_b_i, lru_lambda, ssd_conv_w, ssd_conv_b,
    ssd_dt_bias, ssd_a_log, ssd_d, ssd_norm_g, w_branch_a, w_branch_b, w_branch_c, w_out,
    norm_mlp_g, w_mlp_up, w_mlp_down, final_norm_g, ffn1_pre_g_2, ffn1_w_gate_2, ffn1_w_up_2,
    ffn1_w_down_2, ffn1_post_g_2, mix_pre_g_2, w_in_2, rwkv_mu_prev_2, rwkv_mu_next_2,
    rwkv_w0_2, rwkv_w2_2, rwkv_a0_2, rwkv_a2_2, rwkv_g2_2, rwkv_k_k_2, rwkv_k_a_2, rwkv_r_k_2,
    rwkv_lnx_w_2, rwkv_lnx_b_2, attn_out_g_2, w_out_2, mix_post_g_2, ffn2_pre_g_2,
    ffn2_w_gate_2, ffn2_w_up_2, ffn2_w_down_2, ffn2_post_g_2,
):
    x = first_block(
        x, norm_mix_g, w_in, b_gate, gmlp_ln_g, gmlp_ln_b, gmlp_w_s, gmlp_b_s, lru_conv_w,
        lru_conv_b, lru_w_r, lru_b_r, lru_w_i, lru_b_i, lru_lambda, ssd_conv_w, ssd_conv_b,
        ssd_dt_bias, ssd_a_log, ssd_d, ssd_norm_g, w_branch_a, w_branch_b, w_branch_c, w_out,
        norm_mlp_g, w_mlp_up, w_mlp_down, final_norm_g,
    )
    return second_block(
        x, ffn1_pre_g_2, ffn1_w_gate_2, ffn1_w_up_2, ffn1_w_down_2, ffn1_post_g_2, mix_pre_g_2,
        w_in_2, rwkv_mu_prev_2, rwkv_mu_next_2, rwkv_w0_2, rwkv_w2_2, rwkv_a0_2, rwkv_a2_2,
        rwkv_g2_2, rwkv_k_k_2, rwkv_k_a_2, rwkv_r_k_2, rwkv_lnx_w_2, rwkv_lnx_b_2, attn_out_g_2,
        w_out_2, mix_post_g_2, ffn2_pre_g_2, ffn2_w_gate_2, ffn2_w_up_2, ffn2_w_down_2,
        ffn2_post_g_2,
    )


_drawn_inputs = setup_inputs


def setup_inputs(seed=0):
    import zlib

    import numpy as np

    out = dict(_drawn_inputs(seed))
    spreads = {}
    factors = {'lru_b_r': 8.0,
     'lru_b_i': 6.653,
     'rwkv_w2_2': 2.798,
     'rwkv_k_k_2': 2.768,
     'rwkv_lnx_w_2': 3.679,
     'rwkv_lnx_b_2': 22.2,
     'ffn2_post_g_2': 3.543,
     'attn_out_g_2': 2.824,
     'rwkv_r_k_2': 2.892}
    for name, (base, spread) in spreads.items():
        noise = np.random.default_rng([zlib.crc32(name.encode()), seed]).standard_normal(out[name].shape)
        drawn = base * np.exp(spread * noise) if base else spread * noise
        out[name] = __import__('jax').numpy.asarray(drawn.astype(out[name].dtype))
    for name, factor in factors.items():
        out[name] = (out[name] * factor).astype(out[name].dtype)
    return out
```

```python
from contextlib import ExitStack

import numpy as np

import concourse.bass as bass
from concourse import mybir

F32 = mybir.dt.float32
F32R = mybir.dt.float32r
ALU = mybir.AluOpType
ACT = mybir.ActivationFunctionType
AX_X = mybir.AxisListType.X

P = 128
T = 256
D = 1024
KB = D // P
CH = 128
NCH = T // CH
RING = 4
TILE = KB * P
EPS = 1e-6
GN_EPS = 64e-5

SSD_HEADS = 16
SSD_P = 64
GROUPS = 4
ATT_HEADS = 8
HD = 64
AB = 4
RC = 64
NRC = T // RC
FF2_CHUNKS = (8, 8, 6)
UP_CHUNKS = 4

COLS = {}
_n = 0
for _name, _width in (
    ("norm_mix_g", 8), ("b_gate", 24), ("gmlp_ln_g", 8), ("gmlp_ln_b", 8), ("lru_conv_w", 32),
    ("lru_conv_b", 8), ("lru_b_r", 8), ("lru_b_i", 8), ("lru_lambda", 8), ("ssd_conv_w", 64),
    ("ssd_conv_b", 16), ("ssd_d", 8), ("ssd_norm_g", 8), ("norm_mlp_g", 8), ("final_norm_g", 8),
    ("ffn1_pre_g_2", 8), ("ffn1_post_g_2", 8), ("mix_pre_g_2", 8), ("rwkv_mu_prev_2", 15),
    ("rwkv_mu_next_2", 15), ("rwkv_w0_2", 8), ("rwkv_a0_2", 8), ("rwkv_k_k_2", 4), ("rwkv_k_a_2", 4),
    ("rwkv_r_k_2", 4), ("rwkv_lnx_w_2", 4), ("rwkv_lnx_b_2", 4), ("attn_out_g_2", 4),
    ("mix_post_g_2", 8), ("ffn2_pre_g_2", 8), ("ffn2_post_g_2", 8),
):
    COLS[_name] = _n
    _n += _width
NCOLS = _n


class Segment:

    def __init__(self, name, dram, first, n, start, operand, kt):
        self.name, self.dram, self.first, self.n = name, dram, first, n
        self.start, self.operand, self.kt = start, operand, kt


class Operand:

    def __init__(self, base, n, parts):
        self.base, self.n, self.free = base, n, 0
        self.hi, self.lo = parts


class Kit:
    pass


def plan():
    segments, start = [], 0

    def seg(name, dram, first, n, operand, kt=KB):
        nonlocal start
        segments.append(Segment(name, dram, first, n, start, operand, kt))
        start += n

    seg("xbc", "w_in", 40, 16, "hn")
    seg("z", "w_in", 32, 8, "hn")
    seg("v", "w_in", 8, 8, "hn")
    seg("u", "w_in", 0, 8, "hn")
    seg("xb", "w_in", 16, 8, "hn")
    seg("gt", "w_in", 24, 8, "hn")
    seg("gate_c", "w_in", 72, 8, "hn")
    seg("branch_c", "w_branch_c", 0, 8, "y_c")
    seg("gate_a", "w_in", 56, 8, "hn")
    seg("branch_a", "w_branch_a", 0, 8, "y_a")
    seg("gate_b", "w_in", 64, 8, "hn")
    seg("branch_b", "w_branch_b", 0, 8, "y_b")
    seg("out", "w_out", 0, 8, "merged")

    def mlp(kind, ups, up_dram, down_drams, operand, per):
        def up(c):
            first = sum(ups[:c]) * per
            seg(f"{kind}_up{c}", up_dram, first, ups[c] * per, operand)

        def down(c):
            seg(f"{kind}_down{c}", down_drams[c][0], down_drams[c][1], 8, f"{kind}_hid{c}", ups[c])

        up(0)
        for c in range(1, len(ups)):
            up(c)
            down(c - 1)
        down(len(ups) - 1)

    mlp("mlp", (8,) * UP_CHUNKS, "w_mlp_up", [("w_mlp_down", 8 * c) for c in range(UP_CHUNKS)], "hn_mlp", 1)
    mlp("ffn1", FF2_CHUNKS, "ffn1_gu", [("ffn1_down", 0), ("ffn1_down", 8), ("ffn1_down_tail", 0)], "hn_ffn1", 2)
    seg("rwkv_in", "w_in_2", 12, 15, "hn_mix")
    seg("qkv", "w_in_2", 0, 12, "hn_mix")
    seg("out_2", "w_out_2", 0, 8, "y_mix")
    mlp("ffn2", FF2_CHUNKS, "ffn2_gu", [("ffn2_down", 0), ("ffn2_down", 8), ("ffn2_down_tail", 0)], "hn_ffn2", 2)
    return segments


OPERANDS = [("hn", 8, "A"), ("y_c", 8, "B0"), ("y_a", 8, "B1"), ("y_b", 8, "B0"), ("merged", 8, "A"),
            ("hn_mlp", 8, "A")]
OPERANDS += [(f"mlp_hid{c}", 8, f"B{c % 2}") for c in range(UP_CHUNKS)]
OPERANDS += [("hn_ffn1", 8, "A")]
OPERANDS += [(f"ffn1_hid{c}", n, f"B{c % 2}") for c, n in enumerate(FF2_CHUNKS)]
OPERANDS += [("hn_mix", 8, "A"), ("y_mix", 8, "B0"), ("hn_ffn2", 8, "A")]
OPERANDS += [(f"ffn2_hid{c}", n, f"B{c % 2}") for c, n in enumerate(FF2_CHUNKS)]


ACT_SEGMENTS = [("z", 8), ("v", 8), ("u", 8), ("gt", 8), ("gate_c", 8), ("gate_a", 8), ("gate_b", 8)]
ACT_SEGMENTS += [(f"{f}_up{c}", n) for f in ("ffn1", "ffn2") for c, n in enumerate(FF2_CHUNKS)]

CONST_DMAS = 10


def tiles(eng, n, peel=False):
    first = 1 if peel else 0
    for i in range(first * RING):
        yield i, i % RING, i // RING
    groups = n // RING - first
    if groups > 1:
        with eng.Fori(first, first + groups) as q:
            for j in range(RING):
                yield q * RING + j, j, q
        done = n // RING * RING
    else:
        done = first * RING
    for i in range(done, n):
        yield i, i % RING, i // RING


def at(eng, i, size=1):
    return bass.ds(i * size, size)


class Steps:

    def __init__(self, eng, sem):
        self.eng, self.sem, self.n = eng, sem, 0

    def do(self, ins):
        ins.then_inc(self.sem, 1)
        self.n += 1

    def settle(self, back=0):
        self.eng.wait_ge(self.sem, self.n - back)


SMALL_EVENTS = (
    "x_in consts_in lru_w_in step_v step_a sq rms_mm rms_sqrt hi_ready lo_ready tiles_used evacuated "
    "act_out op_ready zeroed ssd_silu conv_done rs_col_mm dt_mm rs_ready sp_z sp_exp sp_ln sp_u adt acs_mm acs "
    "ds_exp xs_tr xs_ev b_tr b_ev cb_mm cbm xdec st_mm st_ev rb_mm e_min e_exp ex_exp mt ce y_mm y_ev "
    "yz gn_sq gn_mm gn_sqrt gn_done "
    "v_sum_mm v_cent v_sq v_var_mm v_sqrt v_scaled v_norm v_tr v_ev gws mix_mm mix_ev "
    "merged lru_conv ri_mm ri_sig lru_at lru_q lru_sqrt lru_done ssd_done "
    "hid_t hid_w "
    "x_final "
    "rope_in att_in rwkv_in masks_in shifted lora_in w_mm w_sig a_mm a_sig g_mm g_ev kk_sq kk_mm kk_sqrt "
    "lw_scan l_ex ex_exp2 n_exp p_exp bonus_in bonus_mm rope_mm rope_ev "
    "vt_tr vt_ev s_mm s_ev s_red s_exp p_tr p_ev o_mm o_sq o_sqrt o_fin o_tr "
    "zv zv_mm zv_ev z_made za_made zq_made gb_mm gc_mm gb_ev gc_ev y_taken tok_tr tok_ev zn u_mm uc_ev zu_ev t_mm t_ev tt_mm tt_ev ztt "
    "x_mm x_ev sa_mm sa_ev yy_mm yy_ev ss_mm ss_ev zy zy_mm y_fm mu_mm y_cent y_sq var_mm y_sqrt out_done"
).split()


def allocate(nc, ctx):
    k = Kit()
    k.nc = nc

    def sb(name, shape, dtype=F32):
        return ctx.enter_context(nc.sbuf_tensor(name, shape, dtype))

    k.raw = sb("raw_ring", [P, RING, TILE])
    k.whi = sb("weight_hi", [P, RING, TILE], F32R)
    k.wlo = sb("weight_lo", [P, RING, TILE], F32R)
    k.x = sb("x_stream", [P, KB, T])
    k.cols = sb("cols", [P, NCOLS])
    k.ones = sb("ones", [P, P])
    k.ident = sb("ident", [P, P])
    k.tri = sb("tri", [P, P])
    k.blk = sb("block_ones", [P, P])
    k.rs = sb("rs", [P, T])
    k.sd = sb("sd", [P, T])
    k.eps = sb("eps", [P, 2])
    k.rv = sb("rv", [P, T])
    k.wdt = sb("dt_weight", [P, KB, 16])
    k.wdt_hi = sb("dt_weight_hi", [P, KB, 16], F32R)
    k.wdt_lo = sb("dt_weight_lo", [P, KB, 16], F32R)
    k.pre = sb("pre", [P, RING, T])
    k.small = sb("small", [P, 640])
    arena_floats = 22592
    arena_at = -(-nc.sbuf_base // 32) * 32
    k.arena = sb("arena", [P, arena_floats + 6 * KB * T])
    k.operand = {}
    for n, name in enumerate(("A", "B0", "B1")):
        off = arena_at + 4 * (arena_floats + 2 * n * KB * T)
        k.operand[name] = [
            nc.alloc_sbuf_tensor_at(f"operand_{name}_{part}", [P, KB, T], F32R, offset=off + 4 * h * KB * T)
            for h, part in enumerate(("hi", "lo"))]
    k.slots = [ctx.enter_context(nc.psum_tensor(f"product{i}", [P, 512], F32)) for i in range(RING)]
    k.bank = [ctx.enter_context(nc.psum_tensor(f"bank{i}", [P, 512], F32)) for i in range(4)]
    k.half_bank = [k.bank, k.slots]
    k.landed = [ctx.enter_context(nc.semaphore(f"landed{i}")) for i in range(RING)]
    k.s = {name: ctx.enter_context(nc.semaphore(name)) for name in SMALL_EVENTS}
    k.segs = {g.name: g for g in plan()}
    k.total = sum(g.n for g in k.segs.values())
    k.made, n = {}, 0
    for name, blocks, buf in OPERANDS:
        k.made[name] = Operand(n, blocks, k.operand[buf])
        n += blocks

    last_use = {}
    for name, _, buf in OPERANDS:
        k.made[name].free = last_use.get(buf, 0)
        last_use[buf] = max([g.start + g.n for g in k.segs.values() if g.operand == name], default=0)

    k.act_before, k.act_after, n = {}, {}, 0
    for name, blocks in ACT_SEGMENTS:
        k.act_before[name], n = n, n + blocks
        k.act_after[name] = n

    def region(start, blocks, width=T):
        return k.arena[:, start:start + blocks * width].rearrange("p (b t) -> p b t", b=blocks)

    pad = T + 3
    k.xbc_pad = region(0, 16, pad)
    k.xdt = region(0, NCH, D)
    k.xdec = k.arena[:, 2048:3072]
    k.state = k.arena[:, 3072:4096]
    k.gm_sq = region(0, 8)
    k.xc = region(4144, 16)
    k.z = region(8240, 8)
    k.v = region(10288, 8)
    k.u = region(12336, 8)
    k.xb_pad = region(2048, 8, pad)
    k.gt = region(14384, 8)
    k.g = region(16432, 8)
    k.mt = region(16432, 2)
    k.ex = region(16432 + 512, 2, P)
    k.ce = region(16432 + 768, 2, P)
    k.gn_sq = k.gt
    k.vt = region(4144, NCH, D)
    k.m = region(18480, 8)
    k.cbm = region(18480, NCH * GROUPS, P)
    k.bt = k.arena[:, 18480 + 1024:18480 + 1536]
    k.e = region(18480 + 1536, 2)
    k.gn_rs = k.arena[:, 18480:18480 + 512]
    k.gmix = k.arena[:, 18480 + 512:18480 + 1024]
    k.gn_sd = region(18480 + 1024, 2, 512)
    k.wr = region(20528, 8, P)
    k.wi = region(21552, 8, P)
    k.gws = region(20528, 8, P)
    k.bs = region(21552, 8, P)
    k.xb = k.v
    k.r = region(4144, 8)
    k.i = region(4144 + 2048, 8)
    k.a = region(0, 8)
    k.t = region(2048, 8)
    k.sq0 = k.v
    k.sq = k.g
    k.f = k.z
    k.hid = k.v
    k.sg = k.u

    k.stack = sb("stacked_identity", [P, RC])
    k.us = region(0, 15)
    k.upad = region(3840, 15, T + 2)
    k.qkv = region(7712, 12)
    k.gout = region(3072, 4)
    k.lw = region(4096, 8)
    k.kk = region(6144, 4)
    k.reset = k.arena[:, 20000:21024]
    k.bv = region(1024, 4)
    k.y_att = region(10784, 4)
    k.ia = region(11808, 8)
    k.lc = region(13856, 8)
    k.lx = region(15904, 8)
    k.en = region(17952, 8)
    k.kd = region(20000, 8)
    tail = arena_floats
    k.cbaq = k.arena[:, tail + 4096:tail + 12288].rearrange("p (w d b t) -> p w d b t", w=4, d=2, b=AB)
    k.att_v = region(tail, NCH, 512)
    k.att_s = region(tail + 1024, 2, 512)
    k.att_p = region(tail + 2048, 2, 512)
    k.att_o = region(tail + 3072, NCH, 512)
    k.att_mask = region(22048, 2)
    units = lambda start, width: region(start, 8, width)
    k.zc, k.zb, k.za, k.zq = (units(4096 + 1024 * n, P) for n in range(4))
    k.vtok = k.arena[:, 0:1024].rearrange("p (b c v) -> p b c v", b=AB, c=NRC)
    k.ytok = k.arena[:, 8736:9760].rearrange("p (b c v) -> p b c v", b=AB, c=NRC)
    k.xs, k.sa = units(9760, RC), units(10272, RC)
    k.st, k.nt, k.tc, k.ttc = (units(11808 + 512 * n, RC) for n in range(4))
    k.ztt, k.uc, k.zu, k.zn = units(13856, P), units(14880, RC), units(15392, P), units(16416, P)
    k.zaac, k.zaqc, k.zaqb = (units(17440 + 1024 * n, P) for n in range(3))
    k.ctok, k.btok = units(20512, P), units(21536, P)
    k.levels = k.arena[:, tail:tail + 1536].rearrange("p (d l h t) -> p d l h t", d=2, l=6, h=2)
    k.causal = k.arena[:, tail + 1536:tail + 2048].rearrange("p (d s h t) -> p d s h t", d=2, s=2, h=2)
    k.masks = k.arena[:, tail:tail + 2304]
    k.lvl0 = k.arena[:, tail + 2048:tail + 2176].rearrange("p (d t) -> p d t", d=2)
    k.strict = k.arena[:, tail + 2176:tail + 2304].rearrange("p (d t) -> p d t", d=2)
    k.yf = units(13856, P)
    k.ysq = units(15392, P)
    k.ymu = units(17440, P)
    k.lora = k.arena[:, tail + 10240:tail + 11776].rearrange("p (w n) -> p w n", w=3)
    return k


def col(k, name, b=0):
    c = COLS[name] + b
    return k.cols[:, c:c + 1]


class Small:

    def __init__(self, k):
        s = k.small
        self.rs_col = s[:, 0:2]
        self.z = s[:, 8:48]
        self.ab = s[:, 48:88]
        self.e = s[:, 88:128]
        self.u = s[:, 128:168]
        self.um = s[:, 168:208]
        self.d = s[:, 208:248]
        self.ru = s[:, 248:288]
        self.ln = s[:, 288:328]
        self.sp = s[:, 328:368]
        self.ea = s[:, 368:384]
        self.adt = s[:, 384:416]
        self.acs = s[:, 416:448]
        self.dz = s[:, 448:464]
        self.ds = s[:, 464:480]
        self.dtb = s[:, 480:496]
        self.alog = s[:, 496:512]
        self.dtb_alog = s[:, 480:512]
        self.nsp8 = s[:, 512:520]
        self.psp8 = s[:, 520:528]


def sync_program(k, sp, a, out):
    for seg in k.segs.values():
        w = seg.kt * P
        for i, j, _ in tiles(sp, seg.n, peel=seg.start == 0):
            slot = (seg.start + j) % RING
            if seg.start or not isinstance(i, int) or i >= RING:
                sp.wait_ge(k.s["lo_ready"], i + (seg.start - RING + 1))
            src = a[seg.dram][at(sp, i + seg.first), :, :].rearrange("o p n -> p (o n)")
            sp.dma_start(k.raw[:, slot, 0:w], src).then_inc(k.landed[slot], 16)
    sp.wait_ge(k.s["out_done"], 1)
    sp.dma_start(out, k.x[:]).then_inc(k.s["x_in"], 16)
    sp.wait_ge(k.s["x_in"], 32)


def gpsimd_program(k, pool):
    for t, slot, _ in tiles(pool, k.total):
        pool.wait_ge(k.s["hi_ready"], t + 1)
        k.nc.gpsimd.tensor_tensor(k.wlo[:, slot, :], k.raw[:, slot, :], k.whi[:, slot, :].bitcast(F32),
                                  ALU.subtract).then_inc(k.s["lo_ready"], 1)


def dense(k, pe, name):
    seg = k.segs[name]
    op = k.made[seg.operand]
    mm = k.nc.tensor.matmul
    for i, j, _ in tiles(pe, seg.n, peel=seg.start == 0):
        slot = (seg.start + j) % RING
        pe.wait_ge(k.s["lo_ready"], i + (seg.start + 1))
        if seg.start or not isinstance(i, int) or i >= RING:
            pe.wait_ge(k.s["evacuated"], i + (seg.start - RING + 1))
        w_hi, w_lo, ps = k.whi[:, slot, :], k.wlo[:, slot, :], k.slots[slot][:, 0:T]
        for b in range(seg.kt):
            if j == 0:
                pe.wait_ge(k.s["op_ready"], op.base + b + 1)
            n = slice(b * P, (b + 1) * P)
            mm(ps, w_hi[:, n], op.hi[:, b, :], start=b == 0, stop=False)
            mm(ps, w_hi[:, n], op.lo[:, b, :], start=False, stop=False)
            last = mm(ps, w_lo[:, n], op.hi[:, b, :], start=False, stop=b == seg.kt - 1)
        last.then_inc(k.s["tiles_used"], 1)


def column_sums(k, src, blocks, bank, weights=None):
    for b in range(blocks):
        last = k.nc.tensor.matmul(bank, (weights or k.ones)[:], src[:, b, :], start=b == 0, stop=b == blocks - 1)
    return last


def tensor_program(k, pe):
    s, mm, c = k.s, k.nc.tensor.matmul, Small(k)
    pe.wait_ge(s["consts_in"], 16 * CONST_DMAS)

    norms = [0]

    def rms_sums(src):
        norms[0] += 1
        pe.wait_ge(s["sq"], 2 * norms[0])
        column_sums(k, src, KB, k.bank[0][:, 0:T]).then_inc(s["rms_mm"], 1)

    rms_sums(k.sq0)
    dense(k, pe, "xbc")
    dense(k, pe, "z")

    for ch in range(NCH):
        last = mm(k.bank[1][:, ch:ch + 1], k.rs[:, ch * P:(ch + 1) * P], k.ident[:, 0:1], start=True, stop=True)
    last.then_inc(s["rs_col_mm"], 1)
    op = k.made["hn"]
    for ch in range(NCH):
        tok = slice(ch * P, (ch + 1) * P)
        for b in range(KB):
            ps = k.bank[2][:, ch * 16:ch * 16 + 16]
            mm(ps, op.hi[:, b, tok], k.wdt_hi[:, b, :], start=b == 0, stop=False)
            mm(ps, op.lo[:, b, tok], k.wdt_hi[:, b, :], start=False, stop=False)
            last = mm(ps, op.hi[:, b, tok], k.wdt_lo[:, b, :], start=False, stop=b == KB - 1)
    last.then_inc(s["dt_mm"], 1)
    dense(k, pe, "v")
    dense(k, pe, "u")

    pe.wait_ge(s["adt"], 1)
    mm(k.bank[1][:, 0:32], k.tri[:], c.adt, start=True, stop=True)
    mm(k.bank[1][:, 32:64], k.ones[:], c.adt, start=True, stop=True).then_inc(s["acs_mm"], 1)
    pe.wait_ge(s["ssd_silu"], 4)
    for n in range(4):
        ch, half = n // 2, n % 2
        if n >= 2:
            pe.wait_ge(s["xs_ev"], n - 1)
        for b in range(4):
            last = k.nc.tensor.transpose(k.bank[2 + n % 2][:, b * P:(b + 1) * P],
                                         k.xc[:, half * 4 + b, ch * P:(ch + 1) * P], k.ident[:])
        last.then_inc(s["xs_tr"], 1)
    pe.wait_ge(s["xs_ev"], 3)
    for g in range(GROUPS):
        last = k.nc.tensor.transpose(k.bank[2][:, g * P:(g + 1) * P], k.xc[:, 8 + g, 0:P], k.ident[:])
    last.then_inc(s["b_tr"], 1)
    for ch in range(NCH):
        if ch == 0:
            pe.wait_ge(s["xs_ev"], 4)
        else:
            pe.wait_ge(s["b_ev"], 1)
        for g in range(GROUPS):
            tok = slice(ch * P, (ch + 1) * P)
            last = mm(k.bank[3 - ch][:, g * P:(g + 1) * P], k.xc[:, 8 + g, tok], k.xc[:, 12 + g, tok],
                      start=True, stop=True)
        last.then_inc(s["cb_mm"], 1)
    pe.wait_ge(s["xdec"], 1)
    pe.wait_ge(s["acs"], 1)
    for half in range(2):
        if half == 1:
            pe.wait_ge(s["cbm"], 2)
        for g in range(2):
            gg = half * 2 + g
            last = mm(k.bank[(1, 2)[half]][:, g * 256:(g + 1) * 256], k.bt[:, gg * P:(gg + 1) * P],
                      k.xdec[:, gg * 256:(gg + 1) * 256], start=True, stop=True)
        last.then_inc(s["st_mm"], 1)
    pe.wait_ge(s["st_ev"], 2)

    def rb(h):
        if h >= 2:
            pe.wait_ge(s["e_min"], h - 1)
            pe.wait_ge(s["ex_exp"], h - 1)
        for ch in range(NCH):
            last = mm(k.bank[h % 2][:, ch * P:(ch + 1) * P],
                      c.adt[:, ch * 16 + h:ch * 16 + h + 1].to_broadcast([P, P]), k.tri[:],
                      start=True, stop=True)
        last.then_inc(s["rb_mm"], 1)

    rb(0)
    for h in range(SSD_HEADS):
        if h + 1 < SSD_HEADS:
            rb(h + 1)
        b, q = h // 2, 64 * (h % 2)
        y = k.bank[2 + b % 2]
        if h % 2 == 0 and b >= 2:
            pe.wait_ge(s["y_ev"], b - 1)
        pe.wait_ge(s["ce"], h + 1)
        mm(y[q:q + 64, 0:P], k.xdt[:, 0, h * 64:h * 64 + 64], k.mt[:, h % 2, 0:P], start=True, stop=True)
        mm(y[q:q + 64, P:T], k.xdt[:, 1, h * 64:h * 64 + 64], k.mt[:, h % 2, P:T], start=True, stop=False)
        mm(y[q:q + 64, P:T], k.state[:, h * 64:h * 64 + 64], k.ce[:, h % 2, :], start=False,
           stop=True).then_inc(s["y_mm"], 1)
    dense(k, pe, "xb")
    for g in range(GROUPS):
        pe.wait_ge(s["gn_sq"], g + 1)
        column_sums(k, k.gn_sq[:, 2 * g:2 * g + 2, :], 2, k.bank[g // 2][:, (g % 2) * T:(g % 2 + 1) * T]).then_inc(s["gn_mm"], 1)
    pe.wait_ge(s["act_out"], k.act_after["v"])
    pe.wait_ge(s["y_ev"], 8)
    column_sums(k, k.v, KB, k.bank[2][:, 0:T]).then_inc(s["v_sum_mm"], 1)
    dense(k, pe, "gt")
    pe.wait_ge(s["v_sq"], 2)
    column_sums(k, k.gm_sq, KB, k.bank[3][:, 0:T]).then_inc(s["v_var_mm"], 1)
    dense(k, pe, "gate_c")
    pe.wait_ge(s["gn_done"], 2)
    pe.wait_ge(s["v_norm"], KB)
    for n in range(4):
        ch, half = n // 2, n % 2
        if n >= 2:
            pe.wait_ge(s["v_ev"], n - 1)
        for b in range(4):
            last = k.nc.tensor.transpose(k.bank[n % 2][:, b * P:(b + 1) * P],
                                         k.v[:, half * 4 + b, ch * P:(ch + 1) * P], k.ident[:])
        last.then_inc(s["v_tr"], 1)
    pe.wait_ge(s["gws"], 1)
    pe.wait_ge(s["v_ev"], 4)
    for n in range(4):
        if n >= 2:
            pe.wait_ge(s["mix_ev"], n - 1)
        for g in (2 * n, 2 * n + 1):
            for ch in range(NCH):
                last = mm(k.bank[n % 2][:, (g % 2) * T + ch * P:(g % 2) * T + (ch + 1) * P],
                          k.vt[:, ch, g * P:(g + 1) * P], k.gws[:, g, :], start=True, stop=True)
        last.then_inc(s["mix_mm"], 1)
    dense(k, pe, "branch_c")

    pe.wait_ge(s["lru_w_in"], 32)
    pe.wait_ge(s["lru_conv"], 2)
    for b in range(KB):
        if b >= 2:
            pe.wait_ge(s["ri_sig"], 2 * (b - 1))
        mm(k.bank[2 + b % 2][:, 0:T], k.wr[:, b, :], k.xb[:, b, :], start=True, stop=True)
        mm(k.bank[2 + b % 2][:, T:512], k.wi[:, b, :], k.xb[:, b, :], start=True, stop=True).then_inc(s["ri_mm"], 1)
    dense(k, pe, "gate_a")
    dense(k, pe, "branch_a")
    dense(k, pe, "gate_b")
    dense(k, pe, "branch_b")
    dense(k, pe, "out")

    rms_sums(k.sq)
    for c1 in range(UP_CHUNKS):
        dense(k, pe, f"mlp_up{c1}")
        if c1:
            dense(k, pe, f"mlp_down{c1 - 1}")
    dense(k, pe, f"mlp_down{UP_CHUNKS - 1}")
    rms_sums(k.sq)

    def ffn(kind):
        rms_sums(k.sq)
        for c1 in range(len(FF2_CHUNKS)):
            dense(k, pe, f"{kind}_up{c1}")
            if c1:
                dense(k, pe, f"{kind}_down{c1 - 1}")
        dense(k, pe, f"{kind}_down{len(FF2_CHUNKS) - 1}")
        rms_sums(k.sq)

    ffn("ffn1")

    rms_sums(k.sq)
    dense(k, pe, "rwkv_in")

    def lora(which, src, banks, half=None):
        rows = slice(0, P) if half is None else slice(64 * half, 64 * half + 64)
        for b in range(AB):
            last = mm(banks[b // 2][:, (b % 2) * T:(b % 2 + 1) * T], k.lora[rows, which, b * P:(b + 1) * P],
                      src[rows, :], start=True, stop=True)
        return last

    pe.wait_ge(s["rwkv_in"], 16)
    pe.wait_ge(s["lora_in"], 1)
    lora(0, k.us[:, 12, :], k.bank[0:2], 0)
    lora(0, k.us[:, 12, :], k.bank[2:4], 1).then_inc(s["w_mm"], 1)
    dense(k, pe, "qkv")
    pe.wait_ge(s["w_sig"], 8)
    lora(1, k.us[:, 13, :], k.bank[0:2], 0)
    lora(1, k.us[:, 13, :], k.bank[2:4], 1).then_inc(s["a_mm"], 1)
    pe.wait_ge(s["rope_in"], 48)
    pe.wait_ge(s["evacuated"], k.segs["qkv"].start + 12)
    for b in range(8):
        last = mm(k.slots[b // 2][:, (b % 2) * T:(b % 2 + 1) * T], k.pre[:, 2, 0:P], k.qkv[:, b, :],
                  start=True, stop=True)
        if b % 2:
            last.then_inc(s["rope_mm"], 1)
    pe.wait_ge(s["a_sig"], 8)
    pe.wait_ge(s["lora_in"], 2)
    lora(2, k.us[:, 14, :], k.bank[0:2]).then_inc(s["g_mm"], 1)
    pe.wait_ge(s["kk_sq"], 1)
    for b in range(AB):
        last = mm(k.bank[2 + b // 2][:, (b % 2) * T:(b % 2 + 1) * T], k.blk[:], k.en[:, b, :], start=True, stop=True)
    last.then_inc(s["kk_mm"], 1)

    pe.wait_ge(s["rope_ev"], 4)
    for ch in range(NCH):
        for b in range(AB):
            last = k.nc.tensor.transpose(k.slots[ch][:, b * P:(b + 1) * P],
                                         k.qkv[:, 8 + b, ch * P:(ch + 1) * P], k.ident[:])
        last.then_inc(s["vt_tr"], 1)

    def scores(h):
        q = 64 * (h % 2)
        if h >= 2:
            pe.wait_ge(s["s_ev"], h - 1)
        for it in range(NCH):
            last = mm(k.slots[2 + h % 2][:, it * T:(it + 1) * T], k.qkv[q:q + 64, h // 2, it * P:(it + 1) * P],
                      k.qkv[q:q + 64, 4 + h // 2, :], start=True, stop=True)
        last.then_inc(s["s_mm"], 1)

    pe.wait_ge(s["vt_ev"], 2)
    pe.wait_ge(s["kk_sqrt"], 1)
    pe.wait_ge(s["g_ev"], 1)
    scores(0)
    for h in range(ATT_HEADS):
        if h + 1 < ATT_HEADS:
            scores(h + 1)
        pe.wait_ge(s["s_exp"], h + 1)
        if h >= 2:
            pe.wait_ge(s["p_ev"], h - 1)
        for jt in range(NCH):
            for it in range(NCH):
                last = k.nc.tensor.transpose(k.bank[2 + h % 2][:, jt * T + it * P:jt * T + (it + 1) * P],
                                             k.att_s[:, h % 2, it * T + jt * P:it * T + (jt + 1) * P], k.ident[:])
        last.then_inc(s["p_tr"], 1)
        pe.wait_ge(s["p_ev"], h + 1)
        for it in range(NCH):
            for jt in range(NCH):
                last = mm(k.bank[it][:, h * 64:h * 64 + 64], k.att_p[:, h % 2, jt * T + it * P:jt * T + (it + 1) * P],
                          k.att_v[:, jt, h * 64:h * 64 + 64], start=jt == 0, stop=jt == NCH - 1)
        last.then_inc(s["o_mm"], 1)
    pe.wait_ge(s["o_fin"], 1)
    for b in range(AB):
        for ch in range(NCH):
            last = k.nc.tensor.transpose(k.slots[b // 2][:, (b % 2) * T + ch * P:(b % 2) * T + (ch + 1) * P],
                                         k.att_o[:, ch, b * P:(b + 1) * P], k.ident[:])
    last.then_inc(s["o_tr"], 1)

    pe.wait_ge(s["bonus_in"], 1)
    for b in range(AB):
        last = mm(k.bank[b // 2][:, (b % 2) * T:(b % 2 + 1) * T], k.blk[:], k.kk[:, b, :], start=True, stop=True)
    last.then_inc(s["bonus_mm"], 1)

    for c in range(NRC):
        pe.wait_ge(s["zv"], c + 1)
        for b in range(AB):
            last = mm(k.bank[2][:, (c % 2) * T + b * RC:(c % 2) * T + (b + 1) * RC], k.zc[:, (c % 2) * 4 + b, :],
                      k.stack[:], start=True, stop=True)
        last.then_inc(s["zv_mm"], 1)
        pe.wait_ge(s["zv_ev"], c + 1)

    def unit_chunk(u, j):
        return u % 4, (j if u < 4 else NRC - 1 - j)

    s4 = k.slots

    def products(name, z, bank, j):
        for h in range(2):
            for u in range(4 * h, 4 * h + 4):
                b, c = unit_chunk(u, j)
                last = mm(k.half_bank[h][bank][:, (u % 4) * P:(u % 4 + 1) * P].rearrange("p (w t) -> p w t", w=2),
                          z[:, u, :], k.cbaq[:, 2:4, h, b, c * RC:(c + 1) * RC], start=True, stop=True)
            last.then_inc(s[name], 1)

    def per_unit(h, bank, lhs, rhs):
        for u in range(4 * h, 4 * h + 4):
            last = mm(k.half_bank[h][bank][:, (u % 4) * RC:(u % 4 + 1) * RC], lhs[:, u, :], rhs(u),
                      start=True, stop=True)
        return last

    pe.wait_ge(s["z_made"], 2)
    products("gb_mm", k.zb, 3, 0)
    for j in range(NRC):
        for h in range(2):
            if j:
                pe.wait_ge(s["sa_ev"], 2 * j)
            pe.wait_ge(s["zn"], 12 * j + h + 1)
            per_unit(h, 0, k.zn, lambda u: k.stack[:]).then_inc(s["u_mm"], 1)
        if j:
            pe.wait_ge(s["ss_ev"], 2 * j)
        products("gc_mm", k.zc, 1, j)
        if j:
            pe.wait_ge(s["y_taken"], 2 * j)
        for n, z in enumerate((k.zc, k.zb)):
            for h in range(2):
                if n == 1:
                    pe.wait_ge(s["tok_ev"], 4 * j + h + 1)
                for u in range(4 * h, 4 * h + 4):
                    last = k.nc.tensor.transpose(k.half_bank[h][2][:, (u % 4) * P:(u % 4 + 1) * P], z[:, u, :],
                                                 k.ident[:])
                last.then_inc(s["tok_tr"], 1)
        for level in range(1, 6):
            for h in range(2):
                pe.wait_ge(s["zn"], 12 * j + 2 * level + h + 1)
                pe.wait_ge(s["t_ev"], 10 * j + 2 * level + h - 1)
                per_unit(h, 0, k.zn, lambda u: k.tc[:, u, :]).then_inc(s["u_mm"], 1)
            for h in range(2):
                pe.wait_ge(s["ztt"], 12 * j + 2 * level + h - 1)
                if level == 1:
                    pe.wait_ge(s["gc_ev"], 2 * j + h + 1)
                    pe.wait_ge(s["tok_ev"], 4 * j + h + 3)
                if level < 5:
                    pe.wait_ge(s["uc_ev"], 8 * j + 2 * level + h - 1)
                    per_unit(h, 1, k.ztt, lambda u: k.uc[:, u, :]).then_inc(s["t_mm"], 1)
                pe.wait_ge(s["zu_ev"], 10 * j + 2 * level + h - 1)
                per_unit(h, 2, k.zu, lambda u: k.ttc[:, u, :]).then_inc(s["tt_mm"], 1)
            if level == 3:
                if j:
                    pe.wait_ge(s["za_made"], j)
                for h in range(2):
                    pe.wait_ge(s["gb_ev"], 2 * j + h + 1)
                    for u in range(4 * h, 4 * h + 4):
                        b, c = unit_chunk(u, j)
                        o = k.half_bank[h][3][:, (u % 4) * RC:(u % 4 + 1) * RC]
                        if j:
                            mm(o, k.za[:, u, :], k.st[:, u, :], start=True, stop=False)
                        last = mm(o, k.zaac[:, u, :], k.vtok[:, b, c, :], start=j == 0, stop=True)
                    last.then_inc(s["x_mm"], 1)

        for h in range(2):
            pe.wait_ge(s["ztt"], 12 * j + h + 11)
            pe.wait_ge(s["x_ev"], 2 * j + h + 1)
            per_unit(h, 0, k.ztt, lambda u: k.xs[:, u, :]).then_inc(s["sa_mm"], 1)
        if j + 1 < NRC:
            pe.wait_ge(s["z_made"], 2 * j + 4)
            products("gb_mm", k.zb, 3, j + 1)
        for h in range(2):
            pe.wait_ge(s["sa_ev"], 2 * j + h + 1)
            for u in range(4 * h, 4 * h + 4):
                b, c = unit_chunk(u, j)
                o = k.half_bank[h][1][:, (u % 4) * RC:(u % 4 + 1) * RC]
                mm(o, k.ctok[:, u, :], k.vtok[:, b, c, :], start=True, stop=False)
                last = mm(o, k.btok[:, u, :], k.sa[:, u, :], start=False, stop=True)
            last.then_inc(s["ss_mm"], 1)
        if j:
            pe.wait_ge(s["zq_made"], j)
        for h in range(2):
            for u in range(4 * h, 4 * h + 4):
                b, c = unit_chunk(u, j)
                o = k.half_bank[h][2][:, (u % 4) * RC:(u % 4 + 1) * RC]
                mm(o, k.zaqc[:, u, :], k.vtok[:, b, c, :], start=True, stop=False)
                if j:
                    mm(o, k.zq[:, u, :], k.st[:, u, :], start=False, stop=False)
                last = mm(o, k.zaqb[:, u, :], k.sa[:, u, :], start=False, stop=True)
            last.then_inc(s["yy_mm"], 1)

    for n in range(4):
        pe.wait_ge(s["zy"], n + 1)
        for c in range(NRC):
            last = mm(s4[n // 2][:, (n % 2) * T + c * RC:(n % 2) * T + (c + 1) * RC], k.zc[:, (n % 2) * 4 + c, :],
                      k.stack[:], start=True, stop=True)
        last.then_inc(s["zy_mm"], 1)
    for event, made, src in (("mu_mm", "y_fm", k.yf), ("var_mm", "y_sq", k.ysq)):
        pe.wait_ge(s[made], 1)
        banks = s4[2:4] if event == "mu_mm" else s4[0:2]
        for half in range(2):
            last = mm(banks[half][:], k.blk[:], src[:, 4 * half:4 * half + 4, :].rearrange("p b t -> p (b t)"),
                      start=True, stop=True)
        last.then_inc(s[event], 1)
    dense(k, pe, "out_2")
    rms_sums(k.sq)
    ffn("ffn2")


def vector_evacuate(k, v, name, write, first=0, last=None):
    seg = k.segs[name]
    last = seg.n if last is None else last
    for i, j, q in tiles(v, last - first):
        slot = (seg.start + first + j) % RING
        v.wait_ge(k.s["tiles_used"], i + (seg.start + first + 1))
        write(i + first, i + (seg.start + first), j, q, k.slots[slot][:, 0:T])


def vector_to_scalar(k, v, name, first=0, last=None):
    base = k.act_before[name]

    def write(i, t, j, q, product):
        if base or not isinstance(i, int) or i >= RING:
            v.wait_ge(k.s["act_out"], i + (base - RING + 1))
        k.nc.vector.tensor_tensor(k.pre[:, (base + first + j) % RING, :], product, k.rs[:],
                                  ALU.mult).then_inc(k.s["evacuated"], 1)

    vector_evacuate(k, v, name, write, first, last)


def make_operand(k, v, steps, name, first, src, scalar=None):
    op = k.made[name]
    if op.free:
        v.wait_ge(k.s["tiles_used"], op.free)
    n = len(src)
    for b in range(n + 1):
        if b < n:
            hi = op.hi[:, first + b, :]
            if scalar is None:
                steps.do(k.nc.vector.tensor_copy(hi, src[b]))
            else:
                steps.do(k.nc.vector.tensor_scalar(hi, src[b], scalar(b), None, ALU.mult))
        if b > 0:
            steps.settle(1 if b < n else 0)
            hi, lo = op.hi[:, first + b - 1, :].bitcast(F32), op.lo[:, first + b - 1, :]
            if scalar is None:
                ins = k.nc.vector.tensor_tensor(lo, src[b - 1], hi, ALU.subtract)
            else:
                ins = k.nc.vector.scalar_tensor_tensor(lo, src[b - 1], scalar(b - 1), hi, ALU.mult, ALU.subtract)
            ins.then_inc(k.s["op_ready"], 1)


def vector_rms(k, v, steps, sem, value, dst=None):
    v.wait_ge(k.s[sem], value)
    steps.do(k.nc.vector.reciprocal((dst or k.rs)[:], k.sd[:]))
    steps.settle()


def conv(k, v, steps, src, dst, blocks, w, bias, n_blocks):
    for tap in range(4):
        for b in blocks:
            x, wt = src[:, b, tap:tap + T], col(k, w, tap * n_blocks + b)
            if tap == 0:
                steps.do(k.nc.vector.tensor_scalar(dst[:, b, :], x, wt, col(k, bias, b), ALU.mult, ALU.add))
            else:
                steps.settle(len(blocks) - 1)
                steps.do(k.nc.vector.scalar_tensor_tensor(dst[:, b, :], x, wt, dst[:, b, :], ALU.mult, ALU.add))


def gated_sum(k, v, gate, first=False):
    def write(i, t, j, q, product):
        v.wait_ge(k.s["act_out"], i + (k.act_before[gate] + 1))
        g = k.g[:, at(v, i), :].rearrange("p o t -> p (o t)")
        m = k.m[:, at(v, i), :].rearrange("p o t -> p (o t)")
        k.nc.vector.tensor_tensor(m if first else g, product, g, ALU.mult).then_inc(k.s["evacuated"], 1)
        if not first:
            v.wait_ge(k.s["evacuated"], t + 1)
            k.nc.vector.tensor_tensor(m, m, g, ALU.add).then_inc(k.s["merged"], 1)
    return write


def vector_program(k, v):
    s, c, nv = k.s, Small(k), k.nc.vector
    st = Steps(v, s["step_v"])

    nv.memset(k.xbc_pad[:, :, 0:3], 0.0)
    nv.memset(k.eps[:, 0:1], EPS)
    st.do(nv.memset(k.eps[:, 1:2], GN_EPS))
    st.settle()
    v.sem_inc(s["zeroed"], 1)
    v.wait_ge(s["x_in"], 16)
    v.wait_ge(s["consts_in"], 16 * CONST_DMAS)
    make_operand(k, v, st, "hn", 0, [k.x[:, b, :] for b in range(KB)], lambda b: col(k, "norm_mix_g", b))
    st.do(nv.tensor_copy(k.wdt_hi[:], k.wdt[:]))
    st.settle()
    st.do(nv.tensor_tensor(k.wdt_lo[:], k.wdt[:], k.wdt_hi[:].bitcast(F32), ALU.subtract))
    st.settle()
    norms = [0]

    def rms():
        norms[0] += 1
        vector_rms(k, v, st, "rms_sqrt", norms[0])

    rms()
    v.sem_inc(s["rs_ready"], 1)

    def padded(dst):
        def write(i, t, j, q, product):
            o = dst[:, at(v, i), 3:3 + T].rearrange("p o t -> p (o t)")
            k.nc.vector.tensor_tensor(o, product, k.rs[:], ALU.mult).then_inc(s["evacuated"], 1)
        return write

    vector_evacuate(k, v, "xbc", padded(k.xbc_pad))
    v.wait_ge(s["evacuated"], 16)

    def ssd_conv(n):
        conv(k, v, st, k.xbc_pad, k.xc, range(4 * n, 4 * n + 4), "ssd_conv_w", "ssd_conv_b", 16)
        st.settle()
        v.sem_inc(s["conv_done"], 1)

    ssd_conv(0)
    vector_to_scalar(k, v, "z", 0, 4)
    ssd_conv(1)
    vector_to_scalar(k, v, "z", 4, 8)
    ssd_conv(2)
    vector_to_scalar(k, v, "v", 0, 4)
    ssd_conv(3)
    vector_to_scalar(k, v, "v", 4, 8)

    v.wait_ge(s["rs_col_mm"], 1)
    st.do(nv.tensor_copy(c.rs_col, k.bank[1][:, 0:2]))
    v.wait_ge(s["dt_mm"], 1)
    st.settle()
    for ch in range(NCH):
        st.do(nv.scalar_tensor_tensor(c.z[:, ch * 16:ch * 16 + 16], k.bank[2][:, ch * 16:ch * 16 + 16],
                                      c.rs_col[:, ch:ch + 1], c.dtb, ALU.mult, ALU.add))
    nv.tensor_scalar(c.z[:, 32:40], k.cols[:, COLS["lru_lambda"]:COLS["lru_lambda"] + 8], -1.0, None,
                     ALU.mult).then_inc(s["sp_z"], 1)
    v.wait_ge(s["sp_z"], 1)
    st.settle()
    v.sem_inc(s["sp_z"], 1)
    vector_to_scalar(k, v, "u", 0, 4)
    v.wait_ge(s["sp_exp"], 1)
    st.do(nv.tensor_scalar(c.u, c.e, 1.0, None, ALU.add))
    st.settle()
    v.sem_inc(s["sp_u"], 1)
    st.do(nv.tensor_scalar(c.um, c.u, 1.0, None, ALU.subtract))
    st.do(nv.reciprocal(c.ru, c.u))
    st.settle(1)
    st.do(nv.tensor_tensor(c.d, c.e, c.um, ALU.subtract))
    st.settle()
    st.do(nv.tensor_tensor(c.d, c.d, c.ru, ALU.mult))
    v.wait_ge(s["sp_ln"], 1)
    st.settle()
    st.do(nv.tensor_tensor(c.ln, c.ln, c.d, ALU.add))
    st.settle()
    st.do(nv.scalar_tensor_tensor(c.sp, c.z, 0.0, c.ln, ALU.max, ALU.add))
    st.settle()
    for ch in range(NCH):
        st.do(nv.scalar_tensor_tensor(c.adt[:, ch * 16:ch * 16 + 16], c.sp[:, ch * 16:ch * 16 + 16], -1.0,
                                      c.ea, ALU.mult, ALU.mult))
    st.do(nv.tensor_scalar(c.nsp8, c.sp[:, 32:40], -8.0, None, ALU.mult))
    st.do(nv.tensor_scalar(c.psp8, c.sp[:, 32:40], 8.0, None, ALU.mult))
    st.settle()
    v.sem_inc(s["adt"], 1)
    vector_to_scalar(k, v, "u", 4, 8)

    v.wait_ge(s["acs_mm"], 1)
    st.do(nv.tensor_copy(c.acs, k.bank[1][:, 0:32]))
    st.settle()
    st.do(nv.tensor_tensor(c.dz, k.bank[1][:, 32:48], c.acs[:, 0:16], ALU.subtract))
    st.settle()
    v.sem_inc(s["acs"], 1)
    for n in range(4):
        ch, half = n // 2, n % 2
        v.wait_ge(s["xs_tr"], n + 1)
        dt = c.sp[:, ch * 16 + half * 8:ch * 16 + half * 8 + 8].unsqueeze(2).to_broadcast([P, 8, 64])
        nv.tensor_tensor(k.xdt[:, ch, half * 512:half * 512 + 512].rearrange("p (h q) -> p h q", h=8),
                         k.bank[2 + n % 2][:].rearrange("p (h q) -> p h q", h=8), dt,
                         ALU.mult).then_inc(s["xs_ev"], 1)
    v.wait_ge(s["xs_ev"], 2)
    v.wait_ge(s["ds_exp"], 1)
    nv.tensor_tensor(k.xdec.rearrange("p (h q) -> p h q", h=16), k.xdt[:, 0, :].rearrange("p (h q) -> p h q", h=16),
                     c.ds.unsqueeze(2).to_broadcast([P, 16, 64]), ALU.mult).then_inc(s["xdec"], 1)
    for ch in range(NCH):
        v.wait_ge(s["cb_mm"], ch + 1)
        nv.tensor_tensor(k.cbm[:, ch * 4:ch * 4 + 4, :], k.bank[3 - ch][:].rearrange("p (g t) -> p g t", g=4),
                         k.tri[:].unsqueeze(1).to_broadcast([P, 4, P]), ALU.mult).then_inc(s["cbm"], 1)
    v.wait_ge(s["cbm"], 2)
    cbm = k.cbm.rearrange("p (c g) t -> p c g t", c=NCH)

    def least(h):
        v.wait_ge(s["rb_mm"], h + 1)
        if h >= 2:
            v.wait_ge(s["e_exp"], h - 1)
        for ch in range(NCH):
            last = nv.tensor_scalar(k.e[:, h % 2, ch * P:(ch + 1) * P], k.bank[h % 2][:, ch * P:(ch + 1) * P],
                                    c.acs[:, ch * 16 + h:ch * 16 + h + 1], 0.0, ALU.subtract, ALU.min)
        last.then_inc(s["e_min"], 1)

    def y_out(b):
        v.wait_ge(s["y_mm"], 2 * b + 2)
        nv.scalar_tensor_tensor(k.xc[:, b, :], k.xc[:, b, :], col(k, "ssd_d", b), k.bank[2 + b % 2][:, 0:T],
                                ALU.mult, ALU.add).then_inc(s["y_ev"], 1)
        v.wait_ge(s["y_ev"], b + 1)
        nv.tensor_tensor(k.z[:, b, :], k.z[:, b, :], k.xc[:, b, :], ALU.mult).then_inc(s["yz"], 1)

    least(0)
    for h in range(SSD_HEADS):
        if h + 1 < SSD_HEADS:
            least(h + 1)
        g = h // 4
        v.wait_ge(s["e_exp"], h + 1)
        if h >= 2:
            v.wait_ge(s["y_mm"], h - 1)
        nv.tensor_tensor(k.mt[:, h % 2, :].rearrange("p (c t) -> p c t", c=NCH),
                         k.e[:, h % 2, :].rearrange("p (c t) -> p c t", c=NCH), cbm[:, :, g, :],
                         ALU.mult).then_inc(s["mt"], 1)
        v.wait_ge(s["ex_exp"], h + 1)
        v.wait_ge(s["mt"], h + 1)
        nv.tensor_tensor(k.ce[:, h % 2, :], k.xc[:, 12 + g, P:T], k.ex[:, h % 2, :], ALU.mult).then_inc(s["ce"], 1)
        if h % 2 == 1 and h >= 3:
            y_out(h // 2 - 1)
    y_out(7)

    nv.memset(k.xb_pad[:, :, 0:3], 0.0)
    vector_evacuate(k, v, "xb", padded(k.xb_pad))

    def group_norm(half):
        v.wait_ge(s["gn_sqrt"], half + 1)
        st.do(nv.reciprocal(k.gn_rs[:], k.gn_sd[:, half, :]))
        st.settle()
        for b in range(4 * half, 4 * half + 4):
            g = (b // 2) % 2
            st.do(nv.scalar_tensor_tensor(k.z[:, b, :], k.z[:, b, :], col(k, "ssd_norm_g", b),
                                          k.gn_rs[:, g * T:(g + 1) * T], ALU.mult, ALU.mult))
        st.settle()
        v.sem_inc(s["gn_done"], 1)
        make_operand(k, v, st, "y_c", 4 * half, [k.z[:, b, :] for b in range(4 * half, 4 * half + 4)])

    v.wait_ge(s["v_sum_mm"], 1)
    st.do(nv.tensor_scalar(k.rv[:], k.bank[2][:, 0:T], 1.0 / D, None, ALU.mult))
    st.settle()
    for half in range(2):
        h4 = slice(4 * half, 4 * half + 4)
        nv.tensor_tensor(k.v[:, h4, :], k.v[:, h4, :], k.rv[:].unsqueeze(1).to_broadcast([P, 4, T]),
                         ALU.subtract).then_inc(s["v_cent"], 1)
    group_norm(0)
    vector_to_scalar(k, v, "gt", 0, 4)
    group_norm(1)
    vector_to_scalar(k, v, "gt", 4, 8)
    vector_rms(k, v, st, "v_sqrt", 1, k.rv)
    for b in range(KB):
        nv.scalar_tensor_tensor(k.v[:, b, :], k.v[:, b, :], col(k, "gmlp_ln_g", b), k.rv[:], ALU.mult,
                                ALU.mult).then_inc(s["v_scaled"], 1)
    vector_to_scalar(k, v, "gate_c")
    nv.tensor_tensor(k.gws, k.gws, k.tri[:].unsqueeze(1).to_broadcast([P, 8, P]), ALU.mult).then_inc(s["gws"], 1)
    for n in range(4):
        v.wait_ge(s["mix_mm"], n + 1)
        two = slice(2 * n, 2 * n + 2)
        nv.tensor_tensor(k.gmix[:].rearrange("p (g c t) -> p g c t", g=2, c=NCH),
                         k.bank[n % 2][:].rearrange("p (g c t) -> p g c t", g=2, c=NCH),
                         k.bs[:, two, :].unsqueeze(2).to_broadcast([P, 2, NCH, P]), ALU.add).then_inc(s["mix_ev"], 1)
        v.wait_ge(s["mix_ev"], n + 1)
        st.do(nv.tensor_tensor(k.u[:, two, :], k.u[:, two, :], k.gmix[:].rearrange("p (g t) -> p g t", g=2), ALU.mult))
        st.settle()
        make_operand(k, v, st, "y_a", 2 * n, [k.u[:, b, :] for b in (2 * n, 2 * n + 1)])

    v.wait_ge(s["v_ev"], 4)
    for half in range(2):
        conv(k, v, st, k.xb_pad, k.xb, range(4 * half, 4 * half + 4), "lru_conv_w", "lru_conv_b", 8)
        st.settle()
        v.sem_inc(s["lru_conv"], 1)

    vector_evacuate(k, v, "branch_c", gated_sum(k, v, "gate_c", first=True))

    def lru(half):
        h4 = slice(4 * half, 4 * half + 4)
        v.wait_ge(s["lru_at"], 2 * half + 2)
        st.do(nv.tensor_tensor(k.i[:, h4, :], k.i[:, h4, :], k.xb[:, h4, :], ALU.mult))
        st.do(nv.tensor_tensor(k.r[:, h4, :], k.a[:, h4, :], k.a[:, h4, :], ALU.mult))
        st.settle()
        nv.scalar_tensor_tensor(k.t[:, h4, :], k.r[:, h4, :], 1.0, k.t[:, h4, :], ALU.add,
                                ALU.mult).then_inc(s["lru_q"], 1)
        v.wait_ge(s["lru_sqrt"], half + 1)
        st.do(nv.tensor_tensor(k.i[:, h4, :], k.i[:, h4, :], k.t[:, h4, :], ALU.mult))
        st.settle()
        for b in range(4 * half, 4 * half + 4):
            st.do(nv.tensor_tensor_scan(k.r[:, b, :], k.a[:, b, :], k.i[:, b, :], 0.0, ALU.mult, ALU.add))
        st.settle()
        st.do(nv.tensor_tensor(k.gt[:, h4, :], k.gt[:, h4, :], k.r[:, h4, :], ALU.mult))
        st.settle()
        make_operand(k, v, st, "y_b", 4 * half, [k.gt[:, b, :] for b in range(4 * half, 4 * half + 4)])

    vector_to_scalar(k, v, "gate_a")
    lru(0)
    vector_evacuate(k, v, "branch_a", gated_sum(k, v, "gate_a"))
    lru(1)
    vector_to_scalar(k, v, "gate_b")
    for half in range(2):
        vector_evacuate(k, v, "branch_b", gated_sum(k, v, "gate_b"), 4 * half, 4 * half + 4)
        v.wait_ge(s["merged"], 4 * half + 4 + 8)
        make_operand(k, v, st, "merged", 4 * half, [k.m[:, b, :] for b in range(4 * half, 4 * half + 4)])

    def add_to(dst, first=False):
        def write(i, t, j, q, product):
            o = dst[:, at(v, i), :].rearrange("p o t -> p (o t)")
            if first:
                ins = nv.tensor_scalar(o, product, 1.0, None, ALU.mult)
            else:
                ins = nv.tensor_tensor(o, product, o, ALU.add)
            ins.then_inc(s["evacuated"], 1)
        return write

    def accumulate(name, dst, first=False):
        if not first:
            v.wait_ge(s["evacuated"], k.segs[name].start)
        vector_evacuate(k, v, name, add_to(dst, first))
        v.wait_ge(s["evacuated"], k.segs[name].start + 8)

    def final(dst):
        v.sem_inc(s["x_final"], 1)

    x_blocks = [k.x[:, b, :] for b in range(KB)]
    accumulate("out", k.x)
    final(k.x)
    make_operand(k, v, st, "hn_mlp", 0, x_blocks, lambda b: col(k, "norm_mlp_g", b))
    rms()

    hid_done = [0]

    def split_hidden(op, block, base, e):
        hid, hi, lo = block, op.hi[:, at(v, e), :], op.lo[:, at(v, e), :]
        hi, lo = (z.rearrange("p o t -> p (o t)") for z in (hi, lo))
        v.wait_ge(s["hid_t"], e + (base + 1))
        nv.tensor_scalar(hi, hid, 1.0, None, ALU.mult).then_inc(s["hid_w"], 1)
        v.wait_ge(s["hid_w"], e + (base + 1))
        nv.tensor_tensor(lo, hid, hi.bitcast(F32), ALU.subtract).then_inc(s["op_ready"], 1)

    def mlp_up(chunk):
        op, base = k.made[f"mlp_hid{chunk}"], hid_done[0]
        v.wait_ge(s["tiles_used"], op.free)

        def write(i, t, j, q, product):
            nv.tensor_tensor(k.pre[:, j, :], product, k.rs[:], ALU.mult).then_inc(s["evacuated"], 1)
            v.wait_ge(s["evacuated"], t + 1)
            nv.scalar_tensor_tensor(k.hid[:, j, :], k.pre[:, j, :], 0.0, k.pre[:, j, :], ALU.max,
                                    ALU.mult).then_inc(s["hid_t"], 1)
            split_hidden(op, k.hid[:, j, :], base, i)

        vector_evacuate(k, v, f"mlp_up{chunk}", write)
        hid_done[0] += 8

    v.wait_ge(s["act_out"], k.act_after["gate_b"])
    for chunk in range(UP_CHUNKS):
        mlp_up(chunk)
        if chunk:
            accumulate(f"mlp_down{chunk - 1}", k.x)
    accumulate(f"mlp_down{UP_CHUNKS - 1}", k.x)
    final(k.x)

    def scaled(dst, src, name, factor=None):
        rms()
        for b in range(KB):
            o = (dst if factor is None else src)[:, b, :]
            st.do(nv.scalar_tensor_tensor(o, src[:, b, :], col(k, name, b), k.rs[:], ALU.mult, ALU.mult))
        st.settle()
        if factor is not None:
            for b in range(KB):
                st.do(nv.scalar_tensor_tensor(dst[:, b, :], src[:, b, :], factor, dst[:, b, :], ALU.mult, ALU.add))
            st.settle()

    scaled(k.x, k.x, "final_norm_g")

    def ffn_up(kind, chunk):
        op, base, act = k.made[f"{kind}_hid{chunk}"], hid_done[0], k.act_before[f"{kind}_up{chunk}"]
        v.wait_ge(s["tiles_used"], op.free)
        v.wait_ge(s["act_out"], act)

        def write(i, t, j, q, product):
            e = q * 2 + j // 2
            if j % 2 == 0:
                if not isinstance(i, int) or i >= RING:
                    v.wait_ge(s["act_out"], e + (act - 1))
                nv.tensor_tensor(k.pre[:, j, :], product, k.rs[:], ALU.mult).then_inc(s["evacuated"], 1)
                return
            nv.tensor_tensor(k.pre[:, j, :], product, k.rs[:], ALU.mult).then_inc(s["evacuated"], 1)
            v.wait_ge(s["evacuated"], t + 1)
            v.wait_ge(s["act_out"], e + (act + 1))
            nv.tensor_tensor(k.hid[:, j, :], k.pre[:, j, :], k.sg[:, j - 1, :], ALU.mult).then_inc(s["hid_t"], 1)
            split_hidden(op, k.hid[:, j, :], base, e)

        vector_evacuate(k, v, f"{kind}_up{chunk}", write)
        hid_done[0] += FF2_CHUNKS[chunk]

    def ffn(kind):
        final(k.x)
        make_operand(k, v, st, f"hn_{kind}", 0, x_blocks, lambda b: col(k, f"{kind}_pre_g_2", b))
        rms()
        for chunk in range(len(FF2_CHUNKS)):
            ffn_up(kind, chunk)
            if chunk:
                accumulate(f"{kind}_down{chunk - 1}", k.f, first=chunk == 1)
        accumulate(f"{kind}_down{len(FF2_CHUNKS) - 1}", k.f)
        final(k.f)
        scaled(k.x, k.f, f"{kind}_post_g_2", 0.5)

    ffn("ffn1")

    final(k.x)
    make_operand(k, v, st, "hn_mix", 0, x_blocks, lambda b: col(k, "mix_pre_g_2", b))
    sm = k.small
    prev_g, next_g = COLS["rwkv_mu_prev_2"], COLS["rwkv_mu_next_2"]
    st.do(nv.tensor_tensor(sm[:, 0:15], k.cols[:, prev_g:prev_g + 15], k.cols[:, next_g:next_g + 15], ALU.add))
    st.settle()
    st.do(nv.tensor_scalar(sm[:, 0:15], sm[:, 0:15], -1.0, 1.0, ALU.mult, ALU.add))
    ka = COLS["rwkv_k_a_2"]
    st.do(nv.tensor_scalar(sm[:, 16:20], k.cols[:, ka:ka + 4], -1.0, 1.0, ALU.mult, ALU.add))
    nv.memset(k.upad[:, :, 0:1], 0.0)
    nv.memset(k.upad[:, :, T + 1:T + 2], 0.0)
    rms()

    def plain(dst, offset=0):
        def write(i, t, j, q, product):
            o = dst[:, at(v, i), offset:offset + T].rearrange("p o t -> p (o t)")
            nv.tensor_tensor(o, product, k.rs[:], ALU.mult).then_inc(s["evacuated"], 1)
        return write

    vector_evacuate(k, v, "rwkv_in", plain(k.upad, 1))
    v.wait_ge(s["evacuated"], k.segs["rwkv_in"].start + 15)

    def shift(blocks):
        for b in blocks:
            st.do(nv.tensor_scalar(k.us[:, b, :], k.upad[:, b, 1:T + 1], sm[:, b:b + 1], None, ALU.mult))
        for tap, name in ((0, "rwkv_mu_prev_2"), (2, "rwkv_mu_next_2")):
            for b in blocks:
                st.settle(len(blocks) - 1)
                st.do(nv.scalar_tensor_tensor(k.us[:, b, :], k.upad[:, b, tap:tap + T], col(k, name, b),
                                              k.us[:, b, :], ALU.mult, ALU.add))
        st.settle()

    shift((12, 13, 14))
    v.sem_inc(s["shifted"], 1)
    vector_evacuate(k, v, "qkv", plain(k.qkv), 0, 4)
    shift((4, 5, 6, 7))
    vector_evacuate(k, v, "qkv", plain(k.qkv), 4, 8)
    shift((0, 1, 2, 3))
    vector_evacuate(k, v, "qkv", plain(k.qkv), 8, 12)
    shift((8, 9, 10, 11))
    v.sem_inc(s["shifted"], 1)

    wide = lambda x: x.rearrange("p b t -> p (b t)")
    v.wait_ge(s["w_sig"], 8)
    st.do(nv.tensor_scalar(wide(k.lw), wide(k.lw), -float(np.exp(-0.5)), None, ALU.mult))
    v.wait_ge(s["masks_in"], 16)
    st.settle()
    fwd, bwd = wide(k.lc[:, 0:4, :]), wide(k.lc[:, 4:8, :])
    st.do(nv.tensor_tensor_scan(fwd, k.reset, wide(k.lw[:, 0:4, :]), 0.0, ALU.mult, ALU.add))
    st.do(nv.tensor_tensor_scan(bwd[:, ::-1], k.reset, wide(k.lw[:, 4:8, :])[:, ::-1], 0.0, ALU.mult, ALU.add))
    st.settle()
    nv.tensor_tensor(wide(k.lx), wide(k.lc), wide(k.lw), ALU.subtract).then_inc(s["lw_scan"], 1)

    v.wait_ge(s["rope_in"], 48)
    bc = lambda x, n: x.unsqueeze(1).to_broadcast([P, n, x.shape[-1]])
    v.wait_ge(s["rope_mm"], 4)
    for n in range(4):
        two = k.qkv[:, 2 * n:2 * n + 2, :]
        st.do(nv.tensor_tensor(two, two, bc(k.pre[:, 0, :], 2), ALU.mult))
        o = k.att_s[:, n % 2, :].rearrange("p (b t) -> p b t", b=2)
        st.do(nv.tensor_tensor(o, k.slots[n][:].rearrange("p (b t) -> p b t", b=2), bc(k.pre[:, 1, :], 2), ALU.mult))
        st.settle()
        nv.tensor_tensor(two, two, o, ALU.add).then_inc(s["rope_ev"], 1)

    for b in range(AB):
        st.do(nv.tensor_scalar(k.kk[:, b, :], k.us[:, 4 + b, :], col(k, "rwkv_k_k_2", b), None, ALU.mult))
    st.settle()
    st.do(nv.tensor_tensor(k.en[:, 0:4, :], k.kk[:], k.kk[:], ALU.mult))
    st.settle()
    v.sem_inc(s["kk_sq"], 1)
    v.wait_ge(s["a_sig"], 8)
    for d in range(2):
        for b in range(AB):
            st.do(nv.tensor_scalar(k.kd[:, 4 * d + b, :], k.ia[:, 4 * d + b, :], col(k, "rwkv_k_a_2", b),
                                   sm[:, 16 + b:17 + b], ALU.mult, ALU.add))
    st.settle()
    for d in range(2):
        st.do(nv.tensor_tensor(k.kd[:, 4 * d:4 * d + 4, :], k.kd[:, 4 * d:4 * d + 4, :], k.us[:, 4:8, :], ALU.mult))
    v.wait_ge(s["kk_sqrt"], 1)
    st.do(nv.tensor_scalar(wide(k.en[:, 4:8, :]), wide(k.en[:, 4:8, :]), 1e-12, None, ALU.max))
    st.settle()
    st.do(nv.reciprocal(wide(k.en[:, 0:4, :]), wide(k.en[:, 4:8, :])))
    st.settle()
    st.do(nv.tensor_tensor(k.kk[:], k.kk[:], k.en[:, 0:4, :], ALU.mult))
    st.settle()
    v.sem_inc(s["l_ex"], 1)
    for d in range(2):
        st.do(nv.scalar_tensor_tensor(k.ia[:, 4 * d:4 * d + 4, :], k.ia[:, 4 * d:4 * d + 4, :], -1.0, k.kk[:],
                                      ALU.mult, ALU.mult))

    v.wait_ge(s["att_in"], 16)

    def attention_probabilities(h):
        v.wait_ge(s["s_mm"], h + 1)
        if h >= 2:
            v.wait_ge(s["p_tr"], h - 1)
        sc = k.att_s[:, h % 2, :]
        nv.scalar_tensor_tensor(sc, k.slots[2 + h % 2][:], HD ** -0.5, wide(k.att_mask), ALU.mult,
                                ALU.add).then_inc(s["s_ev"], 1)
        v.wait_ge(s["s_ev"], h + 1)
        st.do(nv.tensor_reduce(sm[:, 64 + 2 * h:66 + 2 * h], sc.rearrange("p (i t) -> p i t", i=2), AX_X, ALU.max))
        st.settle()
        nv.tensor_scalar(sm[:, 80 + 2 * h:82 + 2 * h], sm[:, 64 + 2 * h:66 + 2 * h], -1.0, None,
                         ALU.mult).then_inc(s["s_red"], 1)

    for h in range(ATT_HEADS + 1):
        if h < ATT_HEADS:
            attention_probabilities(h)
        if h:
            g = h - 1
            v.wait_ge(s["p_tr"], g + 1)
            if g >= 2:
                v.wait_ge(s["o_mm"], g - 1)
            nv.tensor_copy(k.att_p[:, g % 2, :], k.bank[2 + g % 2][:]).then_inc(s["p_ev"], 1)
    v.wait_ge(s["o_mm"], 8)
    v.wait_ge(s["s_exp"], 8)
    st.do(nv.reciprocal(sm[:, 112:128], sm[:, 96:112]))
    st.settle()
    den = sm[:, 112:128].rearrange("p (h i) -> p i h", i=2)
    for it in range(NCH):
        o = k.att_o[:, it, :].rearrange("p (h q) -> p h q", h=8)
        st.do(nv.tensor_tensor(o, k.bank[it][:].rearrange("p (h q) -> p h q", h=8),
                               den[:, it, :].unsqueeze(2).to_broadcast([P, 8, 64]), ALU.mult))
    st.settle()
    sq = k.att_p.rearrange("p a b -> p (a b)")
    st.do(nv.tensor_tensor(sq, k.att_o.rearrange("p a b -> p (a b)"), k.att_o.rearrange("p a b -> p (a b)"), ALU.mult))
    st.settle()
    nv.tensor_reduce(sm[:, 128:144], sq.rearrange("p (g q) -> p g q", q=64), AX_X, ALU.add).then_inc(s["o_sq"], 1)
    v.wait_ge(s["o_sqrt"], 1)
    st.do(nv.reciprocal(sm[:, 160:176], sm[:, 144:160]))
    st.settle()
    o = k.att_o.rearrange("p a (h q) -> p (a h) q", h=8)
    nv.tensor_tensor(o, o, sm[:, 160:176].unsqueeze(2).to_broadcast([P, 16, 64]), ALU.mult).then_inc(s["o_fin"], 1)
    v.wait_ge(s["o_tr"], 1)
    for b in range(AB):
        st.do(nv.tensor_scalar(k.y_att[:, b, :], k.slots[b // 2][:, (b % 2) * T:(b % 2 + 1) * T],
                               col(k, "attn_out_g_2", b), None, ALU.mult))

    v.wait_ge(s["n_exp"], 1)
    st.settle()
    c_, b_, a_, q_ = (k.cbaq[:, n].rearrange("p d b t -> p (d b) t") for n in range(4))
    st.do(nv.tensor_tensor(c_, k.kd[:], k.en[:], ALU.mult))
    st.do(nv.tensor_tensor(b_, k.ia[:], k.en[:], ALU.mult))
    v.wait_ge(s["ex_exp2"], 1)
    v.wait_ge(s["p_exp"], 1)
    v.wait_ge(s["g_mm"], 1)
    for d in range(2):
        d4 = slice(4 * d, 4 * d + 4)
        st.do(nv.tensor_tensor(a_[:, d4, :], k.kk[:], k.lx[:, d4, :], ALU.mult))
        st.do(nv.tensor_tensor(q_[:, d4, :], k.us[:, 0:4, :], k.lc[:, d4, :], ALU.mult))
    wt = sm[:, 176:208].rearrange("p (u c) -> p u c", u=8)
    for d, at_end in ((0, RC - 1), (1, 0)):
        st.do(nv.tensor_copy(wt[:, 4 * d:4 * d + 4, :],
                             k.lc[:, 4 * d:4 * d + 4, :].rearrange("p b (c t) -> p b c t", c=NRC)[:, :, :, at_end]))
    st.settle()
    st.do(nv.tensor_tensor(k.kd[:, 0:4, :], k.kd[:, 0:4, :], k.kd[:, 4:8, :], ALU.add))
    st.settle()
    for b in range(AB):
        st.do(nv.tensor_scalar(k.kd[:, b, :], k.kd[:, b, :], col(k, "rwkv_r_k_2", b), 0.5, ALU.mult, ALU.mult))
    st.settle()
    nv.tensor_tensor(k.kk[:], k.kd[:, 0:4, :], k.us[:, 0:4, :], ALU.mult).then_inc(s["bonus_in"], 1)
    v.wait_ge(s["bonus_mm"], 1)
    for n in range(2):
        st.do(nv.tensor_tensor(k.bv[:, 2 * n:2 * n + 2, :], k.bank[n][:].rearrange("p (b t) -> p b t", b=2),
                               k.us[:, 8 + 2 * n:10 + 2 * n, :], ALU.mult))
    st.settle()

    blk2 = k.blk[:].rearrange("p (h t) -> p h t", h=2)

    def spread(dst, src, mask):
        n = dst.shape[1]
        return nv.tensor_tensor(dst.rearrange("p n (h t) -> p n h t", h=2), src.unsqueeze(2).to_broadcast([P, n, 2, RC]),
                                mask.unsqueeze(1).to_broadcast([P, n, 2, RC]), ALU.mult)

    for c1 in range(NRC):
        if c1 >= 2:
            v.wait_ge(s["zv_mm"], c1 - 1)
        half = slice((c1 % 2) * 4, (c1 % 2) * 4 + 4)
        spread(k.zc[:, half, :], k.us[:, 8:12, c1 * RC:(c1 + 1) * RC], blk2).then_inc(s["zv"], 1)
        v.wait_ge(s["zv_mm"], c1 + 1)
        nv.tensor_copy(k.vtok[:, :, c1, :], k.bank[2][:, (c1 % 2) * T:(c1 % 2 + 1) * T].rearrange(
            "p (b t) -> p b t", b=4)).then_inc(s["zv_ev"], 1)
    v.wait_ge(s["zv_ev"], 4)
    st.do(nv.memset(k.zu, 0.0))
    v.wait_ge(s["masks_in"], 32)
    v.wait_ge(s["zv_mm"], 4)

    h4 = lambda h: slice(4 * h, 4 * h + 4)
    stack4 = k.stack[:].unsqueeze(1).to_broadcast([P, 4, RC])
    ident4 = k.ident[:].unsqueeze(1).to_broadcast([P, 4, P])
    bank64 = lambda h, n: k.half_bank[h][n][:, 0:4 * RC].rearrange("p (u t) -> p u t", u=4)
    bank128 = lambda h, n: k.half_bank[h][n][:].rearrange("p (u w t) -> p u w t", u=4, w=2)
    chunk_of = lambda h, j: j if h == 0 else NRC - 1 - j

    def spread_inputs(z, n, j):
        for h in range(2):
            c1 = chunk_of(h, j)
            last = spread(z[:, h4(h), :], k.cbaq[:, n, h, :, c1 * RC:(c1 + 1) * RC], blk2)
            if h == 0:
                st.do(last)
        return last

    def level_part(j, level, h):
        spread(k.zn[:, h4(h), :], k.nt[:, h4(h), :], k.levels[:, h, level]).then_inc(s["zn"], 1)

    def begin_inverse(j):
        for h in range(2):
            v.wait_ge(s["gb_mm"], 2 * j + h + 1)
            st.do(nv.tensor_tensor(k.nt[:, h4(h), :], bank128(h, 3)[:, :, 0, :],
                                   k.strict[:, h, :].unsqueeze(1).to_broadcast([P, 4, RC]), ALU.mult))
        for h in range(2):
            st.settle(1 - h)
            level_part(j, 0, h)
        for h in range(2):
            st.do(nv.tensor_tensor(k.ttc[:, h4(h), :], k.nt[:, h4(h), :],
                                   k.lvl0[:, h, :].unsqueeze(1).to_broadcast([P, 4, RC]), ALU.mult))
        for h in range(2):
            v.wait_ge(s["zn"], 12 * j + h + 1)
            nv.tensor_tensor(k.ztt[:, h4(h), :], k.zn[:, h4(h), :], ident4, ALU.add).then_inc(s["ztt"], 1)
        st.settle()
        for h in range(2):
            st.do(nv.tensor_tensor(k.ttc[:, h4(h), :], k.ttc[:, h4(h), :], stack4, ALU.add))

    spread_inputs(k.zc, 0, 0).then_inc(s["z_made"], 1)
    spread_inputs(k.zb, 1, 0).then_inc(s["z_made"], 1)
    begin_inverse(0)
    for j in range(NRC):
        for h in range(2):
            v.wait_ge(s["u_mm"], 12 * j + h + 1)
            nv.tensor_tensor(k.tc[:, h4(h), :], bank64(h, 0), stack4, ALU.add).then_inc(s["t_ev"], 1)
        for h in range(2):
            v.wait_ge(s["ztt"], 12 * j + h + 1)
            level_part(j, 1, h)
        for h in range(2):
            v.wait_ge(s["gc_mm"], 2 * j + h + 1)
            st.do(spread(k.zaac[:, h4(h), :], bank128(h, 1)[:, :, 0, :], k.causal[:, h, 0]))
            spread(k.zaqc[:, h4(h), :], bank128(h, 1)[:, :, 1, :], k.causal[:, h, 1]).then_inc(s["gc_ev"], 1)
        for level in range(1, 6):
            if level < 5:
                for h in range(2):
                    v.wait_ge(s["u_mm"], 12 * j + 2 * level + h + 1)
                    level_part(j, level + 1, h)
            if level == 1:
                for h in range(2):
                    spread(k.zaqb[:, h4(h), :], bank128(h, 3)[:, :, 1, :], k.causal[:, h, 1]).then_inc(s["gb_ev"], 1)
            elif level == 2 and j:
                spread_inputs(k.za, 2, j).then_inc(s["za_made"], 1)
            elif level in (3, 4) and j + 1 < NRC:
                v.wait_ge(s["tok_tr"], 4 * j + 4)
                n = level - 3
                spread_inputs((k.zc, k.zb)[n], n, j + 1).then_inc(s["z_made"], 1)
            elif level == 5 and j:
                spread_inputs(k.zq, 3, j).then_inc(s["zq_made"], 1)
            for h in range(2):
                if level < 5:
                    v.wait_ge(s["t_mm"], 8 * j + 2 * level + h - 1)
                    v.wait_ge(s["t_ev"], 10 * j + 2 * level + h - 1)
                    nv.tensor_tensor(k.tc[:, h4(h), :], bank64(h, 1), k.tc[:, h4(h), :],
                                     ALU.add).then_inc(s["t_ev"], 1)
                v.wait_ge(s["tt_mm"], 10 * j + 2 * level + h - 1)
                st.settle()
                st.do(nv.tensor_tensor(k.ttc[:, h4(h), :], bank64(h, 2), k.ttc[:, h4(h), :], ALU.add))
                st.settle()
                spread(k.ztt[:, h4(h), :], k.ttc[:, h4(h), :], blk2).then_inc(s["ztt"], 1)

        for h in range(2):
            v.wait_ge(s["sa_mm"], 2 * j + h + 1)
            nv.tensor_copy(k.sa[:, h4(h), :], bank64(h, 0)).then_inc(s["sa_ev"], 1)
        if j + 1 < NRC:
            begin_inverse(j + 1)
        for h in range(2):
            v.wait_ge(s["ss_mm"], 2 * j + h + 1)
            w = wt[:, h4(h), chunk_of(h, j)].unsqueeze(2).to_broadcast([P, 4, RC])
            state, new = k.st[:, h4(h), :], bank64(h, 1)
            if j:
                v.wait_ge(s["yy_mm"], 2 * j + h + 1)
                st.do(nv.tensor_tensor(state, new, state, ALU.add))
                st.settle()
                nv.tensor_tensor(state, state, w, ALU.mult).then_inc(s["ss_ev"], 1)
            else:
                nv.tensor_tensor(state, new, w, ALU.mult).then_inc(s["ss_ev"], 1)
        for h in range(2):
            v.wait_ge(s["yy_mm"], 2 * j + h + 1)
            o = k.ytok[:, :, chunk_of(h, j), :]
            y = bank64(h, 2)
            ins = nv.tensor_copy(o, y) if j < NRC // 2 else nv.tensor_tensor(o, y, o, ALU.add)
            ins.then_inc(s["y_taken"], 1)
    v.wait_ge(s["y_taken"], 2 * NRC)

    for n in range(4):
        if n >= 2:
            v.wait_ge(s["zy_mm"], n - 1)
        spread(k.zc[:, (n % 2) * 4:(n % 2) * 4 + 4, :], k.ytok[:, n], blk2).then_inc(s["zy"], 1)
    v.wait_ge(s["zy_mm"], 4)
    yf, ysq, ymu = (x.rearrange("p u t -> p (u t)") for x in (k.yf, k.ysq, k.ymu))
    h512 = lambda n: slice(512 * n, 512 * n + 512)
    for n in range(2):
        st.do(nv.tensor_copy(yf[:, h512(n)], k.slots[n][:]))
    st.settle()
    v.sem_inc(s["y_fm"], 1)
    v.wait_ge(s["mu_mm"], 1)
    for n in range(2):
        st.do(nv.scalar_tensor_tensor(yf[:, h512(n)], k.slots[2 + n][:], -1.0 / HD, yf[:, h512(n)], ALU.mult, ALU.add))
    st.settle()
    nv.tensor_tensor(ysq, yf, yf, ALU.mult).then_inc(s["y_sq"], 1)
    v.wait_ge(s["y_sqrt"], 1)
    st.do(nv.reciprocal(ysq, ymu))
    st.settle()
    st.do(nv.tensor_tensor(yf, yf, ysq, ALU.mult))
    st.settle()
    y4 = yf.rearrange("p (b t) -> p b t", b=4)
    for b in range(AB):
        st.do(nv.tensor_scalar(y4[:, b, :], y4[:, b, :], col(k, "rwkv_lnx_w_2", b), col(k, "rwkv_lnx_b_2", b),
                               ALU.mult, ALU.add))
    st.settle()
    st.do(nv.tensor_tensor(y4, y4, k.bv[:], ALU.add))
    st.settle()
    st.do(nv.tensor_tensor(y4, y4, k.gout[:], ALU.mult))
    st.settle()
    make_operand(k, v, st, "y_mix", 0, [k.y_att[:, b, :] for b in range(AB)] + [y4[:, b, :] for b in range(AB)])
    accumulate("out_2", k.f, first=True)
    final(k.f)
    scaled(k.x, k.f, "mix_post_g_2", 1.0)
    ffn("ffn2")
    v.sem_inc(s["out_done"], 1)


def scalar_segment(k, act, name, work=None, first=0, last=None, every=1):
    seg = k.segs[name]
    last = seg.n if last is None else last
    ahead = RING - 1
    n = last - first
    if seg.start + last + ahead > k.total:
        counted = [(i, i % RING, i // RING) for i in range(n)]
    else:
        counted = tiles(act, n, peel=seg.start + first == 0)
    for i, j, q in counted:
        t0 = seg.start + first + ahead
        if not isinstance(i, int) or t0 + i < k.total:
            slot = (t0 + j) % RING
            act.wait_ge(k.landed[slot], q * 16 + 16 * ((t0 + j) // RING + 1))
            if seg.start + first or not isinstance(i, int) or i >= 1:
                act.wait_ge(k.s["tiles_used"], i + (t0 - RING + 1))
            k.nc.scalar.activation(k.whi[:, slot, :], k.raw[:, slot, :], ACT.Copy).then_inc(k.s["hi_ready"], 1)
        if work is not None and j % every == 0:
            act.wait_ge(k.s["evacuated"], i + (seg.start + first + 1))
            work(i + first, j, q)


def scalar_function(k, act, name, func, dst, bias=None, first=0):
    base = k.act_before[name]

    def work(i, j, q):
        o = dst[:, at(act, i), :].rearrange("p o t -> p (o t)")
        src = k.pre[:, (base + first + j) % RING, :]
        if bias is None:
            ins = k.nc.scalar.activation(o, src, func)
        else:
            c = COLS[bias[0]] + bias[1]
            ins = k.nc.scalar.activation(o, src, func, bias=k.cols[:, bass.ds(i + c, 1)])
        ins.then_inc(k.s["act_out"], 1)
    return work


def scalar_program(k, act, a):
    s, c, na = k.s, Small(k), k.nc.scalar
    st = Steps(act, s["step_a"])
    f = na.activation

    act.dma_start(k.x[:], a["x"]).then_inc(s["x_in"], 16)
    for dst, name in ((k.cols[:], "cols"), (k.ones[:], "ones"), (k.ident[:], "ident"), (k.tri[:], "tri"),
                      (k.wdt[:], "w_dt"), (Small(k).dtb_alog, "dt_rows"), (k.gws, "gmlp_w"), (k.bs, "gmlp_b"),
                      (k.blk[:], "blk"), (k.stack[:], "stack")):
        act.dma_start(dst, a[name]).then_inc(s["consts_in"], 16)
    for t in range(RING - 1):
        act.wait_ge(k.landed[t], 16)
        f(k.whi[:, t, :], k.raw[:, t, :], ACT.Copy).then_inc(s["hi_ready"], 1)
    act.wait_ge(s["x_in"], 16)
    norms = [0]

    def root_mean_square(src, sq):
        for half in range(2):
            h4 = slice(4 * half, 4 * half + 4)
            f(sq[:, h4, :], src[:, h4, :], ACT.Square).then_inc(s["sq"], 1)
        norms[0] += 1
        act.wait_ge(s["rms_mm"], norms[0])
        f(k.sd[:], k.bank[0][:, 0:T], ACT.Sqrt, bias=k.eps[:, 0:1], scale=1.0 / D).then_inc(s["rms_sqrt"], 1)

    act.wait_ge(s["consts_in"], 16 * CONST_DMAS)
    f(c.ea, c.alog, ACT.Exp)
    act.wait_ge(s["zeroed"], 1)
    root_mean_square(k.x, k.sq0)
    scalar_segment(k, act, "xbc")

    def silu(n):
        act.wait_ge(s["conv_done"], n + 1)
        h4 = slice(4 * n, 4 * n + 4)
        f(k.xc[:, h4, :], k.xc[:, h4, :], ACT.Silu).then_inc(s["ssd_silu"], 1)

    for half in range(2):
        silu(half)
        scalar_segment(k, act, "z", scalar_function(k, act, "z", ACT.Silu, k.z), 4 * half, 4 * half + 4)
    for half in range(2):
        silu(2 + half)
        scalar_segment(k, act, "v", scalar_function(k, act, "v", ACT.Gelu_apprx_tanh, k.v), 4 * half, 4 * half + 4)
    act.wait_ge(s["sp_z"], 2)
    st.do(f(c.ab, c.z, ACT.Abs))
    st.settle()
    f(c.e, c.ab, ACT.Exp, scale=-1.0).then_inc(s["sp_exp"], 1)
    scalar_segment(k, act, "u", scalar_function(k, act, "u", ACT.Gelu_apprx_tanh, k.u), 0, 4)
    act.wait_ge(s["sp_u"], 1)
    f(c.ln, c.u, ACT.Ln).then_inc(s["sp_ln"], 1)
    scalar_segment(k, act, "u", scalar_function(k, act, "u", ACT.Gelu_apprx_tanh, k.u), 4, 8)

    act.wait_ge(s["acs"], 1)
    f(c.ds, c.dz, ACT.Exp).then_inc(s["ds_exp"], 1)
    act.wait_ge(s["b_tr"], 1)
    f(k.bt, k.bank[2][:], ACT.Copy).then_inc(s["b_ev"], 1)
    for half in range(2):
        act.wait_ge(s["st_mm"], half + 1)
        f(k.state[:, half * 512:half * 512 + 512], k.bank[(1, 2)[half]][:], ACT.Copy).then_inc(s["st_ev"], 1)
    for h in range(SSD_HEADS):
        act.wait_ge(s["e_min"], h + 1)
        if h >= 2:
            act.wait_ge(s["ce"], h - 1)
        f(k.ex[:, h % 2, :], k.bank[h % 2][:, P:T], ACT.Exp).then_inc(s["ex_exp"], 1)
        f(k.e[:, h % 2, :], k.e[:, h % 2, :], ACT.Exp).then_inc(s["e_exp"], 1)
    for g in range(GROUPS):
        act.wait_ge(s["yz"], 2 * g + 2)
        f(k.gn_sq[:, 2 * g:2 * g + 2, :], k.z[:, 2 * g:2 * g + 2, :], ACT.Square).then_inc(s["gn_sq"], 1)
    scalar_segment(k, act, "xb")
    for half in range(2):
        act.wait_ge(s["gn_mm"], 2 * half + 2)
        f(k.gn_sd[:, half, :], k.bank[half][:], ACT.Sqrt, bias=k.eps[:, 0:1], scale=1.0 / 256).then_inc(s["gn_sqrt"], 1)
    for half in range(2):
        h4 = slice(4 * half, 4 * half + 4)
        act.wait_ge(s["v_cent"], half + 1)
        f(k.gm_sq[:, h4, :], k.v[:, h4, :], ACT.Square).then_inc(s["v_sq"], 1)
    scalar_segment(k, act, "gt", scalar_function(k, act, "gt", ACT.Gelu_apprx_tanh, k.gt))
    act.wait_ge(s["v_var_mm"], 1)
    f(k.sd[:], k.bank[3][:, 0:T], ACT.Sqrt, bias=k.eps[:, 0:1], scale=1.0 / D).then_inc(s["v_sqrt"], 1)
    for b in range(KB):
        act.wait_ge(s["v_scaled"], b + 1)
        f(k.v[:, b, :], k.v[:, b, :], ACT.Identity, bias=col(k, "gmlp_ln_b", b)).then_inc(s["v_norm"], 1)
    scalar_segment(k, act, "gate_c", scalar_function(k, act, "gate_c", ACT.Sigmoid, k.g, ("b_gate", 16)))
    for n in range(4):
        act.wait_ge(s["v_tr"], n + 1)
        ch, half = n // 2, n % 2
        f(k.vt[:, ch, half * 512:half * 512 + 512], k.bank[n % 2][:], ACT.Copy).then_inc(s["v_ev"], 1)
    act.wait_ge(s["mix_mm"], 4)
    act.wait_ge(s["mix_ev"], 4)
    act.dma_start(k.wr, a["lru_w_r"]).then_inc(s["lru_w_in"], 16)
    act.dma_start(k.wi, a["lru_w_i"]).then_inc(s["lru_w_in"], 16)
    scalar_segment(k, act, "branch_c")

    for b in range(KB):
        act.wait_ge(s["ri_mm"], b + 1)
        f(k.r[:, b, :], k.bank[2 + b % 2][:, 0:T], ACT.Sigmoid, bias=col(k, "lru_b_r", b)).then_inc(s["ri_sig"], 1)
        f(k.i[:, b, :], k.bank[2 + b % 2][:, T:512], ACT.Sigmoid, bias=col(k, "lru_b_i", b)).then_inc(s["ri_sig"], 1)
    act.wait_ge(s["ri_sig"], 16)
    for b in range(KB):
        na_a = f(k.a[:, b, :], k.r[:, b, :], ACT.Exp, scale=c.nsp8[:, b:b + 1])
        na_t = f(k.t[:, b, :], k.r[:, b, :], ACT.Tanh, scale=c.psp8[:, b:b + 1])
        if b % 4 == 3:
            na_a.then_inc(s["lru_at"], 1)
            na_t.then_inc(s["lru_at"], 1)
    scalar_segment(k, act, "gate_a", scalar_function(k, act, "gate_a", ACT.Sigmoid, k.g, ("b_gate", 0)))

    def root(half):
        h4 = slice(4 * half, 4 * half + 4)
        act.wait_ge(s["lru_q"], half + 1)
        f(k.t[:, h4, :], k.t[:, h4, :], ACT.Sqrt).then_inc(s["lru_sqrt"], 1)

    root(0)
    scalar_segment(k, act, "branch_a")
    root(1)
    scalar_segment(k, act, "gate_b", scalar_function(k, act, "gate_b", ACT.Sigmoid, k.g, ("b_gate", 8)))
    scalar_segment(k, act, "branch_b")
    scalar_segment(k, act, "out")

    finals = [0]

    def next_norm(src):
        finals[0] += 1
        act.wait_ge(s["x_final"], finals[0])
        root_mean_square(src, k.sq)

    next_norm(k.x)
    for chunk in range(UP_CHUNKS):
        scalar_segment(k, act, f"mlp_up{chunk}")
        if chunk:
            scalar_segment(k, act, f"mlp_down{chunk - 1}")
    scalar_segment(k, act, f"mlp_down{UP_CHUNKS - 1}")
    next_norm(k.x)

    def ffn(kind):
        next_norm(k.x)
        for chunk in range(len(FF2_CHUNKS)):
            def work(i, j, q):
                f(k.sg[:, j, :], k.pre[:, j, :], ACT.Silu).then_inc(s["act_out"], 1)
            scalar_segment(k, act, f"{kind}_up{chunk}", work, every=2)
            if chunk:
                scalar_segment(k, act, f"{kind}_down{chunk - 1}")
        scalar_segment(k, act, f"{kind}_down{len(FF2_CHUNKS) - 1}")
        next_norm(k.f)

    ffn("ffn1")

    act.wait_ge(s["tiles_used"], k.segs["ffn1_down2"].start + 8)
    act.dma_start(k.lora, a["lora"]).then_inc(s["rwkv_in"], 16)
    act.dma_start(k.pre[:, 0, :], a["rope_cos"]).then_inc(s["rope_in"], 16)
    act.dma_start(k.pre[:, 1, :], a["rope_sin"]).then_inc(s["rope_in"], 16)
    act.dma_start(k.pre[:, 2, 0:P], a["rope_turn"]).then_inc(s["rope_in"], 16)
    act.dma_start(k.reset, a["reset"]).then_inc(s["masks_in"], 16)
    next_norm(k.x)
    act.dma_start(k.att_mask, a["att_mask"]).then_inc(s["att_in"], 16)
    scalar_segment(k, act, "rwkv_in")
    act.wait_ge(s["shifted"], 1)
    f(k.us[:, 12, :], k.us[:, 12, :], ACT.Tanh).then_inc(s["lora_in"], 1)
    f(k.us[:, 14, :], k.us[:, 14, :], ACT.Sigmoid).then_inc(s["lora_in"], 1)

    def sigmoids(dst, mm_event, bias, event):
        act.wait_ge(s[mm_event], 1)
        for n in range(8):
            f(dst[:, n, :], k.bank[n // 2][:, (n % 2) * T:(n % 2 + 1) * T], ACT.Sigmoid,
              bias=col(k, bias, n)).then_inc(s[event], 1)

    scalar_segment(k, act, "qkv")
    act.wait_ge(s["shifted"], 2)
    sigmoids(k.lw, "w_mm", "rwkv_w0_2", "w_sig")
    sigmoids(k.ia, "a_mm", "rwkv_a0_2", "a_sig")
    act.wait_ge(s["g_mm"], 1)
    for n in range(2):
        last = f(k.gout[:, 2 * n:2 * n + 2, :], k.bank[n][:].rearrange("p (b t) -> p b t", b=2), ACT.Copy)
    last.then_inc(s["g_ev"], 1)
    act.wait_ge(s["kk_mm"], 1)
    for n in range(2):
        last = f(k.en[:, 4 + 2 * n:6 + 2 * n, :], k.bank[2 + n][:].rearrange("p (b t) -> p b t", b=2), ACT.Sqrt)
    last.then_inc(s["kk_sqrt"], 1)
    for ch in range(NCH):
        act.wait_ge(s["vt_tr"], ch + 1)
        f(k.att_v[:, ch, :], k.slots[ch][:], ACT.Copy).then_inc(s["vt_ev"], 1)
    sm = k.small
    for h in range(ATT_HEADS):
        act.wait_ge(s["s_red"], h + 1)
        for it in range(NCH):
            x = k.att_s[:, h % 2, it * T:(it + 1) * T]
            last = f(x, x, ACT.Exp, bias=sm[:, 80 + 2 * h + it:81 + 2 * h + it],
                     accum_out=sm[:, 96 + 2 * h + it:97 + 2 * h + it])
        last.then_inc(s["s_exp"], 1)
    act.wait_ge(s["lw_scan"], 1)
    act.wait_ge(s["l_ex"], 1)
    f(k.en, k.lc, ACT.Exp, scale=-1.0).then_inc(s["n_exp"], 1)
    act.wait_ge(s["n_exp"], 1)
    f(k.lx, k.lx, ACT.Exp).then_inc(s["ex_exp2"], 1)
    f(k.lc, k.lc, ACT.Exp).then_inc(s["p_exp"], 1)
    act.wait_ge(s["o_sq"], 1)
    f(sm[:, 144:160], sm[:, 128:144], ACT.Sqrt, bias=k.eps[:, 0:1], scale=1.0 / HD).then_inc(s["o_sqrt"], 1)
    act.wait_ge(s["o_tr"], 1)
    act.dma_start(k.masks, a["rwkv_masks"]).then_inc(s["masks_in"], 16)

    bank64 = lambda h, n, rows=slice(0, P): k.half_bank[h][n][rows, 0:4 * RC].rearrange("p (u t) -> p u t", u=4)
    upper, lower = slice(0, 64), slice(64, P)
    for j in range(NRC):
        for n, tok in enumerate((k.ctok, k.btok)):
            for h in range(2):
                act.wait_ge(s["tok_tr"], 4 * j + 2 * n + h + 1)
                f(tok[:, 4 * h:4 * h + 4, :], k.half_bank[h][2][:].rearrange("p (u t) -> p u t", u=4),
                  ACT.Copy).then_inc(s["tok_ev"], 1)
        for level in range(1, 6):
            for h in range(2):
                h4 = slice(4 * h, 4 * h + 4)
                act.wait_ge(s["u_mm"], 12 * j + 2 * level + h + 1)
                if level < 5:
                    f(k.uc[:, h4, :], bank64(h, 0), ACT.Copy).then_inc(s["uc_ev"], 1)
                f(k.zu[upper, h4, 0:64], bank64(h, 0, upper), ACT.Copy)
                f(k.zu[lower, h4, 64:P], bank64(h, 0, lower), ACT.Copy).then_inc(s["zu_ev"], 1)
            if level == 3:
                for h in range(2):
                    act.wait_ge(s["x_mm"], 2 * j + h + 1)
                    f(k.xs[:, 4 * h:4 * h + 4, :], bank64(h, 3), ACT.Copy).then_inc(s["x_ev"], 1)
    act.wait_ge(s["var_mm"], 1)
    for n in range(2):
        last = f(k.ymu[:, 4 * n:4 * n + 4, :], k.slots[n][:].rearrange("p (u t) -> p u t", u=4), ACT.Sqrt,
                 bias=k.eps[:, 1:2], scale=1.0 / HD)
    last.then_inc(s["y_sqrt"], 1)
    scalar_segment(k, act, "out_2")
    next_norm(k.f)
    ffn("ffn2")


def second_constants():
    p, t = np.arange(P), np.arange(T)
    half = HD // 2
    inv = (np.float32(10000.0) ** (-np.arange(0, HD, 2, dtype=np.float32) / np.float32(HD))).astype(np.float32)
    ang = (t.astype(np.float32)[None, :] * inv[p % half][:, None]).astype(np.float32)
    turn = np.zeros((P, P), np.float32)
    for m in range(P):
        turn[m + half if m % HD < half else m - half, m] = -1.0 if m % HD < half else 1.0
    i, j = t[:, None], t[None, :]
    count = sum(((i - j) % d == 0) & (np.abs(i - j) <= w // 2) for w, d in ((128, 1), (512, 4), (2048, 16)))
    logs = np.where(count > 0, np.log(np.maximum(count, 1)), -1e30).astype(np.float32)
    s, r = np.arange(RC)[:, None], np.arange(RC)[None, :]
    heads = lambda m: np.stack([np.concatenate([m * (h == g) for g in range(2)], 1) for h in range(2)]).reshape(P, P)
    levels, causal, lvl0, strict = [], [], [], []
    for d in range(2):
        before = (s < r) if d == 0 else (s > r)
        by_level = [before & (s // (2 << n) == r // (2 << n)) & (s >> n != r >> n) for n in range(6)]
        levels += [heads(m) for m in by_level]
        causal += [heads(before), heads(before | (s == r))]
        lvl0.append(np.tile(by_level[0], (2, 1)))
        strict.append(np.tile(before, (2, 1)))
    masks = np.concatenate([np.asarray(m, np.float32) for m in levels + causal + lvl0 + strict], axis=1)
    return {
        "rope_cos": np.cos(ang), "rope_sin": np.sin(ang), "rope_turn": turn,
        "att_mask": logs.reshape(NCH, P, T).transpose(1, 0, 2),
        "reset": np.broadcast_to((np.arange(AB * T) % RC != 0).astype(np.float32)[None], (P, AB * T)),
        "rwkv_masks": masks,
        "stack": np.tile(np.eye(RC, dtype=np.float32), (2, 1)),
    }


def build_program(nc, a, out):
    with ExitStack() as ctx:
        k = allocate(nc, ctx)
        block = ctx.enter_context(nc.Block())

        @block.sync
        def _(sp):
            sync_program(k, sp, a, out)

        @block.gpsimd
        def _(pool):
            gpsimd_program(k, pool)

        @block.scalar
        def _(act):
            scalar_program(k, act, a)

        @block.vector
        def _(v):
            vector_program(k, v)

        @block.tensor
        def _(pe):
            tensor_program(k, pe)


def weight_tiles(w):
    rows, cols = w.shape
    w = w.reshape(rows // P, P, cols // P, P).transpose(2, 1, 0, 3)
    return np.ascontiguousarray(w).reshape(cols // P, P, rows)


def down_tiles(w, chunks):
    out, row = {}, 0
    for blocks in chunks:
        out.setdefault(blocks, []).append(weight_tiles(w[row:row + blocks * P]))
        row += blocks * P
    return [np.concatenate(x) for x in out.values()]


def turns(a, b):
    return np.stack([a, b], 1).reshape(2 * a.shape[0], *a.shape[1:])


def columns(x):
    return np.asarray(x).reshape(-1, P).T


def layouts(i):
    w = i["w_in"][0]
    o_z, o_xbc, o_dt = 4096, 5120, 7168
    h = {
        "x": i["x"][0].T.reshape(KB, P, T).transpose(1, 0, 2),
        "w_in": np.concatenate([weight_tiles(w[:, :o_dt]), weight_tiles(w[:, o_dt + 16:])]),
        "w_dt": w[:, o_dt:o_dt + 16].reshape(KB, P, 16).transpose(1, 0, 2),
        "w_mlp_up": weight_tiles(i["w_mlp_up"][0]),
        "w_mlp_down": down_tiles(i["w_mlp_down"][0], (8,) * UP_CHUNKS)[0],
        "w_in_2": weight_tiles(i["w_in_2"][0]),
        "lru_w_r": i["lru_w_r"][0].transpose(1, 0, 2),
        "lru_w_i": i["lru_w_i"][0].transpose(1, 0, 2),
        "gmlp_w": i["gmlp_w_s"][0].transpose(2, 0, 1),
        "gmlp_b": np.broadcast_to(i["gmlp_b_s"][0][None], (P, 8, P)),
        "dt_rows": np.broadcast_to(np.concatenate([i["ssd_dt_bias"][0], i["ssd_a_log"][0]])[None], (P, 32)),
    }
    for name in ("w_branch_a", "w_branch_b", "w_branch_c", "w_out", "w_out_2"):
        h[name] = weight_tiles(i[name][0])
    for kind in ("ffn1", "ffn2"):
        h[f"{kind}_gu"] = turns(weight_tiles(i[f"{kind}_w_gate_2"][0]), weight_tiles(i[f"{kind}_w_up_2"][0]))
        h[f"{kind}_down"], h[f"{kind}_down_tail"] = down_tiles(i[f"{kind}_w_down_2"][0], FF2_CHUNKS)
    cols = np.zeros((P, NCOLS), np.float32)
    for name, c in COLS.items():
        x = i[name]
        x = np.repeat(x, SSD_P, axis=-1) if name == "ssd_d" else x
        x = columns(x)
        cols[:, c:c + x.shape[1]] = x
    h["cols"] = cols
    r = np.arange(P)
    h["ones"] = np.ones((P, P), np.float32)
    h["ident"] = np.eye(P, dtype=np.float32)
    h["tri"] = (r[:, None] <= r[None, :]).astype(np.float32)
    h["blk"] = (r[:, None] // HD == r[None, :] // HD).astype(np.float32)
    h["lora"] = np.stack([i["rwkv_w2_2"][0].reshape(P, 512), i["rwkv_a2_2"][0].reshape(P, 512),
                          i["rwkv_g2_2"][0]], axis=1)
    h.update(second_constants())
    return {n: np.ascontiguousarray(x) for n, x in h.items()}


def kernel(**inputs):
    import concourse.bacc as bacc
    from concourse.bass_utils import run_bass_kernel_spmd

    arrays = layouts({n: np.asarray(x) for n, x in inputs.items()})
    nc = bacc.Bacc("TRN2", target_bir_lowering=False, num_devices=1)
    aps = {n: nc.dram_tensor(f"in_{n}", x.shape, F32, kind="ExternalInput").ap() for n, x in arrays.items()}
    out = nc.dram_tensor("out_x", (P, KB, T), F32, kind="ExternalOutput").ap()
    build_program(nc, aps, out)
    r = run_bass_kernel_spmd(nc, [{f"in_{n}": x for n, x in arrays.items()}], core_ids=[0])
    y = r.results[0]["out_x"]
    return np.ascontiguousarray(y.transpose(1, 0, 2).reshape(D, T).T)[None]
```

```python
from contextlib import ExitStack

import numpy as np

import concourse.bass as bass
from concourse import mybir

F32 = mybir.dt.float32
F32R = mybir.dt.float32r
BF16 = mybir.dt.bfloat16
ALU = mybir.AluOpType
ACT = mybir.ActivationFunctionType
AX_X = mybir.AxisListType.X

P = 128
T = 256
D = 1024
KB = D // P
CH = 128
NCH = T // CH
RING = 4
TILE = KB * P
EPS = 1e-6
GN_EPS = 64e-5

SSD_HEADS = 16
SSD_P = 64
GROUPS = 4
ATT_HEADS = 8
HD = 64
AB = 4
RC = 64
NRC = T // RC
FF2_CHUNKS = (8, 8, 6)
UP_CHUNKS = 4

COLS = {}
_n = 0
for _name, _width in (
    ("norm_mix_g", 8), ("b_gate", 24), ("gmlp_ln_g", 8), ("gmlp_ln_b", 8), ("lru_conv_w", 32),
    ("lru_conv_b", 8), ("lru_b_r", 8), ("lru_b_i", 8), ("lru_lambda", 8), ("ssd_conv_w", 64),
    ("ssd_conv_b", 16), ("ssd_d", 8), ("ssd_norm_g", 8), ("norm_mlp_g", 8), ("final_norm_g", 8),
    ("ffn1_pre_g_2", 8), ("ffn1_post_g_2", 8), ("mix_pre_g_2", 8), ("rwkv_mu_prev_2", 15),
    ("rwkv_mu_next_2", 15), ("rwkv_w0_2", 8), ("rwkv_a0_2", 8), ("rwkv_k_k_2", 4), ("rwkv_k_a_2", 4),
    ("rwkv_r_k_2", 4), ("rwkv_lnx_w_2", 4), ("rwkv_lnx_b_2", 4), ("attn_out_g_2", 4),
    ("mix_post_g_2", 8), ("ffn2_pre_g_2", 8), ("ffn2_post_g_2", 8),
):
    COLS[_name] = _n
    _n += _width
NCOLS = _n


class Segment:

    def __init__(self, name, dram, first, n, start, operand, kt):
        self.name, self.dram, self.first, self.n = name, dram, first, n
        self.start, self.operand, self.kt = start, operand, kt


class Operand:

    def __init__(self, base, n, parts):
        self.base, self.n, self.free = base, n, 0
        self.hi, self.lo = parts


class Kit:
    pass


def plan():
    segments, start = [], 0

    def seg(name, dram, first, n, operand, kt=KB):
        nonlocal start
        segments.append(Segment(name, dram, first, n, start, operand, kt))
        start += n

    seg("xbc", "w_in", 40, 16, "hn")
    seg("z", "w_in", 32, 8, "hn")
    seg("v", "w_in", 8, 8, "hn")
    seg("u", "w_in", 0, 8, "hn")
    seg("xb", "w_in", 16, 8, "hn")
    seg("gt", "w_in", 24, 8, "hn")
    seg("gate_c", "w_in", 72, 8, "hn")
    seg("branch_c", "w_branch_c", 0, 8, "y_c")
    seg("gate_a", "w_in", 56, 8, "hn")
    seg("branch_a", "w_branch_a", 0, 8, "y_a")
    seg("gate_b", "w_in", 64, 8, "hn")
    seg("branch_b", "w_branch_b", 0, 8, "y_b")
    seg("out", "w_out", 0, 8, "merged")

    def mlp(kind, ups, up_dram, down_drams, operand, per):
        def up(c):
            first = sum(ups[:c]) * per
            seg(f"{kind}_up{c}", up_dram, first, ups[c] * per, operand)

        def down(c):
            seg(f"{kind}_down{c}", down_drams[c][0], down_drams[c][1], 8, f"{kind}_hid{c}", ups[c])

        up(0)
        for c in range(1, len(ups)):
            up(c)
            down(c - 1)
        down(len(ups) - 1)

    mlp("mlp", (8,) * UP_CHUNKS, "w_mlp_up", [("w_mlp_down", 8 * c) for c in range(UP_CHUNKS)], "hn_mlp", 1)
    mlp("ffn1", FF2_CHUNKS, "ffn1_gu", [("ffn1_down", 0), ("ffn1_down", 8), ("ffn1_down_tail", 0)], "hn_ffn1", 2)
    seg("rwkv_in", "w_in_2", 12, 15, "hn_mix")
    seg("qkv", "w_in_2", 0, 12, "hn_mix")
    seg("out_2", "w_out_2", 0, 8, "y_mix")
    mlp("ffn2", FF2_CHUNKS, "ffn2_gu", [("ffn2_down", 0), ("ffn2_down", 8), ("ffn2_down_tail", 0)], "hn_ffn2", 2)
    return segments


OPERANDS = [("hn", 8, "A"), ("y_c", 8, "B0"), ("y_a", 8, "B1"), ("y_b", 8, "B0"), ("merged", 8, "A"),
            ("hn_mlp", 8, "B0")]
OPERANDS += [(f"mlp_hid{c}", 8, ("B1", "A")[c % 2]) for c in range(UP_CHUNKS)]
OPERANDS += [("hn_ffn1", 8, "B0")]
OPERANDS += [(f"ffn1_hid{c}", n, ("B1", "A")[c % 2]) for c, n in enumerate(FF2_CHUNKS)]
OPERANDS += [("hn_mix", 8, "A"), ("y_mix", 8, "A"), ("hn_ffn2", 8, "B0")]
OPERANDS += [(f"ffn2_hid{c}", n, ("B1", "A")[c % 2]) for c, n in enumerate(FF2_CHUNKS)]


ACT_SEGMENTS = [("z", 8), ("v", 8), ("u", 8), ("gt", 8), ("gate_c", 8), ("gate_a", 8), ("gate_b", 8)]
ACT_SEGMENTS += [(f"{f}_up{c}", n) for f in ("ffn1", "ffn2") for c, n in enumerate(FF2_CHUNKS)]

CONST_DMAS = 6


def tiles(eng, n, peel=False, unroll=False):
    if unroll:
        yield from ((i, i % RING, i // RING) for i in range(n))
        return
    first = 1 if peel else 0
    for i in range(first * RING):
        yield i, i % RING, i // RING
    groups = n // RING - first
    if groups > 1:
        with eng.Fori(first, first + groups) as q:
            for j in range(RING):
                yield q * RING + j, j, q
        done = n // RING * RING
    else:
        done = first * RING
    for i in range(done, n):
        yield i, i % RING, i // RING


def at(eng, i, size=1):
    return bass.ds(i * size, size)


class Steps:

    def __init__(self, eng, sem):
        self.eng, self.sem, self.n = eng, sem, 0

    def do(self, ins):
        ins.then_inc(self.sem, 1)
        self.n += 1

    def settle(self, back=0):
        self.eng.wait_ge(self.sem, self.n - back)


SMALL_EVENTS = (
    "x_in consts_in late_in lru_w_in step_v step_a sq rms_mm rms_sqrt hi_ready lo_ready tiles_used evacuated "
    "act_out op_ready zeroed ssd_silu conv_done rs_col_mm dt_mm rs_ready sp_z sp_exp sp_ln sp_u adt acs_mm acs "
    "ds_exp xs_tr xs_ev b_tr b_ev cb_mm cbm xdec st_mm st_ev rb_mm e_min e_exp ex_exp mt ce y_mm y_ev "
    "yz gn_sq gn_mm gn_sqrt gn_done "
    "v_sum_mm v_cent v_sq v_var_mm v_sqrt v_scaled v_norm v_tr v_ev gws mix_mm mix_ev "
    "merged lru_conv ri_mm ri_sig lru_at lru_q lru_sqrt lru_done ssd_done "
    "hid_t hid_w "
    "x_final "
    "rope_in att_in rwkv_in masks_in shifted lora_in w_mm w_sig a_mm a_sig g_mm g_ev kk_sq kk_mm kk_sqrt "
    "lw_scan l_ex ex_exp2 n_exp p_exp bonus_in bonus_mm rope_mm rope_ev "
    "vt_tr vt_ev s_mm s_ev s_red s_exp p_tr p_ev o_mm o_sq o_sqrt o_fin o_tr "
    "v_tok_mm v_tok_ev kka cb_made cbaq_made z_made za_made zq_made z_cleared gb_mm gc_mm gb_ev gc_ev y_taken tok_tr tok_ev zn u_mm uc_ev zu_ev ztt t_mm t_ev tt_mm tt_ev bonus_ev "
    "x_mm x_ev sa_mm sa_ev yy_mm yy_ev ss_mm ss_ev y_sq y_sqrt y_norm y_fm out_done"
).split()


def allocate(nc, ctx):
    k = Kit()
    k.nc = nc

    def sb(name, shape, dtype=F32):
        return ctx.enter_context(nc.sbuf_tensor(name, shape, dtype))

    k.raw = sb("raw_ring", [P, RING, TILE])
    k.whi = sb("weight_hi", [P, RING, TILE], F32R)
    k.wlo = sb("weight_lo", [P, RING, TILE], F32R)
    k.x = sb("x_stream", [P, KB, T])
    k.cols = sb("cols", [P, NCOLS])
    k.ones = sb("ones", [P, P])
    k.ident = sb("ident", [P, P])
    k.tri = sb("tri", [P, P])
    k.blk = sb("block_ones", [P, P])
    k.rs = sb("rs", [P, T])
    k.sd = sb("sd", [P, T])
    k.eps = sb("eps", [P, 2])
    k.rv = sb("rv", [P, T])
    k.wdt = sb("dt_weight", [P, KB, 16])
    k.wdt_hi = sb("dt_weight_hi", [P, KB, 16], F32R)
    k.wdt_lo = sb("dt_weight_lo", [P, KB, 16], F32R)
    k.pre = sb("pre", [P, RING, T])
    k.small = sb("small", [P, 640])
    arena_floats = 22592
    arena_at = -(-nc.sbuf_base // 32) * 32
    k.arena = sb("arena", [P, arena_floats + 6 * KB * T])
    k.operand = {}
    for n, name in enumerate(("A", "B0", "B1")):
        off = arena_at + 4 * (arena_floats + 2 * n * KB * T)
        k.operand[name] = [
            nc.alloc_sbuf_tensor_at(f"operand_{name}_{part}", [P, KB, T], F32R, offset=off + 4 * h * KB * T)
            for h, part in enumerate(("hi", "lo"))]
    k.slots = [ctx.enter_context(nc.psum_tensor(f"product{i}", [P, 512], F32)) for i in range(RING)]
    k.bank = [ctx.enter_context(nc.psum_tensor(f"bank{i}", [P, 512], F32)) for i in range(4)]
    k.decay_bank = k.bank[0:2] + k.slots[0:2]
    k.half_bank = [k.bank, k.slots]
    k.landed = [ctx.enter_context(nc.semaphore(f"landed{i}")) for i in range(RING)]
    k.s = {name: ctx.enter_context(nc.semaphore(name)) for name in SMALL_EVENTS}
    k.segs = {g.name: g for g in plan()}
    k.total = sum(g.n for g in k.segs.values())
    k.made, n = {}, 0
    for name, blocks, buf in OPERANDS:
        k.made[name] = Operand(n, blocks, k.operand[buf])
        n += blocks

    last_use = {}
    for name, _, buf in OPERANDS:
        k.made[name].free = last_use.get(buf, 0)
        last_use[buf] = max([g.start + g.n for g in k.segs.values() if g.operand == name], default=0)

    k.act_before, k.act_after, n = {}, {}, 0
    for name, blocks in ACT_SEGMENTS:
        k.act_before[name], n = n, n + blocks
        k.act_after[name] = n

    def region(start, blocks, width=T):
        return k.arena[:, start:start + blocks * width].rearrange("p (b t) -> p b t", b=blocks)

    pad = T + 3
    k.xbc_pad = region(0, 16, pad)
    k.xdt = region(0, NCH, D)
    k.xdec = k.arena[:, 2048:3072]
    k.state = k.arena[:, 3072:4096]
    k.gm_sq = region(0, 8)
    k.xc = region(4144, 16)
    k.z = region(8240, 8)
    k.v = region(10288, 8)
    k.u = region(12336, 8)
    k.xb_pad = region(2048, 8, pad)
    k.gt = region(14384, 8)
    k.g = region(16432, 8)
    k.mt = region(16432, 2)
    k.ex = region(16432 + 512, 2, P)
    k.ce = region(16432 + 768, 2, P)
    k.gn_sq = k.gt
    k.vt = region(4144, NCH, D)
    k.m = region(18480, 8)
    k.cbm = region(18480, NCH * GROUPS, P)
    k.bt = k.arena[:, 18480 + 1024:18480 + 1536]
    k.e = region(18480 + 1536, 2)
    k.gn_rs = k.arena[:, 18480:18480 + 512]
    k.gmix = k.arena[:, 18480 + 512:18480 + 1024]
    k.gn_sd = region(18480 + 1024, 2, 512)
    k.wr = region(20528, 8, P)
    k.wi = region(21552, 8, P)
    k.gws = region(20528, 8, P)
    k.bs = region(21552, 8, P)
    k.xb = k.v
    k.r = region(4144, 8)
    k.i = region(4144 + 2048, 8)
    k.a = region(0, 8)
    k.t = region(2048, 8)
    k.sq0 = k.v
    k.sq = k.g
    k.f = k.z
    k.hid = k.v
    k.sg = k.u

    k.stack = sb("stacked_identity", [P, RC])
    k.us = region(0, 15)
    k.upad = region(3840, 15, T + 2)
    k.qkv = region(7712, 12)
    k.gout = region(3072, 4)
    k.lw = region(4096, 8)
    k.kk = region(6144, 4)
    k.reset = k.arena[:, 20000:21024]
    k.bv = region(1024, 4)
    k.y_att = region(10784, 4)
    k.ia = region(11808, 8)
    k.lc = region(13856, 8)
    k.lx = region(15904, 8)
    k.en = region(17952, 8)
    k.kd = region(20000, 8)
    tail = arena_floats
    k.cbaq = k.arena[:, tail + 4096:tail + 12288].rearrange("p (w d b t) -> p w d b t", w=4, d=2, b=AB)
    k.att_v = region(tail, NCH, 512)
    k.att_s = region(tail + 1024, 2, 512)
    k.att_p = region(tail + 2048, 2, 512)
    k.att_o = region(tail + 3072, NCH, 512)
    k.att_mask = region(22048, 2)
    units = lambda start, width: region(start, 8, width)
    k.vtok = k.arena[:, 4096:5120].rearrange("p (c b v) -> p c b v", b=AB, c=NRC)
    k.masks = k.arena[:, 5120:6144]
    k.levels = k.masks.rearrange("p (d m t) -> p d m t", d=2, m=8)
    k.zc, k.zb, k.za, k.zq = units(6144, P), units(0, P), units(2048, P), units(7712, P)
    k.ysq = k.arena[:, 7168:7680].rearrange("p (c b v) -> p c b v", b=AB, c=2)
    k.ytok = k.arena[:, 8736:9760].rearrange("p (c b v) -> p c b v", b=AB, c=NRC)
    k.xs, k.sa = units(9760, RC), units(10272, RC)
    k.st, k.nt, k.tc, k.ttc = (units(11808 + 512 * n, RC) for n in range(4))
    k.ztt, k.uc, k.zu, k.zn = units(13856, P), units(14880, RC), units(15392, P), units(16416, P)
    k.zaac, k.zaqc, k.zaqb = (units(17440 + 1024 * n, P) for n in range(3))
    k.ctok, k.btok = units(20512, P), units(21536, P)
    k.bonus = region(tail + 4096, 4)
    k.yf = region(7712, 4)
    k.lora = k.arena[:, tail + 10240:tail + 11776].rearrange("p (w n) -> p w n", w=3)
    return k


def col(k, name, b=0):
    c = COLS[name] + b
    return k.cols[:, c:c + 1]


class Small:

    def __init__(self, k):
        s = k.small
        self.rs_col = s[:, 0:2]
        self.z = s[:, 8:48]
        self.ab = s[:, 48:88]
        self.e = s[:, 88:128]
        self.u = s[:, 128:168]
        self.um = s[:, 168:208]
        self.d = s[:, 208:248]
        self.ru = s[:, 248:288]
        self.ln = s[:, 288:328]
        self.sp = s[:, 328:368]
        self.ea = s[:, 368:384]
        self.adt = s[:, 384:416]
        self.acs = s[:, 416:448]
        self.dz = s[:, 448:464]
        self.ds = s[:, 464:480]
        self.dtb = s[:, 480:496]
        self.alog = s[:, 496:512]
        self.dtb_alog = s[:, 480:512]
        self.nsp8 = s[:, 512:520]
        self.psp8 = s[:, 520:528]


def sync_program(k, sp, a, out):
    for seg in k.segs.values():
        w = seg.kt * P
        for i, j, _ in tiles(sp, seg.n, peel=seg.start == 0):
            slot = (seg.start + j) % RING
            if seg.start or not isinstance(i, int) or i >= RING:
                sp.wait_ge(k.s["lo_ready"], i + (seg.start - RING + 1))
            src = a[seg.dram][at(sp, i + seg.first), :, :].rearrange("o p n -> p (o n)")
            sp.dma_start(k.raw[:, slot, 0:w], src).then_inc(k.landed[slot], 16)
    for half in range(2):
        h4 = slice(4 * half, 4 * half + 4)
        sp.wait_ge(k.s["out_done"], half + 1)
        sp.dma_start(out[:, h4, :], k.x[:, h4, :]).then_inc(k.s["x_in"], 16)
    sp.wait_ge(k.s["x_in"], 48)


def gpsimd_program(k, pool):
    def low_parts(first, last):
        for i, j, _ in tiles(pool, last - first):
            slot = (first + j) % RING
            pool.wait_ge(k.s["hi_ready"], i + (first + 1))
            k.nc.gpsimd.tensor_tensor(k.wlo[:, slot, :], k.raw[:, slot, :], k.whi[:, slot, :].bitcast(F32),
                                      ALU.subtract).then_inc(k.s["lo_ready"], 1)

    before_rwkv = k.segs["out_2"].start + RING - 1
    low_parts(0, before_rwkv)
    pool.wait_ge(k.s["kka"], 1)
    pool.wait_ge(k.s["n_exp"], 1)
    pool.wait_ge(k.s["bonus_mm"], 1)
    c_, b_ = (k.cbaq[:, n].rearrange("p d b t -> p (d b) t") for n in range(2))
    for out, x in ((b_, k.ia), (c_, k.kd)):
        k.nc.gpsimd.tensor_tensor(out, x, k.en, ALU.mult).then_inc(k.s["cb_made"], 1)
    pool.wait_ge(k.s["cbaq_made"], 1)
    for z in (k.zn, k.zaac, k.zaqc, k.zaqb, k.zu):
        k.nc.gpsimd.memset(z, 0.0).then_inc(k.s["z_cleared"], 1)
    low_parts(before_rwkv, k.total)


def dense(k, pe, name, peel=False, unroll=False, after=None):
    seg = k.segs[name]
    op = k.made[seg.operand]
    mm = k.nc.tensor.matmul
    for i, j, _ in tiles(pe, seg.n, peel or seg.start == 0, unroll):
        slot = (seg.start + j) % RING
        pe.wait_ge(k.s["lo_ready"], i + (seg.start + 1))
        if seg.start or not isinstance(i, int) or i >= RING:
            pe.wait_ge(k.s["evacuated"], i + (seg.start - RING + 1))
        w_hi, w_lo, ps = k.whi[:, slot, :], k.wlo[:, slot, :], k.slots[slot][:, 0:T]
        for b in range(seg.kt):
            if j == 0:
                pe.wait_ge(k.s["op_ready"], op.base + b + 1)
            n = slice(b * P, (b + 1) * P)
            mm(ps, w_hi[:, n], op.hi[:, b, :], start=b == 0, stop=False)
            mm(ps, w_hi[:, n], op.lo[:, b, :], start=False, stop=False)
            last = mm(ps, w_lo[:, n], op.hi[:, b, :], start=False, stop=b == seg.kt - 1)
        last.then_inc(k.s["tiles_used"], 1)
        if after and isinstance(i, int):
            after(i)


def column_sums(k, src, blocks, bank, weights=None):
    for b in range(blocks):
        last = k.nc.tensor.matmul(bank, (weights or k.ones)[:], src[:, b, :], start=b == 0, stop=b == blocks - 1)
    return last


def tensor_program(k, pe):
    s, mm, c = k.s, k.nc.tensor.matmul, Small(k)
    pe.wait_ge(s["consts_in"], 16 * CONST_DMAS)

    norms = [0]

    def rms_sum(norm, b, src):
        pe.wait_ge(s["sq"], KB * norm + b + 1)
        last = mm(k.bank[0][:, 0:T], k.ones[:], src[:, b, :], start=b == 0, stop=b == KB - 1)
        if b == KB - 1:
            last.then_inc(s["rms_mm"], 1)

    def sums_behind_first(name, src):
        norm = norms[0]
        norms[0] += 1

        def after(i):
            if i == 0:
                for b in range(KB):
                    rms_sum(norm, b, src)
        dense(k, pe, name, peel=True, after=after)

    def sums_of_outputs(name):
        norm = norms[0]
        norms[0] += 1
        dense(k, pe, name, unroll=True, after=lambda i: rms_sum(norm, i - 2, k.sq) if i >= 2 else None)
        for b in (KB - 2, KB - 1):
            rms_sum(norm, b, k.sq)

    sums_behind_first("xbc", k.sq0)
    dense(k, pe, "z")

    for ch in range(NCH):
        last = mm(k.bank[1][:, ch:ch + 1], k.rs[:, ch * P:(ch + 1) * P], k.ident[:, 0:1], start=True, stop=True)
    last.then_inc(s["rs_col_mm"], 1)
    op = k.made["hn"]
    for ch in range(NCH):
        tok = slice(ch * P, (ch + 1) * P)
        for b in range(KB):
            ps = k.bank[2][:, ch * 16:ch * 16 + 16]
            mm(ps, op.hi[:, b, tok], k.wdt_hi[:, b, :], start=b == 0, stop=False)
            mm(ps, op.lo[:, b, tok], k.wdt_hi[:, b, :], start=False, stop=False)
            last = mm(ps, op.hi[:, b, tok], k.wdt_lo[:, b, :], start=False, stop=b == KB - 1)
    last.then_inc(s["dt_mm"], 1)
    dense(k, pe, "v")
    dense(k, pe, "u")

    pe.wait_ge(s["adt"], 1)
    mm(k.bank[1][:, 0:32], k.tri[:], c.adt, start=True, stop=True)
    mm(k.bank[1][:, 32:64], k.ones[:], c.adt, start=True, stop=True).then_inc(s["acs_mm"], 1)
    pe.wait_ge(s["ssd_silu"], 4)
    for n in range(4):
        ch, half = n // 2, n % 2
        if n >= 2:
            pe.wait_ge(s["xs_ev"], n - 1)
        for b in range(4):
            last = k.nc.tensor.transpose(k.bank[2 + n % 2][:, b * P:(b + 1) * P],
                                         k.xc[:, half * 4 + b, ch * P:(ch + 1) * P], k.ident[:])
        last.then_inc(s["xs_tr"], 1)
    pe.wait_ge(s["xs_ev"], 3)
    for g in range(GROUPS):
        last = k.nc.tensor.transpose(k.bank[2][:, g * P:(g + 1) * P], k.xc[:, 8 + g, 0:P], k.ident[:])
    last.then_inc(s["b_tr"], 1)
    for ch in range(NCH):
        if ch == 0:
            pe.wait_ge(s["xs_ev"], 4)
        else:
            pe.wait_ge(s["b_ev"], 1)
        for g in range(GROUPS):
            tok = slice(ch * P, (ch + 1) * P)
            last = mm(k.bank[3 - ch][:, g * P:(g + 1) * P], k.xc[:, 8 + g, tok], k.xc[:, 12 + g, tok],
                      start=True, stop=True)
        last.then_inc(s["cb_mm"], 1)
    pe.wait_ge(s["xdec"], 1)
    pe.wait_ge(s["acs"], 1)
    for half in range(2):
        if half == 1:
            pe.wait_ge(s["cbm"], 2)
        for g in range(2):
            gg = half * 2 + g
            last = mm(k.bank[(1, 2)[half]][:, g * 256:(g + 1) * 256], k.bt[:, gg * P:(gg + 1) * P],
                      k.xdec[:, gg * 256:(gg + 1) * 256], start=True, stop=True)
        last.then_inc(s["st_mm"], 1)
    pe.wait_ge(s["st_ev"], 2)

    def rb(h):
        if h >= 4:
            pe.wait_ge(s["e_min"], h - 3)
            pe.wait_ge(s["ex_exp"], h - 3)
        for ch in range(NCH):
            last = mm(k.decay_bank[h % 4][:, ch * P:(ch + 1) * P],
                      c.adt[:, ch * 16 + h:ch * 16 + h + 1].to_broadcast([P, P]), k.tri[:],
                      start=True, stop=True)
        last.then_inc(s["rb_mm"], 1)

    pe.wait_ge(s["evacuated"], k.segs["u"].start + 8)
    rb(0)
    rb(1)
    for h in range(SSD_HEADS):
        if h + 2 < SSD_HEADS:
            rb(h + 2)
        b, q = h // 2, 64 * (h % 2)
        y = k.bank[2 + b % 2]
        if h % 2 == 0 and b >= 2:
            pe.wait_ge(s["y_ev"], b - 1)
        pe.wait_ge(s["ce"], h + 1)
        mm(y[q:q + 64, 0:P], k.xdt[:, 0, h * 64:h * 64 + 64], k.mt[:, h % 2, 0:P], start=True, stop=True)
        mm(y[q:q + 64, P:T], k.xdt[:, 1, h * 64:h * 64 + 64], k.mt[:, h % 2, P:T], start=True, stop=False)
        mm(y[q:q + 64, P:T], k.state[:, h * 64:h * 64 + 64], k.ce[:, h % 2, :], start=False,
           stop=True).then_inc(s["y_mm"], 1)
    dense(k, pe, "xb")
    for g in range(GROUPS):
        pe.wait_ge(s["gn_sq"], g + 1)
        column_sums(k, k.gn_sq[:, 2 * g:2 * g + 2, :], 2, k.bank[g // 2][:, (g % 2) * T:(g % 2 + 1) * T]).then_inc(s["gn_mm"], 1)
    pe.wait_ge(s["act_out"], k.act_after["v"])
    pe.wait_ge(s["y_ev"], 8)
    column_sums(k, k.v, KB, k.bank[2][:, 0:T]).then_inc(s["v_sum_mm"], 1)
    dense(k, pe, "gt")
    pe.wait_ge(s["v_sq"], 2)
    column_sums(k, k.gm_sq, KB, k.bank[3][:, 0:T]).then_inc(s["v_var_mm"], 1)
    dense(k, pe, "gate_c")
    pe.wait_ge(s["gn_done"], 2)
    pe.wait_ge(s["v_norm"], KB)
    for n in range(4):
        ch, half = n // 2, n % 2
        if n >= 2:
            pe.wait_ge(s["v_ev"], n - 1)
        for b in range(4):
            last = k.nc.tensor.transpose(k.bank[n % 2][:, b * P:(b + 1) * P],
                                         k.v[:, half * 4 + b, ch * P:(ch + 1) * P], k.ident[:])
        last.then_inc(s["v_tr"], 1)
    pe.wait_ge(s["gws"], 1)
    pe.wait_ge(s["v_ev"], 4)
    for n in range(4):
        if n >= 2:
            pe.wait_ge(s["mix_ev"], n - 1)
        for g in (2 * n, 2 * n + 1):
            for ch in range(NCH):
                last = mm(k.bank[n % 2][:, (g % 2) * T + ch * P:(g % 2) * T + (ch + 1) * P],
                          k.vt[:, ch, g * P:(g + 1) * P], k.gws[:, g, :], start=True, stop=True)
        last.then_inc(s["mix_mm"], 1)
    dense(k, pe, "branch_c")

    pe.wait_ge(s["lru_w_in"], 32)
    pe.wait_ge(s["lru_conv"], 2)
    for b in range(KB):
        if b >= 2:
            pe.wait_ge(s["ri_sig"], 2 * (b - 1))
        mm(k.bank[2 + b % 2][:, 0:T], k.wr[:, b, :], k.xb[:, b, :], start=True, stop=True)
        mm(k.bank[2 + b % 2][:, T:512], k.wi[:, b, :], k.xb[:, b, :], start=True, stop=True).then_inc(s["ri_mm"], 1)
    dense(k, pe, "gate_a")
    dense(k, pe, "branch_a")
    dense(k, pe, "gate_b")
    dense(k, pe, "branch_b")
    sums_of_outputs("out")

    for c1 in range(UP_CHUNKS):
        dense(k, pe, f"mlp_up{c1}")
        if c1:
            dense(k, pe, f"mlp_down{c1 - 1}")
    sums_of_outputs(f"mlp_down{UP_CHUNKS - 1}")

    def ffn(kind):
        sums_behind_first(f"{kind}_up0", k.sq)
        for c1 in range(1, len(FF2_CHUNKS)):
            dense(k, pe, f"{kind}_up{c1}")
            dense(k, pe, f"{kind}_down{c1 - 1}")
        sums_of_outputs(f"{kind}_down{len(FF2_CHUNKS) - 1}")

    ffn("ffn1")

    sums_behind_first("rwkv_in", k.sq)

    def lora(which, src, banks, half=None):
        rows = slice(0, P) if half is None else slice(64 * half, 64 * half + 64)
        for b in range(AB):
            last = mm(banks[b // 2][:, (b % 2) * T:(b % 2 + 1) * T], k.lora[rows, which, b * P:(b + 1) * P],
                      src[rows, :], start=True, stop=True)
        return last

    pe.wait_ge(s["late_in"], 64)
    pe.wait_ge(s["rwkv_in"], 16)
    pe.wait_ge(s["lora_in"], 1)
    lora(0, k.us[:, 12, :], k.bank[0:2], 0)
    lora(0, k.us[:, 12, :], k.bank[2:4], 1).then_inc(s["w_mm"], 1)
    dense(k, pe, "qkv")
    pe.wait_ge(s["w_sig"], 8)
    lora(1, k.us[:, 13, :], k.bank[0:2], 0)
    lora(1, k.us[:, 13, :], k.bank[2:4], 1).then_inc(s["a_mm"], 1)
    pe.wait_ge(s["rope_in"], 48)
    pe.wait_ge(s["evacuated"], k.segs["qkv"].start + 12)
    for b in range(8):
        last = mm(k.slots[b // 2][:, (b % 2) * T:(b % 2 + 1) * T], k.pre[:, 2, 0:P], k.qkv[:, b, :],
                  start=True, stop=True)
        if b % 2:
            last.then_inc(s["rope_mm"], 1)
    pe.wait_ge(s["a_sig"], 8)
    pe.wait_ge(s["lora_in"], 2)
    lora(2, k.us[:, 14, :], k.bank[0:2]).then_inc(s["g_mm"], 1)

    s4 = k.slots

    def by_head(out, lhs, rhs, start=True, stop=True):
        for rows in (slice(0, HD), slice(HD, P)):
            last = mm(out[rows], lhs[rows], rhs[rows], start=start, stop=stop)
        return last

    pe.wait_ge(s["rope_ev"], 4)
    for ch in range(NCH):
        for b in range(AB):
            last = k.nc.tensor.transpose(k.slots[ch][:, b * P:(b + 1) * P],
                                         k.qkv[:, 8 + b, ch * P:(ch + 1) * P], k.ident[:])
        last.then_inc(s["vt_tr"], 1)

    def scores(h):
        q = 64 * (h % 2)
        if h >= 2:
            pe.wait_ge(s["s_ev"], h - 1)
        for it in range(NCH):
            last = mm(k.slots[2 + h % 2][:, it * T:(it + 1) * T], k.qkv[q:q + 64, h // 2, it * P:(it + 1) * P],
                      k.qkv[q:q + 64, 4 + h // 2, :], start=True, stop=True)
        last.then_inc(s["s_mm"], 1)

    pe.wait_ge(s["vt_ev"], 2)
    pe.wait_ge(s["g_ev"], 1)
    scores(0)
    for h in range(ATT_HEADS + 1):
        if h + 1 < ATT_HEADS:
            scores(h + 1)
        if h < ATT_HEADS:
            pe.wait_ge(s["s_exp"], h + 1)
            if h >= 2:
                pe.wait_ge(s["p_ev"], h - 1)
            for jt in range(NCH):
                for it in range(NCH):
                    last = k.nc.tensor.transpose(k.bank[2 + h % 2][:, jt * T + it * P:jt * T + (it + 1) * P],
                                                 k.att_s[:, h % 2, it * T + jt * P:it * T + (jt + 1) * P], k.ident[:])
            last.then_inc(s["p_tr"], 1)
        if h:
            g = h - 1
            pe.wait_ge(s["p_ev"], g + 1)
            for it in range(NCH):
                for jt in range(NCH):
                    last = mm(k.bank[it][:, g * 64:g * 64 + 64],
                              k.att_p[:, g % 2, jt * T + it * P:jt * T + (it + 1) * P],
                              k.att_v[:, jt, g * 64:g * 64 + 64], start=jt == 0, stop=jt == NCH - 1)
            last.then_inc(s["o_mm"], 1)
        if h == 1:
            pe.wait_ge(s["kk_sq"], 1)
            for b in range(AB):
                last = mm(k.slots[b // 2][:, (b % 2) * T:(b % 2 + 1) * T], k.blk[:], k.en[:, b, :],
                          start=True, stop=True)
            last.then_inc(s["kk_mm"], 1)
        if h == 4:
            pe.wait_ge(s["kk_sqrt"], 1)
            pe.wait_ge(s["lw_scan"], 1)
            for c in range(NRC):
                for b in range(AB):
                    last = by_head(s4[c // 2][:, (c % 2) * T + b * RC:(c % 2) * T + (b + 1) * RC],
                                   k.us[:, 8 + b, c * RC:(c + 1) * RC], k.stack[:])
            last.then_inc(s["v_tok_mm"], 1)
        if h == 5:
            pe.wait_ge(s["v_tok_ev"], 2)
            pe.wait_ge(s["bonus_in"], 1)
            for b in range(AB):
                last = mm(s4[b // 2][:, (b % 2) * T:(b % 2 + 1) * T], k.blk[:], k.bonus[:, b, :],
                          start=True, stop=True)
            last.then_inc(s["bonus_mm"], 1)
    pe.wait_ge(s["bonus_ev"], 2)
    pe.wait_ge(s["o_fin"], 1)
    for b in range(AB):
        for ch in range(NCH):
            last = k.nc.tensor.transpose(k.slots[b // 2][:, (b % 2) * T + ch * P:(b % 2) * T + (ch + 1) * P],
                                         k.att_o[:, ch, b * P:(b + 1) * P], k.ident[:])
    last.then_inc(s["o_tr"], 1)

    def block_chunk(u, j):
        return u % 4, (j if u < 4 else NRC - 1 - j)

    def products(name, z, bank, j):
        for h in range(2):
            for u in range(4 * h, 4 * h + 4):
                b, c = block_chunk(u, j)
                last = mm(k.half_bank[h][bank][:, (u % 4) * P:(u % 4 + 1) * P].rearrange("p (w t) -> p w t", w=2),
                          z[:, u, :], k.cbaq[:, 2:4, h, b, c * RC:(c + 1) * RC], start=True, stop=True)
            last.then_inc(s[name], 1)

    def keep_clock(h, bank, n):
        for _ in range(n):
            mm(k.half_bank[h][bank][:, T:2 * T], k.ones[:, 0:P // 2].bitcast(BF16), k.ones[:].bitcast(BF16),
               start=True, stop=True)

    def per_unit(h, bank, lhs, rhs):
        for u in range(4 * h, 4 * h + 4):
            last = mm(k.half_bank[h][bank][:, (u % 4) * RC:(u % 4 + 1) * RC], lhs[:, u, :], rhs(u),
                      start=True, stop=True)
        return last

    pe.wait_ge(s["z_made"], 1)
    products("gb_mm", k.zb, 3, 0)
    for j in range(NRC):
        for h in range(2):
            if j:
                pe.wait_ge(s["sa_ev"], 2 * j)
            pe.wait_ge(s["zn"], 12 * j + h + 1)
            keep_clock(h, 0, 2)
            per_unit(h, 0, k.zn, lambda u: k.stack[:]).then_inc(s["u_mm"], 1)
        if j:
            pe.wait_ge(s["ss_ev"], 2 * j)
        pe.wait_ge(s["z_made"], 2 * j + 2)
        products("gc_mm", k.zc, 1, j)
        if j:
            pe.wait_ge(s["y_taken"], 2 * j)
        for n, z in enumerate((k.zc, k.zb)):
            for h in range(2):
                if n == 1:
                    pe.wait_ge(s["tok_ev"], 4 * j + h + 1)
                for u in range(4 * h, 4 * h + 4):
                    last = k.nc.tensor.transpose(k.half_bank[h][2][:, (u % 4) * P:(u % 4 + 1) * P], z[:, u, :],
                                                 k.ident[:])
                last.then_inc(s["tok_tr"], 1)
        for level in range(1, 6):
            for h in range(2):
                pe.wait_ge(s["zn"], 12 * j + 2 * level + h + 1)
                pe.wait_ge(s["t_ev"], 10 * j + 2 * level + h - 1)
                keep_clock(h, 0, 1)
                per_unit(h, 0, k.zn, lambda u: k.tc[:, u, :]).then_inc(s["u_mm"], 1)
            if level == 5:
                if j:
                    pe.wait_ge(s["za_made"], j)
                    pe.wait_ge(s["ss_ev"], 2 * j)
                for h in range(2):
                    pe.wait_ge(s["gb_ev"], 2 * j + h + 1)
                    keep_clock(h, 3, 1)
                    for u in range(4 * h, 4 * h + 4):
                        b, c = block_chunk(u, j)
                        o = k.half_bank[h][3][:, (u % 4) * RC:(u % 4 + 1) * RC]
                        if j:
                            mm(o, k.za[:, u, :], k.st[:, u, :], start=True, stop=False)
                        last = mm(o, k.zaac[:, u, :], k.vtok[:, c, b, :], start=j == 0, stop=True)
                    last.then_inc(s["x_mm"], 1)
            for h in range(2):
                pe.wait_ge(s["ztt"], 12 * j + 2 * level + h - 1)
                if level == 1:
                    pe.wait_ge(s["gc_ev"], 2 * j + h + 1)
                    pe.wait_ge(s["tok_ev"], 4 * j + h + 3)
                if level < 5:
                    pe.wait_ge(s["uc_ev"], 8 * j + 2 * level + h - 1)
                    per_unit(h, 1, k.ztt, lambda u: k.uc[:, u, :]).then_inc(s["t_mm"], 1)
                pe.wait_ge(s["zu_ev"], 10 * j + 2 * level + h - 1)
                pe.wait_ge(s["tt_ev"], 12 * j + 2 * level + h - 1)
                per_unit(h, 2, k.zu, lambda u: k.ttc[:, u, :]).then_inc(s["tt_mm"], 1)

        for h in range(2):
            pe.wait_ge(s["ztt"], 12 * j + h + 11)
            pe.wait_ge(s["x_ev"], 2 * j + h + 1)
            per_unit(h, 0, k.ztt, lambda u: k.xs[:, u, :]).then_inc(s["sa_mm"], 1)
        if j + 1 < NRC:
            pe.wait_ge(s["z_made"], 2 * j + 4)
            products("gb_mm", k.zb, 3, j + 1)
        for h in range(2):
            pe.wait_ge(s["sa_ev"], 2 * j + h + 1)
            keep_clock(h, 1, 1)
            for u in range(4 * h, 4 * h + 4):
                b, c = block_chunk(u, j)
                o = k.half_bank[h][1][:, (u % 4) * RC:(u % 4 + 1) * RC]
                mm(o, k.ctok[:, u, :], k.vtok[:, c, b, :], start=True, stop=False)
                last = mm(o, k.btok[:, u, :], k.sa[:, u, :], start=False, stop=True)
            last.then_inc(s["ss_mm"], 1)
        if j:
            pe.wait_ge(s["zq_made"], j)
        for h in range(2):
            keep_clock(h, 2, 1)
            for u in range(4 * h, 4 * h + 4):
                b, c = block_chunk(u, j)
                o = k.half_bank[h][2][:, (u % 4) * RC:(u % 4 + 1) * RC]
                mm(o, k.zaqc[:, u, :], k.vtok[:, c, b, :], start=True, stop=False)
                if j:
                    mm(o, k.zq[:, u, :], k.st[:, u, :], start=False, stop=False)
                last = mm(o, k.zaqb[:, u, :], k.sa[:, u, :], start=False, stop=True)
            last.then_inc(s["yy_mm"], 1)

    pe.wait_ge(s["y_taken"], 2 * NRC)
    for n, chunks in enumerate(((1, 2), (0, 3))):
        pe.wait_ge(s["y_norm"], n + 1)
        for b in range(AB):
            for c in chunks:
                last = by_head(s4[b // 2][:, (b % 2) * T + c * RC:(b % 2) * T + (c + 1) * RC], k.ytok[:, c, b, :],
                               k.stack[:])
    last.then_inc(s["y_fm"], 1)
    sums_of_outputs("out_2")
    ffn("ffn2")


def vector_evacuate(k, v, name, write, first=0, last=None):
    seg = k.segs[name]
    last = seg.n if last is None else last
    for i, j, q in tiles(v, last - first):
        slot = (seg.start + first + j) % RING
        v.wait_ge(k.s["tiles_used"], i + (seg.start + first + 1))
        write(i + first, i + (seg.start + first), j, q, k.slots[slot][:, 0:T])


def vector_to_scalar(k, v, name, first=0, last=None):
    base = k.act_before[name]

    def write(i, t, j, q, product):
        if base or not isinstance(i, int) or i >= RING:
            v.wait_ge(k.s["act_out"], i + (base - RING + 1))
        k.nc.vector.tensor_tensor(k.pre[:, (base + first + j) % RING, :], product, k.rs[:],
                                  ALU.mult).then_inc(k.s["evacuated"], 1)

    vector_evacuate(k, v, name, write, first, last)


def make_operand(k, v, steps, name, first, src, scalar=None):
    op = k.made[name]
    if op.free:
        v.wait_ge(k.s["tiles_used"], op.free)
    n = len(src)
    for b in range(n + 1):
        if b < n:
            hi = op.hi[:, first + b, :]
            if scalar is None:
                steps.do(k.nc.vector.tensor_copy(hi, src[b]))
            else:
                steps.do(k.nc.vector.tensor_scalar(hi, src[b], scalar(b), None, ALU.mult))
        if b > 0:
            steps.settle(1 if b < n else 0)
            hi, lo = op.hi[:, first + b - 1, :].bitcast(F32), op.lo[:, first + b - 1, :]
            if scalar is None:
                ins = k.nc.vector.tensor_tensor(lo, src[b - 1], hi, ALU.subtract)
            else:
                ins = k.nc.vector.scalar_tensor_tensor(lo, src[b - 1], scalar(b - 1), hi, ALU.mult, ALU.subtract)
            ins.then_inc(k.s["op_ready"], 1)


def vector_rms(k, v, steps, sem, value, dst=None):
    v.wait_ge(k.s[sem], value)
    steps.do(k.nc.vector.reciprocal((dst or k.rs)[:], k.sd[:]))
    steps.settle()


def conv(k, v, steps, src, dst, blocks, w, bias, n_blocks):
    for tap in range(4):
        for b in blocks:
            x, wt = src[:, b, tap:tap + T], col(k, w, tap * n_blocks + b)
            if tap == 0:
                steps.do(k.nc.vector.tensor_scalar(dst[:, b, :], x, wt, col(k, bias, b), ALU.mult, ALU.add))
            else:
                steps.settle(len(blocks) - 1)
                steps.do(k.nc.vector.scalar_tensor_tensor(dst[:, b, :], x, wt, dst[:, b, :], ALU.mult, ALU.add))


def gated_sum(k, v, gate, first=False):
    def write(i, t, j, q, product):
        v.wait_ge(k.s["act_out"], i + (k.act_before[gate] + 1))
        g = k.g[:, at(v, i), :].rearrange("p o t -> p (o t)")
        m = k.m[:, at(v, i), :].rearrange("p o t -> p (o t)")
        k.nc.vector.tensor_tensor(m if first else g, product, g, ALU.mult).then_inc(k.s["evacuated"], 1)
        if not first:
            v.wait_ge(k.s["evacuated"], t + 1)
            k.nc.vector.tensor_tensor(m, m, g, ALU.add).then_inc(k.s["merged"], 1)
    return write


def vector_program(k, v):
    s, c, nv = k.s, Small(k), k.nc.vector
    st = Steps(v, s["step_v"])

    nv.memset(k.xbc_pad[:, :, 0:3], 0.0)
    nv.memset(k.eps[:, 0:1], EPS)
    st.do(nv.memset(k.eps[:, 1:2], GN_EPS))
    st.settle()
    v.sem_inc(s["zeroed"], 1)
    v.wait_ge(s["x_in"], 16)
    v.wait_ge(s["consts_in"], 16 * CONST_DMAS)
    make_operand(k, v, st, "hn", 0, [k.x[:, b, :] for b in range(KB)], lambda b: col(k, "norm_mix_g", b))
    st.do(nv.tensor_copy(k.wdt_hi[:], k.wdt[:]))
    st.settle()
    st.do(nv.tensor_tensor(k.wdt_lo[:], k.wdt[:], k.wdt_hi[:].bitcast(F32), ALU.subtract))
    st.settle()
    norms = [0]

    def rms():
        norms[0] += 1
        vector_rms(k, v, st, "rms_sqrt", norms[0])

    rms()
    v.sem_inc(s["rs_ready"], 1)

    def padded(dst):
        def write(i, t, j, q, product):
            o = dst[:, at(v, i), 3:3 + T].rearrange("p o t -> p (o t)")
            k.nc.vector.tensor_tensor(o, product, k.rs[:], ALU.mult).then_inc(s["evacuated"], 1)
        return write

    vector_evacuate(k, v, "xbc", padded(k.xbc_pad))
    v.wait_ge(s["evacuated"], 16)

    def ssd_conv(n):
        conv(k, v, st, k.xbc_pad, k.xc, range(4 * n, 4 * n + 4), "ssd_conv_w", "ssd_conv_b", 16)
        st.settle()
        v.sem_inc(s["conv_done"], 1)

    ssd_conv(0)
    vector_to_scalar(k, v, "z", 0, 4)
    ssd_conv(1)
    vector_to_scalar(k, v, "z", 4, 8)
    ssd_conv(2)
    vector_to_scalar(k, v, "v", 0, 4)
    ssd_conv(3)
    vector_to_scalar(k, v, "v", 4, 8)

    v.wait_ge(s["rs_col_mm"], 1)
    st.do(nv.tensor_copy(c.rs_col, k.bank[1][:, 0:2]))
    v.wait_ge(s["dt_mm"], 1)
    st.settle()
    for ch in range(NCH):
        st.do(nv.scalar_tensor_tensor(c.z[:, ch * 16:ch * 16 + 16], k.bank[2][:, ch * 16:ch * 16 + 16],
                                      c.rs_col[:, ch:ch + 1], c.dtb, ALU.mult, ALU.add))
    nv.tensor_scalar(c.z[:, 32:40], k.cols[:, COLS["lru_lambda"]:COLS["lru_lambda"] + 8], -1.0, None,
                     ALU.mult).then_inc(s["sp_z"], 1)
    v.wait_ge(s["sp_z"], 1)
    st.settle()
    v.sem_inc(s["sp_z"], 1)
    vector_to_scalar(k, v, "u", 0, 4)
    v.wait_ge(s["sp_exp"], 1)
    st.do(nv.tensor_scalar(c.u, c.e, 1.0, None, ALU.add))
    st.settle()
    v.sem_inc(s["sp_u"], 1)
    st.do(nv.tensor_scalar(c.um, c.u, 1.0, None, ALU.subtract))
    st.do(nv.reciprocal(c.ru, c.u))
    st.settle(1)
    st.do(nv.tensor_tensor(c.d, c.e, c.um, ALU.subtract))
    st.settle()
    st.do(nv.tensor_tensor(c.d, c.d, c.ru, ALU.mult))
    v.wait_ge(s["sp_ln"], 1)
    st.settle()
    st.do(nv.tensor_tensor(c.ln, c.ln, c.d, ALU.add))
    st.settle()
    st.do(nv.scalar_tensor_tensor(c.sp, c.z, 0.0, c.ln, ALU.max, ALU.add))
    st.settle()
    for ch in range(NCH):
        st.do(nv.scalar_tensor_tensor(c.adt[:, ch * 16:ch * 16 + 16], c.sp[:, ch * 16:ch * 16 + 16], -1.0,
                                      c.ea, ALU.mult, ALU.mult))
    st.do(nv.tensor_scalar(c.nsp8, c.sp[:, 32:40], -8.0, None, ALU.mult))
    st.do(nv.tensor_scalar(c.psp8, c.sp[:, 32:40], 8.0, None, ALU.mult))
    st.settle()
    v.sem_inc(s["adt"], 1)
    vector_to_scalar(k, v, "u", 4, 8)

    v.wait_ge(s["acs_mm"], 1)
    st.do(nv.tensor_copy(c.acs, k.bank[1][:, 0:32]))
    st.settle()
    st.do(nv.tensor_tensor(c.dz, k.bank[1][:, 32:48], c.acs[:, 0:16], ALU.subtract))
    st.settle()
    v.sem_inc(s["acs"], 1)
    for n in range(4):
        ch, half = n // 2, n % 2
        v.wait_ge(s["xs_tr"], n + 1)
        dt = c.sp[:, ch * 16 + half * 8:ch * 16 + half * 8 + 8].unsqueeze(2).to_broadcast([P, 8, 64])
        nv.tensor_tensor(k.xdt[:, ch, half * 512:half * 512 + 512].rearrange("p (h q) -> p h q", h=8),
                         k.bank[2 + n % 2][:].rearrange("p (h q) -> p h q", h=8), dt,
                         ALU.mult).then_inc(s["xs_ev"], 1)
    v.wait_ge(s["xs_ev"], 2)
    v.wait_ge(s["ds_exp"], 1)
    nv.tensor_tensor(k.xdec.rearrange("p (h q) -> p h q", h=16), k.xdt[:, 0, :].rearrange("p (h q) -> p h q", h=16),
                     c.ds.unsqueeze(2).to_broadcast([P, 16, 64]), ALU.mult).then_inc(s["xdec"], 1)
    for ch in range(NCH):
        v.wait_ge(s["cb_mm"], ch + 1)
        nv.tensor_tensor(k.cbm[:, ch * 4:ch * 4 + 4, :], k.bank[3 - ch][:].rearrange("p (g t) -> p g t", g=4),
                         k.tri[:].unsqueeze(1).to_broadcast([P, 4, P]), ALU.mult).then_inc(s["cbm"], 1)
    v.wait_ge(s["cbm"], 2)
    cbm = k.cbm.rearrange("p (c g) t -> p c g t", c=NCH)

    def least(h):
        v.wait_ge(s["rb_mm"], h + 1)
        if h >= 2:
            v.wait_ge(s["e_exp"], h - 1)
        for ch in range(NCH):
            last = nv.tensor_scalar(k.e[:, h % 2, ch * P:(ch + 1) * P], k.decay_bank[h % 4][:, ch * P:(ch + 1) * P],
                                    c.acs[:, ch * 16 + h:ch * 16 + h + 1], 0.0, ALU.subtract, ALU.min)
        last.then_inc(s["e_min"], 1)

    def y_out(b):
        v.wait_ge(s["y_mm"], 2 * b + 2)
        nv.scalar_tensor_tensor(k.xc[:, b, :], k.xc[:, b, :], col(k, "ssd_d", b), k.bank[2 + b % 2][:, 0:T],
                                ALU.mult, ALU.add).then_inc(s["y_ev"], 1)
        v.wait_ge(s["y_ev"], b + 1)
        nv.tensor_tensor(k.z[:, b, :], k.z[:, b, :], k.xc[:, b, :], ALU.mult).then_inc(s["yz"], 1)

    least(0)
    for h in range(SSD_HEADS):
        if h + 1 < SSD_HEADS:
            least(h + 1)
        g = h // 4
        v.wait_ge(s["e_exp"], h + 1)
        if h >= 2:
            v.wait_ge(s["y_mm"], h - 1)
        nv.tensor_tensor(k.mt[:, h % 2, :].rearrange("p (c t) -> p c t", c=NCH),
                         k.e[:, h % 2, :].rearrange("p (c t) -> p c t", c=NCH), cbm[:, :, g, :],
                         ALU.mult).then_inc(s["mt"], 1)
        v.wait_ge(s["ex_exp"], h + 1)
        v.wait_ge(s["mt"], h + 1)
        nv.tensor_tensor(k.ce[:, h % 2, :], k.xc[:, 12 + g, P:T], k.ex[:, h % 2, :], ALU.mult).then_inc(s["ce"], 1)
        if h % 2 == 1 and h >= 3:
            y_out(h // 2 - 1)
    y_out(7)

    nv.memset(k.xb_pad[:, :, 0:3], 0.0)
    vector_evacuate(k, v, "xb", padded(k.xb_pad))

    def group_norm(half):
        v.wait_ge(s["gn_sqrt"], half + 1)
        st.do(nv.reciprocal(k.gn_rs[:], k.gn_sd[:, half, :]))
        st.settle()
        for b in range(4 * half, 4 * half + 4):
            g = (b // 2) % 2
            st.do(nv.scalar_tensor_tensor(k.z[:, b, :], k.z[:, b, :], col(k, "ssd_norm_g", b),
                                          k.gn_rs[:, g * T:(g + 1) * T], ALU.mult, ALU.mult))
        st.settle()
        v.sem_inc(s["gn_done"], 1)
        make_operand(k, v, st, "y_c", 4 * half, [k.z[:, b, :] for b in range(4 * half, 4 * half + 4)])

    v.wait_ge(s["v_sum_mm"], 1)
    st.do(nv.tensor_scalar(k.rv[:], k.bank[2][:, 0:T], 1.0 / D, None, ALU.mult))
    st.settle()
    for half in range(2):
        h4 = slice(4 * half, 4 * half + 4)
        nv.tensor_tensor(k.v[:, h4, :], k.v[:, h4, :], k.rv[:].unsqueeze(1).to_broadcast([P, 4, T]),
                         ALU.subtract).then_inc(s["v_cent"], 1)
    group_norm(0)
    vector_to_scalar(k, v, "gt", 0, 4)
    group_norm(1)
    vector_to_scalar(k, v, "gt", 4, 8)
    vector_rms(k, v, st, "v_sqrt", 1, k.rv)
    for b in range(KB):
        nv.scalar_tensor_tensor(k.v[:, b, :], k.v[:, b, :], col(k, "gmlp_ln_g", b), k.rv[:], ALU.mult,
                                ALU.mult).then_inc(s["v_scaled"], 1)
    vector_to_scalar(k, v, "gate_c")
    v.wait_ge(s["late_in"], 64)
    nv.tensor_tensor(k.gws, k.gws, k.tri[:].unsqueeze(1).to_broadcast([P, 8, P]), ALU.mult).then_inc(s["gws"], 1)
    for n in range(4):
        v.wait_ge(s["mix_mm"], n + 1)
        two = slice(2 * n, 2 * n + 2)
        nv.tensor_tensor(k.gmix[:].rearrange("p (g c t) -> p g c t", g=2, c=NCH),
                         k.bank[n % 2][:].rearrange("p (g c t) -> p g c t", g=2, c=NCH),
                         k.bs[:, two, :].unsqueeze(2).to_broadcast([P, 2, NCH, P]), ALU.add).then_inc(s["mix_ev"], 1)
        v.wait_ge(s["mix_ev"], n + 1)
        st.do(nv.tensor_tensor(k.u[:, two, :], k.u[:, two, :], k.gmix[:].rearrange("p (g t) -> p g t", g=2), ALU.mult))
        st.settle()
        make_operand(k, v, st, "y_a", 2 * n, [k.u[:, b, :] for b in (2 * n, 2 * n + 1)])

    v.wait_ge(s["v_ev"], 4)
    for half in range(2):
        conv(k, v, st, k.xb_pad, k.xb, range(4 * half, 4 * half + 4), "lru_conv_w", "lru_conv_b", 8)
        st.settle()
        v.sem_inc(s["lru_conv"], 1)
        vector_evacuate(k, v, "branch_c", gated_sum(k, v, "gate_c", first=True), 4 * half, 4 * half + 4)

    def lru(half):
        h4 = slice(4 * half, 4 * half + 4)
        v.wait_ge(s["lru_at"], 2 * half + 2)
        st.do(nv.tensor_tensor(k.i[:, h4, :], k.i[:, h4, :], k.xb[:, h4, :], ALU.mult))
        st.do(nv.tensor_tensor(k.r[:, h4, :], k.a[:, h4, :], k.a[:, h4, :], ALU.mult))
        st.settle()
        nv.scalar_tensor_tensor(k.t[:, h4, :], k.r[:, h4, :], 1.0, k.t[:, h4, :], ALU.add,
                                ALU.mult).then_inc(s["lru_q"], 1)
        v.wait_ge(s["lru_sqrt"], half + 1)
        st.do(nv.tensor_tensor(k.i[:, h4, :], k.i[:, h4, :], k.t[:, h4, :], ALU.mult))
        st.settle()
        for b in range(4 * half, 4 * half + 4):
            st.do(nv.tensor_tensor_scan(k.r[:, b, :], k.a[:, b, :], k.i[:, b, :], 0.0, ALU.mult, ALU.add))
        st.settle()
        st.do(nv.tensor_tensor(k.gt[:, h4, :], k.gt[:, h4, :], k.r[:, h4, :], ALU.mult))
        st.settle()
        make_operand(k, v, st, "y_b", 4 * half, [k.gt[:, b, :] for b in range(4 * half, 4 * half + 4)])

    vector_to_scalar(k, v, "gate_a")
    lru(0)
    vector_evacuate(k, v, "branch_a", gated_sum(k, v, "gate_a"))
    lru(1)
    vector_to_scalar(k, v, "gate_b")
    for half in range(2):
        vector_evacuate(k, v, "branch_b", gated_sum(k, v, "gate_b"), 4 * half, 4 * half + 4)
        v.wait_ge(s["merged"], 4 * half + 4 + 8)
        make_operand(k, v, st, "merged", 4 * half, [k.m[:, b, :] for b in range(4 * half, 4 * half + 4)])

    def add_to(dst, first=False):
        def write(i, t, j, q, product):
            o = dst[:, at(v, i), :].rearrange("p o t -> p (o t)")
            if first:
                ins = nv.tensor_scalar(o, product, 1.0, None, ALU.mult)
            else:
                ins = nv.tensor_tensor(o, product, o, ALU.add)
            ins.then_inc(s["evacuated"], 1)
        return write

    def accumulate(name, dst, first=False):
        if not first:
            v.wait_ge(s["evacuated"], k.segs[name].start)
        vector_evacuate(k, v, name, add_to(dst, first))
        v.wait_ge(s["evacuated"], k.segs[name].start + 8)

    op = k.made["hn_mlp"]
    v.wait_ge(s["tiles_used"], op.free)
    seg = k.segs["out"]
    for b, _, _ in tiles(v, seg.n, unroll=True):
        v.wait_ge(s["tiles_used"], seg.start + b + 1)
        x, hi, gain = k.x[:, b, :], op.hi[:, b, :], col(k, "norm_mlp_g", b)
        nv.tensor_tensor(x, k.slots[(seg.start + b) % RING][:, 0:T], x, ALU.add).then_inc(s["evacuated"], 1)
        v.wait_ge(s["evacuated"], seg.start + b + 1)
        st.do(nv.tensor_scalar(hi, x, gain, None, ALU.mult))
        st.settle()
        nv.scalar_tensor_tensor(op.lo[:, b, :], x, gain, hi.bitcast(F32), ALU.mult,
                                ALU.subtract).then_inc(s["op_ready"], 1)
    rms()

    hid_done = [0]

    def split_hidden(op, block, base, e):
        hid, hi, lo = block, op.hi[:, at(v, e), :], op.lo[:, at(v, e), :]
        hi, lo = (z.rearrange("p o t -> p (o t)") for z in (hi, lo))
        v.wait_ge(s["hid_t"], e + (base + 1))
        nv.tensor_scalar(hi, hid, 1.0, None, ALU.mult).then_inc(s["hid_w"], 1)
        v.wait_ge(s["hid_w"], e + (base + 1))
        nv.tensor_tensor(lo, hid, hi.bitcast(F32), ALU.subtract).then_inc(s["op_ready"], 1)

    def mlp_up(chunk):
        op, base = k.made[f"mlp_hid{chunk}"], hid_done[0]
        v.wait_ge(s["tiles_used"], op.free)

        def write(i, t, j, q, product):
            nv.tensor_tensor(k.pre[:, j, :], product, k.rs[:], ALU.mult).then_inc(s["evacuated"], 1)
            v.wait_ge(s["evacuated"], t + 1)
            nv.scalar_tensor_tensor(k.hid[:, j, :], k.pre[:, j, :], 0.0, k.pre[:, j, :], ALU.max,
                                    ALU.mult).then_inc(s["hid_t"], 1)
            split_hidden(op, k.hid[:, j, :], base, i)

        vector_evacuate(k, v, f"mlp_up{chunk}", write)
        hid_done[0] += 8

    v.wait_ge(s["act_out"], k.act_after["gate_b"])
    for chunk in range(UP_CHUNKS):
        mlp_up(chunk)
        if chunk:
            accumulate(f"mlp_down{chunk - 1}", k.x)
    accumulate(f"mlp_down{UP_CHUNKS - 1}", k.x)

    renewed = [0]

    def renew(src, gain, factor, operand=None, operand_gain=None):
        rms()
        base = renewed[0]
        if operand:
            op = k.made[operand]
            v.wait_ge(s["tiles_used"], op.free)
            renewed[0] += KB
        issued = lambda b: 0 <= b < KB
        for b in range(KB + 3):
            if issued(b):
                if factor is None:
                    nv.scalar_tensor_tensor(k.x[:, b, :], src[:, b, :], col(k, gain, b), k.rs[:], ALU.mult,
                                            ALU.mult).then_inc(s["x_final"], 1)
                else:
                    st.do(nv.scalar_tensor_tensor(src[:, b, :], src[:, b, :], col(k, gain, b), k.rs[:],
                                                  ALU.mult, ALU.mult))
            c1 = b - 1
            if issued(c1) and factor is not None:
                st.settle(issued(b) + (issued(c1 - 2) and operand is not None))
                nv.scalar_tensor_tensor(k.x[:, c1, :], src[:, c1, :], factor, k.x[:, c1, :], ALU.mult,
                                        ALU.add).then_inc(s["x_final"], 1)
            if not operand:
                if c1 in (3, 7):
                    v.wait_ge(s["x_final"], base + c1 + 1)
                    v.sem_inc(s["out_done"], 1)
                continue
            c1 = b - 2
            if issued(c1):
                v.wait_ge(s["x_final"], base + c1 + 1)
                st.do(nv.tensor_scalar(op.hi[:, c1, :], k.x[:, c1, :], col(k, operand_gain, c1), None, ALU.mult))
            c1 = b - 3
            if issued(c1):
                st.settle((issued(b) and factor is not None) + issued(c1 + 1))
                nv.scalar_tensor_tensor(op.lo[:, c1, :], k.x[:, c1, :], col(k, operand_gain, c1),
                                        op.hi[:, c1, :].bitcast(F32), ALU.mult, ALU.subtract).then_inc(s["op_ready"], 1)

    renew(k.x, "final_norm_g", None, "hn_ffn1", "ffn1_pre_g_2")

    def ffn_up(kind, chunk):
        op, base, act = k.made[f"{kind}_hid{chunk}"], hid_done[0], k.act_before[f"{kind}_up{chunk}"]
        v.wait_ge(s["tiles_used"], op.free)
        v.wait_ge(s["act_out"], act)

        def write(i, t, j, q, product):
            e = q * 2 + j // 2
            if j % 2 == 0:
                if not isinstance(i, int) or i >= RING:
                    v.wait_ge(s["act_out"], e + (act - 1))
                nv.tensor_tensor(k.pre[:, j, :], product, k.rs[:], ALU.mult).then_inc(s["evacuated"], 1)
                return
            nv.tensor_tensor(k.pre[:, j, :], product, k.rs[:], ALU.mult).then_inc(s["evacuated"], 1)
            v.wait_ge(s["evacuated"], t + 1)
            v.wait_ge(s["act_out"], e + (act + 1))
            nv.tensor_tensor(k.hid[:, j, :], k.pre[:, j, :], k.sg[:, j - 1, :], ALU.mult).then_inc(s["hid_t"], 1)
            split_hidden(op, k.hid[:, j, :], base, e)

        vector_evacuate(k, v, f"{kind}_up{chunk}", write)
        hid_done[0] += FF2_CHUNKS[chunk]

    def ffn(kind):
        rms()
        for chunk in range(len(FF2_CHUNKS)):
            ffn_up(kind, chunk)
            if chunk:
                accumulate(f"{kind}_down{chunk - 1}", k.f, first=chunk == 1)
        accumulate(f"{kind}_down{len(FF2_CHUNKS) - 1}", k.f)

    ffn("ffn1")

    renew(k.f, "ffn1_post_g_2", 0.5, "hn_mix", "mix_pre_g_2")
    sm = k.small
    prev_g, next_g = COLS["rwkv_mu_prev_2"], COLS["rwkv_mu_next_2"]
    st.do(nv.tensor_tensor(sm[:, 0:15], k.cols[:, prev_g:prev_g + 15], k.cols[:, next_g:next_g + 15], ALU.add))
    st.settle()
    st.do(nv.tensor_scalar(sm[:, 0:15], sm[:, 0:15], -1.0, 1.0, ALU.mult, ALU.add))
    ka = COLS["rwkv_k_a_2"]
    st.do(nv.tensor_scalar(sm[:, 16:20], k.cols[:, ka:ka + 4], -1.0, 1.0, ALU.mult, ALU.add))
    nv.memset(k.upad[:, :, 0:1], 0.0)
    nv.memset(k.upad[:, :, T + 1:T + 2], 0.0)
    rms()

    def plain(dst, offset=0):
        def write(i, t, j, q, product):
            o = dst[:, at(v, i), offset:offset + T].rearrange("p o t -> p (o t)")
            nv.tensor_tensor(o, product, k.rs[:], ALU.mult).then_inc(s["evacuated"], 1)
        return write

    vector_evacuate(k, v, "rwkv_in", plain(k.upad, 1))
    v.wait_ge(s["evacuated"], k.segs["rwkv_in"].start + 15)

    def shift(blocks):
        for b in blocks:
            st.do(nv.tensor_scalar(k.us[:, b, :], k.upad[:, b, 1:T + 1], sm[:, b:b + 1], None, ALU.mult))
        for tap, name in ((0, "rwkv_mu_prev_2"), (2, "rwkv_mu_next_2")):
            for b in blocks:
                st.settle(len(blocks) - 1)
                st.do(nv.scalar_tensor_tensor(k.us[:, b, :], k.upad[:, b, tap:tap + T], col(k, name, b),
                                              k.us[:, b, :], ALU.mult, ALU.add))
        st.settle()

    shift((12, 13, 14))
    v.sem_inc(s["shifted"], 1)
    vector_evacuate(k, v, "qkv", plain(k.qkv), 0, 4)
    shift((4, 5, 6, 7))
    vector_evacuate(k, v, "qkv", plain(k.qkv), 4, 8)
    shift((0, 1, 2, 3))
    vector_evacuate(k, v, "qkv", plain(k.qkv), 8, 12)
    shift((8, 9, 10, 11))
    v.sem_inc(s["shifted"], 1)

    wide = lambda x: x.rearrange("p b t -> p (b t)")

    def kk_squares():
        for b in range(AB):
            st.do(nv.tensor_scalar(k.kk[:, b, :], k.us[:, 4 + b, :], col(k, "rwkv_k_k_2", b), None, ALU.mult))
        st.settle()
        nv.tensor_tensor(k.en[:, 0:4, :], k.kk[:], k.kk[:], ALU.mult).then_inc(s["kk_sq"], 1)

    def decay_scans():
        v.wait_ge(s["w_sig"], 8)
        st.do(nv.tensor_scalar(wide(k.lw), wide(k.lw), -float(np.exp(-0.5)), None, ALU.mult))
        v.wait_ge(s["masks_in"], 16)
        st.settle()
        fwd, bwd = wide(k.lc[:, 0:4, :]), wide(k.lc[:, 4:8, :])
        st.do(nv.tensor_tensor_scan(fwd, k.reset, wide(k.lw[:, 0:4, :]), 0.0, ALU.mult, ALU.add))
        st.do(nv.tensor_tensor_scan(bwd[:, ::-1], k.reset, wide(k.lw[:, 4:8, :])[:, ::-1], 0.0, ALU.mult, ALU.add))

    def decay_before():
        st.settle()
        nv.tensor_tensor(wide(k.lx), wide(k.lc), wide(k.lw), ALU.subtract).then_inc(s["lw_scan"], 1)

    def directed_keys(d):
        v.wait_ge(s["a_sig"], 8)
        for b in range(AB):
            st.do(nv.tensor_scalar(k.kd[:, 4 * d + b, :], k.ia[:, 4 * d + b, :], col(k, "rwkv_k_a_2", b),
                                   sm[:, 16 + b:17 + b], ALU.mult, ALU.add))
        st.settle()
        d4 = slice(4 * d, 4 * d + 4)
        st.do(nv.tensor_tensor(k.kd[:, d4, :], k.kd[:, d4, :], k.us[:, 4:8, :], ALU.mult))

    def kk_norm(half):
        v.wait_ge(s["kk_sqrt"], 1)
        root = wide(k.en[:, 4 + 2 * half:6 + 2 * half, :])
        st.do(nv.tensor_scalar(root, root, 1e-12, None, ALU.max))
        st.settle()
        st.do(nv.reciprocal(wide(k.en[:, 2 * half:2 * half + 2, :]), root))

    def kk_and_a():
        st.settle()
        st.do(nv.tensor_tensor(k.kk[:], k.kk[:], k.en[:, 0:4, :], ALU.mult))
        st.settle()
        v.sem_inc(s["l_ex"], 1)
        for d in range(2):
            st.do(nv.scalar_tensor_tensor(k.ia[:, 4 * d:4 * d + 4, :], k.ia[:, 4 * d:4 * d + 4, :], -1.0, k.kk[:],
                                          ALU.mult, ALU.mult))
        st.settle()
        v.sem_inc(s["kka"], 1)

    def bonus():
        st.settle()
        st.do(nv.tensor_tensor(k.bonus[:], k.kd[:, 0:4, :], k.kd[:, 4:8, :], ALU.add))
        st.settle()
        for b in range(AB):
            st.do(nv.tensor_scalar(k.bonus[:, b, :], k.bonus[:, b, :], col(k, "rwkv_r_k_2", b), 0.5,
                                   ALU.mult, ALU.mult))
        st.settle()
        nv.tensor_tensor(k.bonus[:], k.bonus[:], k.us[:, 0:4, :], ALU.mult).then_inc(s["bonus_in"], 1)

    def bonus_values():
        v.wait_ge(s["bonus_mm"], 1)
        for n in range(2):
            nv.tensor_tensor(k.bv[:, 2 * n:2 * n + 2, :], k.slots[n][:].rearrange("p (b t) -> p b t", b=2),
                             k.us[:, 8 + 2 * n:10 + 2 * n, :], ALU.mult).then_inc(s["bonus_ev"], 1)

    def rwkv_inputs(h):
        if h == 0:
            kk_squares()
        elif h == 1:
            decay_scans()
        elif h == 2:
            decay_before()
        elif h == 3:
            directed_keys(0)
            directed_keys(1)
        elif h == 4:
            kk_norm(0)
            bonus()
        elif h == 5:
            kk_norm(1)
        elif h == 6:
            kk_and_a()
        elif h == 8:
            bonus_values()

    v.wait_ge(s["rope_in"], 48)
    bc = lambda x, n: x.unsqueeze(1).to_broadcast([P, n, x.shape[-1]])
    v.wait_ge(s["rope_mm"], 4)
    for n in range(4):
        two = k.qkv[:, 2 * n:2 * n + 2, :]
        st.do(nv.tensor_tensor(two, two, bc(k.pre[:, 0, :], 2), ALU.mult))
        o = k.att_s[:, n % 2, :].rearrange("p (b t) -> p b t", b=2)
        st.do(nv.tensor_tensor(o, k.slots[n][:].rearrange("p (b t) -> p b t", b=2), bc(k.pre[:, 1, :], 2), ALU.mult))
        st.settle()
        nv.tensor_tensor(two, two, o, ALU.add).then_inc(s["rope_ev"], 1)

    v.wait_ge(s["att_in"], 16)

    def attention_probabilities(h):
        v.wait_ge(s["s_mm"], h + 1)
        if h >= 2:
            v.wait_ge(s["p_tr"], h - 1)
        sc = k.att_s[:, h % 2, :]
        nv.scalar_tensor_tensor(sc, k.slots[2 + h % 2][:], HD ** -0.5, wide(k.att_mask), ALU.mult,
                                ALU.add).then_inc(s["s_ev"], 1)
        v.wait_ge(s["s_ev"], h + 1)
        st.do(nv.tensor_reduce(sm[:, 64 + 2 * h:66 + 2 * h], sc.rearrange("p (i t) -> p i t", i=2), AX_X, ALU.max))
        st.settle()
        nv.tensor_scalar(sm[:, 80 + 2 * h:82 + 2 * h], sm[:, 64 + 2 * h:66 + 2 * h], -1.0, None,
                         ALU.mult).then_inc(s["s_red"], 1)

    for h in range(ATT_HEADS + 1):
        if h < ATT_HEADS:
            attention_probabilities(h)
        if h:
            g = h - 1
            v.wait_ge(s["p_tr"], g + 1)
            if g >= 2:
                v.wait_ge(s["o_mm"], g - 1)
            nv.tensor_copy(k.att_p[:, g % 2, :], k.bank[2 + g % 2][:]).then_inc(s["p_ev"], 1)
        rwkv_inputs(h)
    v.wait_ge(s["o_mm"], 8)
    v.wait_ge(s["s_exp"], 8)
    st.do(nv.reciprocal(sm[:, 112:128], sm[:, 96:112]))
    st.settle()
    den = sm[:, 112:128].rearrange("p (h i) -> p i h", i=2)
    for it in range(NCH):
        o = k.att_o[:, it, :].rearrange("p (h q) -> p h q", h=8)
        st.do(nv.tensor_tensor(o, k.bank[it][:].rearrange("p (h q) -> p h q", h=8),
                               den[:, it, :].unsqueeze(2).to_broadcast([P, 8, 64]), ALU.mult))
    st.settle()
    sq = k.att_p.rearrange("p a b -> p (a b)")
    st.do(nv.tensor_tensor(sq, k.att_o.rearrange("p a b -> p (a b)"), k.att_o.rearrange("p a b -> p (a b)"), ALU.mult))
    st.settle()
    nv.tensor_reduce(sm[:, 128:144], sq.rearrange("p (g q) -> p g q", q=64), AX_X, ALU.add).then_inc(s["o_sq"], 1)
    a_, q_ = (k.cbaq[:, n].rearrange("p d b t -> p (d b) t") for n in (2, 3))
    v.wait_ge(s["o_sqrt"], 1)
    st.do(nv.reciprocal(sm[:, 160:176], sm[:, 144:160]))
    st.settle()
    o = k.att_o.rearrange("p a (h q) -> p (a h) q", h=8)
    nv.tensor_tensor(o, o, sm[:, 160:176].unsqueeze(2).to_broadcast([P, 16, 64]), ALU.mult).then_inc(s["o_fin"], 1)
    v.wait_ge(s["ex_exp2"], 1)
    v.wait_ge(s["p_exp"], 1)
    v.wait_ge(s["g_mm"], 1)
    for d in range(2):
        d4 = slice(4 * d, 4 * d + 4)
        st.do(nv.tensor_tensor(a_[:, d4, :], k.kk[:], k.lx[:, d4, :], ALU.mult))
        st.do(nv.tensor_tensor(q_[:, d4, :], k.us[:, 0:4, :], k.lc[:, d4, :], ALU.mult))
    wt = sm[:, 176:208].rearrange("p (u c) -> p u c", u=8)
    for d, at_end in ((0, RC - 1), (1, 0)):
        st.do(nv.tensor_copy(wt[:, 4 * d:4 * d + 4, :],
                             k.lc[:, 4 * d:4 * d + 4, :].rearrange("p b (c t) -> p b c t", c=NRC)[:, :, :, at_end]))
    v.wait_ge(s["cb_made"], 2)
    st.settle()
    v.sem_inc(s["cbaq_made"], 1)
    v.wait_ge(s["masks_in"], 32)
    st.settle()

    h4 = lambda h: slice(4 * h, 4 * h + 4)
    over4 = lambda x: x.unsqueeze(1).to_broadcast([P, 4, RC])
    stack4 = over4(k.stack[:])
    BEFORE, BEFORE_OR_SAME = 6, 7
    bank64 = lambda h, n: k.half_bank[h][n][:, 0:4 * RC].rearrange("p (u t) -> p u t", u=4)
    bank128 = lambda h, n: k.half_bank[h][n][:].rearrange("p (u w t) -> p u w t", u=4, w=2)
    chunk_of = lambda h, j: j if h == 0 else NRC - 1 - j

    blk2 = k.blk[:].rearrange("p (h t) -> p h t", h=2)

    def spread_inputs(z, n, j):
        for h in range(2):
            c1 = chunk_of(h, j)
            dst, src = z[:, h4(h), :], k.cbaq[:, n, h, :, c1 * RC:(c1 + 1) * RC]
            last = nv.tensor_tensor(dst.rearrange("p n (h t) -> p n h t", h=2),
                                    src.unsqueeze(2).to_broadcast([P, 4, 2, RC]),
                                    blk2.unsqueeze(1).to_broadcast([P, 4, 2, RC]), ALU.mult)
            if h == 0:
                st.do(last)
        return last

    def on_diagonal(dst, h, src, other, op):
        for g in range(2):
            rows = slice(HD * g, HD * g + HD)
            last = nv.tensor_tensor(dst[rows, h4(h), HD * g:HD * g + HD], src[rows], other[rows], op)
            if g == 0:
                st.do(last)
        return last

    def masked(dst, src, h, mask):
        return on_diagonal(dst, h, src, over4(k.levels[:, h, mask]), ALU.mult)

    def level_part(j, level, h):
        masked(k.zn, k.nt[:, h4(h), :], h, level).then_inc(s["zn"], 1)

    def begin_inverse(j):
        for h in range(2):
            v.wait_ge(s["gb_mm"], 2 * j + h + 1)
            st.do(nv.tensor_tensor(k.nt[:, h4(h), :], bank128(h, 3)[:, :, 0, :], over4(k.levels[:, h, BEFORE]),
                                   ALU.mult))
        for h in range(2):
            st.settle()
            level_part(j, 0, h)
        for h in range(2):
            st.do(nv.tensor_tensor(k.ttc[:, h4(h), :], k.nt[:, h4(h), :], over4(k.levels[:, h, 0]), ALU.mult))
        ident4 = k.ident[:].unsqueeze(1).to_broadcast([P, 4, P])
        for h in range(2):
            v.wait_ge(s["zn"], 12 * j + h + 1)
            nv.tensor_tensor(k.ztt[:, h4(h), :], k.zn[:, h4(h), :], ident4, ALU.add).then_inc(s["ztt"], 1)
        st.settle()
        for h in range(2):
            nv.tensor_tensor(k.ttc[:, h4(h), :], k.ttc[:, h4(h), :], stack4, ALU.add).then_inc(s["tt_ev"], 1)

    def y_norm(n, stage):
        y = (k.ytok[:, 1:3], k.ytok[:, 0:4:3])[n]
        mean, var, root, inv = (sm[:, c1:c1 + 8].rearrange("p (c b) -> p c b", c=2)
                                for c1 in range(256 + 32 * n, 288 + 32 * n, 8))
        wide4 = lambda x: x.unsqueeze(3).to_broadcast([P, 2, AB, RC])
        st.settle()
        if stage == 0:
            st.do(nv.tensor_reduce(mean, y, AX_X, ALU.add))
            st.settle()
            st.do(nv.tensor_scalar(mean, mean, 1.0 / HD, None, ALU.mult))
        elif stage == 1:
            st.do(nv.tensor_tensor(y, y, wide4(mean), ALU.subtract))
            st.settle()
            st.do(nv.tensor_tensor(k.ysq, y, y, ALU.mult))
        elif stage == 2:
            nv.tensor_reduce(var, k.ysq, AX_X, ALU.add).then_inc(s["y_sq"], 1)
        else:
            v.wait_ge(s["y_sqrt"], n + 1)
            st.do(nv.reciprocal(inv, root))
            st.settle()
            nv.tensor_tensor(y, y, wide4(inv), ALU.mult).then_inc(s["y_norm"], 1)

    spread_inputs(k.zb, 1, 0).then_inc(s["z_made"], 1)
    spread_inputs(k.zc, 0, 0).then_inc(s["z_made"], 1)
    v.wait_ge(s["o_tr"], 1)
    for b in range(AB):
        st.do(nv.tensor_scalar(k.y_att[:, b, :], k.slots[b // 2][:, (b % 2) * T:(b % 2 + 1) * T],
                               col(k, "attn_out_g_2", b), None, ALU.mult))
    v.wait_ge(s["z_cleared"], 5)
    begin_inverse(0)
    for j in range(NRC):
        for h in range(2):
            v.wait_ge(s["u_mm"], 12 * j + h + 1)
            nv.tensor_tensor(k.tc[:, h4(h), :], bank64(h, 0), stack4, ALU.add).then_inc(s["t_ev"], 1)
        for h in range(2):
            v.wait_ge(s["ztt"], 12 * j + h + 1)
            level_part(j, 1, h)
        for h in range(2):
            v.wait_ge(s["gc_mm"], 2 * j + h + 1)
            st.do(masked(k.zaac, bank128(h, 1)[:, :, 0, :], h, BEFORE))
            masked(k.zaqc, bank128(h, 1)[:, :, 1, :], h, BEFORE_OR_SAME).then_inc(s["gc_ev"], 1)
        for level in range(1, 6):
            if level < 5:
                for h in range(2):
                    v.wait_ge(s["u_mm"], 12 * j + 2 * level + h + 1)
                    level_part(j, level + 1, h)
            if level == 1:
                for h in range(2):
                    masked(k.zaqb, bank128(h, 3)[:, :, 1, :], h, BEFORE_OR_SAME).then_inc(s["gb_ev"], 1)
            elif level == 2 and j:
                spread_inputs(k.za, 2, j).then_inc(s["za_made"], 1)
            elif level in (3, 4) and j + 1 < NRC:
                v.wait_ge(s["tok_tr"], 4 * j + 4)
                n = level - 3
                spread_inputs((k.zc, k.zb)[n], n, j + 1).then_inc(s["z_made"], 1)
            elif level == 5 and j:
                spread_inputs(k.zq, 3, j).then_inc(s["zq_made"], 1)
            if j == NRC - 1 and level > 1:
                y_norm(0, level - 2)
            for h in range(2):
                if level < 5:
                    v.wait_ge(s["t_mm"], 8 * j + 2 * level + h - 1)
                    v.wait_ge(s["t_ev"], 10 * j + 2 * level + h - 1)
                    nv.tensor_tensor(k.tc[:, h4(h), :], bank64(h, 1), k.tc[:, h4(h), :],
                                     ALU.add).then_inc(s["t_ev"], 1)
                v.wait_ge(s["tt_mm"], 10 * j + 2 * level + h - 1)
                v.wait_ge(s["tt_ev"], 12 * j + 2 * level + h - 1)
                on_diagonal(k.ztt, h, bank64(h, 2), k.ttc[:, h4(h), :], ALU.add).then_inc(s["ztt"], 1)
                v.wait_ge(s["ztt"], 12 * j + 2 * level + h + 1)
                nv.tensor_tensor(k.ttc[:, h4(h), :], bank64(h, 2), k.ttc[:, h4(h), :],
                                 ALU.add).then_inc(s["tt_ev"], 1)
            if j == 0 and level < 5:
                make_operand(k, v, st, "y_mix", level - 1, [k.y_att[:, level - 1, :]])

        for h in range(2):
            v.wait_ge(s["sa_mm"], 2 * j + h + 1)
            nv.tensor_copy(k.sa[:, h4(h), :], bank64(h, 0)).then_inc(s["sa_ev"], 1)
        if j + 1 < NRC:
            begin_inverse(j + 1)
            for h in range(2):
                v.wait_ge(s["ss_mm"], 2 * j + h + 1)
                w = wt[:, h4(h), chunk_of(h, j)].unsqueeze(2).to_broadcast([P, 4, RC])
                state, new = k.st[:, h4(h), :], bank64(h, 1)
                if j:
                    v.wait_ge(s["yy_mm"], 2 * j + h + 1)
                    st.do(nv.tensor_tensor(state, new, state, ALU.add))
                    st.settle()
                    nv.tensor_tensor(state, state, w, ALU.mult).then_inc(s["ss_ev"], 1)
                else:
                    nv.tensor_tensor(state, new, w, ALU.mult).then_inc(s["ss_ev"], 1)
        for h in range(2):
            v.wait_ge(s["yy_mm"], 2 * j + h + 1)
            o = k.ytok[:, chunk_of(h, j), :, :]
            y = bank64(h, 2)
            ins = nv.tensor_copy(o, y) if j < NRC // 2 else nv.tensor_tensor(o, y, o, ALU.add)
            ins.then_inc(s["y_taken"], 1)
    v.wait_ge(s["y_taken"], 2 * NRC)
    for stage in range(4):
        y_norm(1, stage)

    v.wait_ge(s["y_fm"], 1)
    for b in range(AB):
        st.do(nv.tensor_scalar(k.yf[:, b, :], k.slots[b // 2][:, (b % 2) * T:(b % 2 + 1) * T],
                               col(k, "rwkv_lnx_w_2", b), col(k, "rwkv_lnx_b_2", b), ALU.mult, ALU.add))
    for b in range(AB):
        st.settle(AB - 1)
        st.do(nv.tensor_tensor(k.yf[:, b, :], k.yf[:, b, :], k.bv[:, b, :], ALU.add))
    for b in range(AB):
        st.settle(AB - 1)
        st.do(nv.tensor_tensor(k.yf[:, b, :], k.yf[:, b, :], k.gout[:, b, :], ALU.mult))
    st.settle()
    make_operand(k, v, st, "y_mix", 4, [k.yf[:, b, :] for b in range(AB)])
    accumulate("out_2", k.f, first=True)
    renew(k.f, "mix_post_g_2", 1.0, "hn_ffn2", "ffn2_pre_g_2")
    ffn("ffn2")
    renew(k.f, "ffn2_post_g_2", 0.5)


def scalar_segment(k, act, name, work=None, first=0, last=None, every=1, unroll=False):
    seg = k.segs[name]
    last = seg.n if last is None else last
    ahead = RING - 1
    n = last - first
    if seg.start + last + ahead > k.total:
        counted = [(i, i % RING, i // RING) for i in range(n)]
    else:
        counted = tiles(act, n, seg.start + first == 0, unroll)
    for i, j, q in counted:
        t0 = seg.start + first + ahead
        if not isinstance(i, int) or t0 + i < k.total:
            slot = (t0 + j) % RING
            act.wait_ge(k.landed[slot], q * 16 + 16 * ((t0 + j) // RING + 1))
            if seg.start + first or not isinstance(i, int) or i >= 1:
                act.wait_ge(k.s["tiles_used"], i + (t0 - RING + 1))
            k.nc.scalar.activation(k.whi[:, slot, :], k.raw[:, slot, :], ACT.Copy).then_inc(k.s["hi_ready"], 1)
        if work is not None and j % every == 0:
            act.wait_ge(k.s["evacuated"], i + (seg.start + first + 1))
            work(i + first, j, q)


def scalar_function(k, act, name, func, dst, bias=None, first=0):
    base = k.act_before[name]

    def work(i, j, q):
        o = dst[:, at(act, i), :].rearrange("p o t -> p (o t)")
        src = k.pre[:, (base + first + j) % RING, :]
        if bias is None:
            ins = k.nc.scalar.activation(o, src, func)
        else:
            c = COLS[bias[0]] + bias[1]
            ins = k.nc.scalar.activation(o, src, func, bias=k.cols[:, bass.ds(i + c, 1)])
        ins.then_inc(k.s["act_out"], 1)
    return work


def scalar_program(k, act, a):
    s, c, na = k.s, Small(k), k.nc.scalar
    st = Steps(act, s["step_a"])
    f = na.activation

    act.dma_start(k.x[:], a["x"]).then_inc(s["x_in"], 16)
    for dst, name in ((k.cols[:], "cols"), (k.ones[:], "ones"), (k.ident[:], "ident"), (k.tri[:], "tri"),
                      (k.wdt[:], "w_dt"), (Small(k).dtb_alog, "dt_rows")):
        act.dma_start(dst, a[name]).then_inc(s["consts_in"], 16)
    for t in range(RING - 1):
        act.wait_ge(k.landed[t], 16)
        f(k.whi[:, t, :], k.raw[:, t, :], ACT.Copy).then_inc(s["hi_ready"], 1)
    act.wait_ge(s["x_in"], 16)
    norms = [0]

    def root():
        norms[0] += 1
        act.wait_ge(s["rms_mm"], norms[0])
        f(k.sd[:], k.bank[0][:, 0:T], ACT.Sqrt, bias=k.eps[:, 0:1], scale=1.0 / D).then_inc(s["rms_sqrt"], 1)

    def square(sq, src, b):
        f(sq[:, b, :], src[:, b, :], ACT.Square).then_inc(s["sq"], 1)

    act.wait_ge(s["consts_in"], 16 * CONST_DMAS)
    f(c.ea, c.alog, ACT.Exp)
    act.wait_ge(s["zeroed"], 1)
    for b in range(KB):
        square(k.sq0, k.x, b)
    root()
    for dst, name in ((k.gws, "gmlp_w"), (k.bs, "gmlp_b"), (k.blk[:], "blk"), (k.stack[:], "stack")):
        act.dma_start(dst, a[name]).then_inc(s["late_in"], 16)
    scalar_segment(k, act, "xbc")

    def silu(n):
        act.wait_ge(s["conv_done"], n + 1)
        h4 = slice(4 * n, 4 * n + 4)
        f(k.xc[:, h4, :], k.xc[:, h4, :], ACT.Silu).then_inc(s["ssd_silu"], 1)

    for half in range(2):
        silu(half)
        scalar_segment(k, act, "z", scalar_function(k, act, "z", ACT.Silu, k.z), 4 * half, 4 * half + 4)
    for half in range(2):
        silu(2 + half)
        scalar_segment(k, act, "v", scalar_function(k, act, "v", ACT.Gelu_apprx_tanh, k.v), 4 * half, 4 * half + 4)
    act.wait_ge(s["sp_z"], 2)
    st.do(f(c.ab, c.z, ACT.Abs))
    st.settle()
    f(c.e, c.ab, ACT.Exp, scale=-1.0).then_inc(s["sp_exp"], 1)
    scalar_segment(k, act, "u", scalar_function(k, act, "u", ACT.Gelu_apprx_tanh, k.u), 0, 4)
    act.wait_ge(s["sp_u"], 1)
    f(c.ln, c.u, ACT.Ln).then_inc(s["sp_ln"], 1)
    scalar_segment(k, act, "u", scalar_function(k, act, "u", ACT.Gelu_apprx_tanh, k.u), 4, 8)

    act.wait_ge(s["acs"], 1)
    f(c.ds, c.dz, ACT.Exp).then_inc(s["ds_exp"], 1)
    act.wait_ge(s["b_tr"], 1)
    f(k.bt, k.bank[2][:], ACT.Copy).then_inc(s["b_ev"], 1)
    for half in range(2):
        act.wait_ge(s["st_mm"], half + 1)
        f(k.state[:, half * 512:half * 512 + 512], k.bank[(1, 2)[half]][:], ACT.Copy).then_inc(s["st_ev"], 1)
    for h in range(SSD_HEADS):
        act.wait_ge(s["e_min"], h + 1)
        if h >= 2:
            act.wait_ge(s["ce"], h - 1)
        f(k.ex[:, h % 2, :], k.decay_bank[h % 4][:, P:T], ACT.Exp).then_inc(s["ex_exp"], 1)
        f(k.e[:, h % 2, :], k.e[:, h % 2, :], ACT.Exp).then_inc(s["e_exp"], 1)
    for g in range(GROUPS):
        act.wait_ge(s["yz"], 2 * g + 2)
        f(k.gn_sq[:, 2 * g:2 * g + 2, :], k.z[:, 2 * g:2 * g + 2, :], ACT.Square).then_inc(s["gn_sq"], 1)
    scalar_segment(k, act, "xb")
    for half in range(2):
        act.wait_ge(s["gn_mm"], 2 * half + 2)
        f(k.gn_sd[:, half, :], k.bank[half][:], ACT.Sqrt, bias=k.eps[:, 0:1], scale=1.0 / 256).then_inc(s["gn_sqrt"], 1)
    for half in range(2):
        h4 = slice(4 * half, 4 * half + 4)
        act.wait_ge(s["v_cent"], half + 1)
        f(k.gm_sq[:, h4, :], k.v[:, h4, :], ACT.Square).then_inc(s["v_sq"], 1)
    scalar_segment(k, act, "gt", scalar_function(k, act, "gt", ACT.Gelu_apprx_tanh, k.gt))
    act.wait_ge(s["v_var_mm"], 1)
    f(k.sd[:], k.bank[3][:, 0:T], ACT.Sqrt, bias=k.eps[:, 0:1], scale=1.0 / D).then_inc(s["v_sqrt"], 1)
    for b in range(KB):
        act.wait_ge(s["v_scaled"], b + 1)
        f(k.v[:, b, :], k.v[:, b, :], ACT.Identity, bias=col(k, "gmlp_ln_b", b)).then_inc(s["v_norm"], 1)
    scalar_segment(k, act, "gate_c", scalar_function(k, act, "gate_c", ACT.Sigmoid, k.g, ("b_gate", 16)))
    for n in range(4):
        act.wait_ge(s["v_tr"], n + 1)
        ch, half = n // 2, n % 2
        f(k.vt[:, ch, half * 512:half * 512 + 512], k.bank[n % 2][:], ACT.Copy).then_inc(s["v_ev"], 1)
    act.wait_ge(s["mix_mm"], 4)
    act.wait_ge(s["mix_ev"], 4)
    act.dma_start(k.wr, a["lru_w_r"]).then_inc(s["lru_w_in"], 16)
    act.dma_start(k.wi, a["lru_w_i"]).then_inc(s["lru_w_in"], 16)
    scalar_segment(k, act, "branch_c")

    for b in range(KB):
        act.wait_ge(s["ri_mm"], b + 1)
        f(k.r[:, b, :], k.bank[2 + b % 2][:, 0:T], ACT.Sigmoid, bias=col(k, "lru_b_r", b)).then_inc(s["ri_sig"], 1)
        f(k.i[:, b, :], k.bank[2 + b % 2][:, T:512], ACT.Sigmoid, bias=col(k, "lru_b_i", b)).then_inc(s["ri_sig"], 1)
    act.wait_ge(s["ri_sig"], 16)
    for half in range(2):
        for b in range(4 * half, 4 * half + 4):
            na_a = f(k.a[:, b, :], k.r[:, b, :], ACT.Exp, scale=c.nsp8[:, b:b + 1])
            na_t = f(k.t[:, b, :], k.r[:, b, :], ACT.Tanh, scale=c.psp8[:, b:b + 1])
        na_a.then_inc(s["lru_at"], 1)
        na_t.then_inc(s["lru_at"], 1)
        scalar_segment(k, act, "gate_a", scalar_function(k, act, "gate_a", ACT.Sigmoid, k.g, ("b_gate", 0)),
                       4 * half, 4 * half + 4)

    def lru_root(half):
        h4 = slice(4 * half, 4 * half + 4)
        act.wait_ge(s["lru_q"], half + 1)
        f(k.t[:, h4, :], k.t[:, h4, :], ACT.Sqrt).then_inc(s["lru_sqrt"], 1)

    lru_root(0)
    scalar_segment(k, act, "branch_a")
    lru_root(1)
    scalar_segment(k, act, "gate_b", scalar_function(k, act, "gate_b", ACT.Sigmoid, k.g, ("b_gate", 8)))
    scalar_segment(k, act, "branch_b")
    finals = [0]

    def squares_of_outputs(name, src):
        scalar_segment(k, act, name, lambda i, j, q: square(k.sq, src, i), unroll=True)
        root()

    squares_of_outputs("out", k.x)

    def norm_of_stream():
        for b in range(KB):
            finals[0] += 1
            act.wait_ge(s["x_final"], finals[0])
            square(k.sq, k.x, b)
        root()

    for chunk in range(UP_CHUNKS):
        scalar_segment(k, act, f"mlp_up{chunk}")
        if chunk:
            scalar_segment(k, act, f"mlp_down{chunk - 1}")
    squares_of_outputs(f"mlp_down{UP_CHUNKS - 1}", k.x)

    def ffn(kind):
        norm_of_stream()
        for chunk in range(len(FF2_CHUNKS)):
            def work(i, j, q):
                f(k.sg[:, j, :], k.pre[:, j, :], ACT.Silu).then_inc(s["act_out"], 1)
            scalar_segment(k, act, f"{kind}_up{chunk}", work, every=2)
            if chunk:
                scalar_segment(k, act, f"{kind}_down{chunk - 1}")
        squares_of_outputs(f"{kind}_down{len(FF2_CHUNKS) - 1}", k.f)

    ffn("ffn1")

    act.wait_ge(s["tiles_used"], k.segs["ffn1_down2"].start + 8)
    act.dma_start(k.lora, a["lora"]).then_inc(s["rwkv_in"], 16)
    act.dma_start(k.pre[:, 0, :], a["rope_cos"]).then_inc(s["rope_in"], 16)
    act.dma_start(k.pre[:, 1, :], a["rope_sin"]).then_inc(s["rope_in"], 16)
    act.dma_start(k.pre[:, 2, 0:P], a["rope_turn"]).then_inc(s["rope_in"], 16)
    act.dma_start(k.reset, a["reset"]).then_inc(s["masks_in"], 16)
    norm_of_stream()
    act.dma_start(k.att_mask, a["att_mask"]).then_inc(s["att_in"], 16)
    scalar_segment(k, act, "rwkv_in")
    act.wait_ge(s["shifted"], 1)
    f(k.us[:, 12, :], k.us[:, 12, :], ACT.Tanh).then_inc(s["lora_in"], 1)
    f(k.us[:, 14, :], k.us[:, 14, :], ACT.Sigmoid).then_inc(s["lora_in"], 1)

    def sigmoids(dst, mm_event, bias, event):
        act.wait_ge(s[mm_event], 1)
        for n in range(8):
            f(dst[:, n, :], k.bank[n // 2][:, (n % 2) * T:(n % 2 + 1) * T], ACT.Sigmoid,
              bias=col(k, bias, n)).then_inc(s[event], 1)

    scalar_segment(k, act, "qkv")
    act.wait_ge(s["shifted"], 2)
    sigmoids(k.lw, "w_mm", "rwkv_w0_2", "w_sig")
    sigmoids(k.ia, "a_mm", "rwkv_a0_2", "a_sig")
    act.wait_ge(s["g_mm"], 1)
    for n in range(2):
        last = f(k.gout[:, 2 * n:2 * n + 2, :], k.bank[n][:].rearrange("p (b t) -> p b t", b=2), ACT.Copy)
    last.then_inc(s["g_ev"], 1)
    for ch in range(NCH):
        act.wait_ge(s["vt_tr"], ch + 1)
        f(k.att_v[:, ch, :], k.slots[ch][:], ACT.Copy).then_inc(s["vt_ev"], 1)
    sm = k.small
    for h in range(ATT_HEADS):
        act.wait_ge(s["s_red"], h + 1)
        for it in range(NCH):
            x = k.att_s[:, h % 2, it * T:(it + 1) * T]
            last = f(x, x, ACT.Exp, bias=sm[:, 80 + 2 * h + it:81 + 2 * h + it],
                     accum_out=sm[:, 96 + 2 * h + it:97 + 2 * h + it])
        last.then_inc(s["s_exp"], 1)
        if h == 2:
            act.wait_ge(s["kk_mm"], 1)
            for n in range(2):
                last = f(k.en[:, 4 + 2 * n:6 + 2 * n, :], k.slots[n][:].rearrange("p (b t) -> p b t", b=2), ACT.Sqrt)
            last.then_inc(s["kk_sqrt"], 1)
        if h == 3:
            act.wait_ge(s["lw_scan"], 1)
            act.dma_start(k.masks, a["rwkv_masks"]).then_inc(s["masks_in"], 16)
        if h == 5:
            act.wait_ge(s["v_tok_mm"], 1)
            for n in range(2):
                f(k.vtok[:, 2 * n:2 * n + 2].rearrange("p c b v -> p (c b v)"), k.slots[n][:],
                  ACT.Copy).then_inc(s["v_tok_ev"], 1)
    act.wait_ge(s["l_ex"], 1)
    f(k.en, k.lc, ACT.Exp, scale=-1.0).then_inc(s["n_exp"], 1)
    f(k.lx, k.lx, ACT.Exp).then_inc(s["ex_exp2"], 1)
    act.wait_ge(s["n_exp"], 1)
    f(k.lc, k.lc, ACT.Exp).then_inc(s["p_exp"], 1)
    act.wait_ge(s["o_sq"], 1)
    f(sm[:, 144:160], sm[:, 128:144], ACT.Sqrt, bias=k.eps[:, 0:1], scale=1.0 / HD).then_inc(s["o_sqrt"], 1)

    bank64 = lambda h, n: k.half_bank[h][n][:, 0:4 * RC].rearrange("p (u t) -> p u t", u=4)

    def y_root(n):
        c0 = 256 + 32 * n
        act.wait_ge(s["y_sq"], n + 1)
        f(sm[:, c0 + 16:c0 + 24], sm[:, c0 + 8:c0 + 16], ACT.Sqrt, bias=k.eps[:, 1:2],
          scale=1.0 / HD).then_inc(s["y_sqrt"], 1)

    act.wait_ge(s["z_cleared"], 5)
    for j in range(NRC):
        for n, tok in enumerate((k.ctok, k.btok)):
            for h in range(2):
                act.wait_ge(s["tok_tr"], 4 * j + 2 * n + h + 1)
                f(tok[:, 4 * h:4 * h + 4, :], k.half_bank[h][2][:].rearrange("p (u t) -> p u t", u=4),
                  ACT.Copy).then_inc(s["tok_ev"], 1)
        for level in range(1, 6):
            for h in range(2):
                h4 = slice(4 * h, 4 * h + 4)
                act.wait_ge(s["u_mm"], 12 * j + 2 * level + h + 1)
                if level < 5:
                    f(k.uc[:, h4, :], bank64(h, 0), ACT.Copy).then_inc(s["uc_ev"], 1)
                for g in range(2):
                    rows = slice(HD * g, HD * g + HD)
                    last = f(k.zu[rows, h4, HD * g:HD * g + HD], bank64(h, 0)[rows], ACT.Copy)
                last.then_inc(s["zu_ev"], 1)
            if level == 5:
                for h in range(2):
                    act.wait_ge(s["x_mm"], 2 * j + h + 1)
                    f(k.xs[:, 4 * h:4 * h + 4, :], bank64(h, 3), ACT.Copy).then_inc(s["x_ev"], 1)
            if j == NRC - 1 and level == 4:
                y_root(0)
    y_root(1)
    squares_of_outputs("out_2", k.f)
    ffn("ffn2")


def second_constants():
    p, t = np.arange(P), np.arange(T)
    half = HD // 2
    inv = (np.float32(10000.0) ** (-np.arange(0, HD, 2, dtype=np.float32) / np.float32(HD))).astype(np.float32)
    ang = (t.astype(np.float32)[None, :] * inv[p % half][:, None]).astype(np.float32)
    turn = np.zeros((P, P), np.float32)
    for m in range(P):
        turn[m + half if m % HD < half else m - half, m] = -1.0 if m % HD < half else 1.0
    i, j = t[:, None], t[None, :]
    count = sum(((i - j) % d == 0) & (np.abs(i - j) <= w // 2) for w, d in ((128, 1), (512, 4), (2048, 16)))
    logs = np.where(count > 0, np.log(np.maximum(count, 1)), -1e30).astype(np.float32)
    s, r = np.arange(RC)[:, None], np.arange(RC)[None, :]
    by_direction = []
    for d in range(2):
        before = (s < r) if d == 0 else (s > r)
        levels = [before & (s // (2 << n) == r // (2 << n)) & (s >> n != r >> n) for n in range(6)]
        by_direction += levels + [before, before | (s == r)]
    masks = np.concatenate([np.tile(np.asarray(m, np.float32), (2, 1)) for m in by_direction], axis=1)
    return {
        "rope_cos": np.cos(ang), "rope_sin": np.sin(ang), "rope_turn": turn,
        "att_mask": logs.reshape(NCH, P, T).transpose(1, 0, 2),
        "reset": np.broadcast_to((np.arange(AB * T) % RC != 0).astype(np.float32)[None], (P, AB * T)),
        "rwkv_masks": masks,
        "stack": np.tile(np.eye(RC, dtype=np.float32), (2, 1)),
    }


def build_program(nc, a, out):
    with ExitStack() as ctx:
        k = allocate(nc, ctx)
        block = ctx.enter_context(nc.Block())

        @block.sync
        def _(sp):
            sync_program(k, sp, a, out)

        @block.gpsimd
        def _(pool):
            gpsimd_program(k, pool)

        @block.scalar
        def _(act):
            scalar_program(k, act, a)

        @block.vector
        def _(v):
            vector_program(k, v)

        @block.tensor
        def _(pe):
            tensor_program(k, pe)


def weight_tiles(w):
    rows, cols = w.shape
    w = w.reshape(rows // P, P, cols // P, P).transpose(2, 1, 0, 3)
    return np.ascontiguousarray(w).reshape(cols // P, P, rows)


def down_tiles(w, chunks):
    out, row = {}, 0
    for blocks in chunks:
        out.setdefault(blocks, []).append(weight_tiles(w[row:row + blocks * P]))
        row += blocks * P
    return [np.concatenate(x) for x in out.values()]


def turns(a, b):
    return np.stack([a, b], 1).reshape(2 * a.shape[0], *a.shape[1:])


def columns(x):
    return np.asarray(x).reshape(-1, P).T


def layouts(i):
    w = i["w_in"][0]
    o_z, o_xbc, o_dt = 4096, 5120, 7168
    h = {
        "x": i["x"][0].T.reshape(KB, P, T).transpose(1, 0, 2),
        "w_in": np.concatenate([weight_tiles(w[:, :o_dt]), weight_tiles(w[:, o_dt + 16:])]),
        "w_dt": w[:, o_dt:o_dt + 16].reshape(KB, P, 16).transpose(1, 0, 2),
        "w_mlp_up": weight_tiles(i["w_mlp_up"][0]),
        "w_mlp_down": down_tiles(i["w_mlp_down"][0], (8,) * UP_CHUNKS)[0],
        "w_in_2": weight_tiles(i["w_in_2"][0]),
        "lru_w_r": i["lru_w_r"][0].transpose(1, 0, 2),
        "lru_w_i": i["lru_w_i"][0].transpose(1, 0, 2),
        "gmlp_w": i["gmlp_w_s"][0].transpose(2, 0, 1),
        "gmlp_b": np.broadcast_to(i["gmlp_b_s"][0][None], (P, 8, P)),
        "dt_rows": np.broadcast_to(np.concatenate([i["ssd_dt_bias"][0], i["ssd_a_log"][0]])[None], (P, 32)),
    }
    for name in ("w_branch_a", "w_branch_b", "w_branch_c", "w_out", "w_out_2"):
        h[name] = weight_tiles(i[name][0])
    for kind in ("ffn1", "ffn2"):
        h[f"{kind}_gu"] = turns(weight_tiles(i[f"{kind}_w_gate_2"][0]), weight_tiles(i[f"{kind}_w_up_2"][0]))
        h[f"{kind}_down"], h[f"{kind}_down_tail"] = down_tiles(i[f"{kind}_w_down_2"][0], FF2_CHUNKS)
    cols = np.zeros((P, NCOLS), np.float32)
    for name, c in COLS.items():
        x = i[name]
        x = np.repeat(x, SSD_P, axis=-1) if name == "ssd_d" else x
        x = columns(x)
        cols[:, c:c + x.shape[1]] = x
    h["cols"] = cols
    r = np.arange(P)
    h["ones"] = np.ones((P, P), np.float32)
    h["ident"] = np.eye(P, dtype=np.float32)
    h["tri"] = (r[:, None] <= r[None, :]).astype(np.float32)
    h["blk"] = (r[:, None] // HD == r[None, :] // HD).astype(np.float32)
    h["lora"] = np.stack([i["rwkv_w2_2"][0].reshape(P, 512), i["rwkv_a2_2"][0].reshape(P, 512),
                          i["rwkv_g2_2"][0]], axis=1)
    h.update(second_constants())
    return {n: np.ascontiguousarray(x) for n, x in h.items()}


def kernel(**inputs):
    import concourse.bacc as bacc
    from concourse.bass_utils import run_bass_kernel_spmd

    arrays = layouts({n: np.asarray(x) for n, x in inputs.items()})
    nc = bacc.Bacc("TRN2", target_bir_lowering=False, num_devices=1)
    aps = {n: nc.dram_tensor(f"in_{n}", x.shape, F32, kind="ExternalInput").ap() for n, x in arrays.items()}
    out = nc.dram_tensor("out_x", (P, KB, T), F32, kind="ExternalOutput").ap()
    build_program(nc, aps, out)
    r = run_bass_kernel_spmd(nc, [{f"in_{n}": x for n, x in arrays.items()}], core_ids=[0])
    y = r.results[0]["out_x"]
    return np.ascontiguousarray(y.transpose(1, 0, 2).reshape(D, T).T)[None]
```
